# Optimizing a Trainium2 kernel written in Bass

```python
import jax
import jax.numpy as jnp
from jax import lax
import numpy as np
import math
import jax, jax.numpy as jnp

D_MODEL = 1024
BATCH = 1
SEQ = 256
DEPTH = 1

HEAD_DIM = 64
RET_W = 3 * D_MODEL // 8
RET_HEADS = RET_W // HEAD_DIM
HGRN_W = 3 * D_MODEL // 8
HGRN_HEADS = HGRN_W // HEAD_DIM
HGRN_DK = HEAD_DIM
GLA_W = D_MODEL // 4
GLA_HEADS = GLA_W // HEAD_DIM
GLA_DK = HEAD_DIM // 2
GLA_QK = GLA_HEADS * GLA_DK
GLA_GATE_RANK = 16
GLA_TAU = 16.0
D_MIX = RET_W + HGRN_W + GLA_W
CHUNK = 64
ROPE_BASE = 10000.0
EPS = 1e-6
F_MIN = 1e-30
N_GROUPS = 4
EXPERTS_PER_GROUP = 8
N_EXPERTS = N_GROUPS * EXPERTS_PER_GROUP
TOP_K_INNER = 2
D_EXPERT = D_MODEL // 4
N_MOD = 6
IN_PROJ_SIZES = (RET_W,) * 4 + (HGRN_W,) * 4 + (GLA_QK, GLA_QK, GLA_W, GLA_W, GLA_GATE_RANK)
IN_PROJ_DIM = sum(IN_PROJ_SIZES)


def rmsnorm(x, gain):
    xf = x.astype(jnp.float32)
    y = xf * lax.rsqrt(jnp.mean(xf * xf, axis=-1, keepdims=True) + EPS)
    return y.astype(x.dtype) * gain

def split_heads(t, n_heads):
    b, s, w = t.shape
    return t.reshape(b, s, n_heads, w // n_heads).transpose(0, 2, 1, 3).astype(jnp.float32)

def head_rmsnorm(o, gain):
    b, h, s, d = o.shape
    o = o.transpose(0, 2, 1, 3)
    o = o * lax.rsqrt(jnp.mean(o * o, axis=-1, keepdims=True) + EPS)
    return o.reshape(b, s, h * d) * gain.astype(jnp.float32)

def rope_tables(positions, dim):
    inv_freq = ROPE_BASE ** (-jnp.arange(0, dim, 2, dtype=jnp.float32) / dim)
    ang = positions.astype(jnp.float32)[..., None] * inv_freq
    return jnp.cos(ang)[:, None], jnp.sin(ang)[:, None]

def apply_rope(t, cos, sin):
    t1, t2 = jnp.split(t, 2, axis=-1)
    return jnp.concatenate([t1 * cos - t2 * sin, t1 * sin + t2 * cos], axis=-1)

def retention_chunkwise(q, k, v):
    b, h, s, dk = q.shape
    dv = v.shape[-1]
    n = s // CHUNK
    log_gamma = jnp.log1p(-jnp.exp2(-5.0 - jnp.arange(h, dtype=jnp.float32)))
    idx = jnp.arange(CHUNK, dtype=jnp.float32)
    rel = idx[:, None] - idx[None, :]
    decay = jnp.where(rel >= 0, jnp.exp(log_gamma[:, None, None] * jnp.maximum(rel, 0.0)), 0.0)
    zeta = jnp.exp(log_gamma[:, None] * (CHUNK - 1 - idx))
    xi = jnp.exp(log_gamma[:, None] * (idx + 1.0))
    chunk_decay = jnp.exp(log_gamma * CHUNK)[:, None, None]
    qc = q.reshape(b, h, n, CHUNK, dk)
    kc = k.reshape(b, h, n, CHUNK, dk)
    vc = v.reshape(b, h, n, CHUNK, dv)
    scores = jnp.einsum('bhnid,bhnjd->bhnij', qc, kc) * decay[:, None]
    o_intra = jnp.einsum('bhnij,bhnje->bhnie', scores, vc)
    u = jnp.einsum('bhnjd,hj,bhnje->nbhde', kc, zeta, vc)

    def step(r, u_i):
        return r * chunk_decay + u_i, r

    _, r_prev = lax.scan(step, jnp.zeros((b, h, dk, dv), jnp.float32), u)
    o_inter = jnp.einsum('bhnid,nbhde,hi->bhnie', qc, r_prev, xi)
    return (o_intra + o_inter).reshape(b, h, s, dv)

def gated_linear_recurrence_chunkwise(q, k, v, log_a):
    b, h, s, dk = q.shape
    dv = v.shape[-1]
    n = s // CHUNK
    mask = jnp.tril(jnp.ones((CHUNK, CHUNK), dtype=bool))[:, :, None]

    def to_chunks(t):
        return jnp.moveaxis(t.reshape(b, h, n, CHUNK, t.shape[-1]), 2, 0)

    def step(state, inp):
        qc, kc, vc, lac = inp
        cum = jnp.cumsum(lac, axis=-2)
        o_inter = jnp.einsum('bhcd,bhde->bhce', qc * jnp.exp(cum), state)
        diff = cum[:, :, :, None, :] - cum[:, :, None, :, :]
        dec = jnp.where(mask, jnp.exp(jnp.where(mask, diff, 0.0)), 0.0)
        scores = jnp.einsum('bhtd,bhsd,bhtsd->bhts', qc, kc, dec)
        o = o_inter + jnp.einsum('bhts,bhse->bhte', scores, vc)
        cum_last = cum[:, :, -1:, :]
        new_state = (jnp.exp(cum_last[:, :, 0, :])[..., None] * state
                     + jnp.einsum('bhsd,bhse->bhde', kc * jnp.exp(cum_last - cum), vc))
        return new_state, o

    s0 = jnp.zeros((b, h, dk, dv), jnp.float32)
    _, o = lax.scan(step, s0, (to_chunks(q), to_chunks(k), to_chunks(v), to_chunks(log_a)))
    return jnp.moveaxis(o, 0, 2).reshape(b, h, s, dv)

def hybrid_mixer(h, cos, sin, w_in, ret_norm, hgrn_norm, hgrn_lb, gla_wa2, gla_ba, gla_norm, w_out):
    proj = h @ w_in
    splits = np.cumsum(IN_PROJ_SIZES)[:-1].tolist()
    (rq, rk, rv, rg, hq, hf, hi, hg, gq, gk, gv, gg, ga) = jnp.split(proj, splits, axis=-1)

    q = apply_rope(split_heads(rq, RET_HEADS), cos, sin)
    k = apply_rope(split_heads(rk, RET_HEADS), cos, sin) * HEAD_DIM ** -0.5
    o_ret = retention_chunkwise(q, k, split_heads(rv, RET_HEADS))
    o_ret = head_rmsnorm(o_ret, ret_norm) * jax.nn.silu(rg.astype(jnp.float32))

    lb = hgrn_lb.astype(jnp.float32).reshape(HGRN_HEADS, 1, HGRN_DK)
    z = split_heads(hf, HGRN_HEADS)
    f = lb + (1.0 - lb) * jax.nn.sigmoid(z)
    log_f = jnp.log(jnp.maximum(f, F_MIN))
    k = (1.0 - lb) * jax.nn.sigmoid(-z)
    q = jax.nn.silu(split_heads(hq, HGRN_HEADS)) * HGRN_DK ** -0.5
    o_hgrn = gated_linear_recurrence_chunkwise(q, k, split_heads(hi, HGRN_HEADS), log_f)
    o_hgrn = head_rmsnorm(o_hgrn, hgrn_norm) * jax.nn.silu(hg.astype(jnp.float32))

    log_a = jax.nn.log_sigmoid((ga @ gla_wa2 + gla_ba).astype(jnp.float32)) / GLA_TAU
    q = split_heads(gq, GLA_HEADS) * GLA_DK ** -0.5
    o_gla = gated_linear_recurrence_chunkwise(q, split_heads(gk, GLA_HEADS), split_heads(gv, GLA_HEADS),
                                              split_heads(log_a, GLA_HEADS))
    o_gla = head_rmsnorm(o_gla, gla_norm) * jax.nn.silu(gg.astype(jnp.float32))

    merged = jnp.concatenate([o_ret, o_hgrn, o_gla], axis=-1).astype(h.dtype)
    return merged @ w_out

def hierarchical_moe(h, w_rg, b_rg, w_re, b_re, w_gate, w_up, w_down):
    b, s, d = h.shape
    tok = h.reshape(b * s, d)
    g_logits = (tok @ w_rg + b_rg).astype(jnp.float32)
    g_idx = jnp.argmax(g_logits, axis=-1)
    g_w = jnp.max(jax.nn.softmax(g_logits, axis=-1), axis=-1, keepdims=True)
    e_logits = (tok @ w_re + b_re).astype(jnp.float32).reshape(-1, N_GROUPS, EXPERTS_PER_GROUP)
    e_in_group = jnp.einsum('nge,ng->ne', e_logits, jax.nn.one_hot(g_idx, N_GROUPS, dtype=jnp.float32))
    top_val, top_idx = lax.top_k(e_in_group, TOP_K_INNER)
    top_w = jax.nn.softmax(top_val, axis=-1) * g_w
    expert_ids = g_idx[:, None] * EXPERTS_PER_GROUP + top_idx
    combine = jnp.einsum('nk,nke->ne', top_w,
                         jax.nn.one_hot(expert_ids, N_EXPERTS, dtype=jnp.float32)).astype(h.dtype)
    out = jnp.zeros_like(tok)
    for e in range(N_EXPERTS):
        hid = jax.nn.silu(tok @ w_gate[e]) * (tok @ w_up[e])
        out = out + combine[:, e:e + 1] * (hid @ w_down[e])
    return out.reshape(b, s, d)

def first_inputs(seed: int = 0) -> dict:
    key = jax.random.key(seed)
    ks = jax.random.split(key, 24)
    f32 = jnp.float32

    def nrm(k, shape, scale):
        return jax.random.normal(k, shape, f32) * scale

    x = nrm(ks[0], (BATCH, SEQ, D_MODEL), 1.0)
    c = nrm(ks[1], (BATCH, D_MODEL), 1.0)
    positions = (jax.random.randint(ks[2], (BATCH, 1), 0, 1024)
                 + jnp.arange(SEQ, dtype=jnp.int32)[None, :]).astype(jnp.int32)
    w_ada = nrm(ks[3], (DEPTH, D_MODEL, N_MOD * D_MODEL), 0.5 * D_MODEL ** -0.5)
    b_ada = nrm(ks[4], (DEPTH, N_MOD * D_MODEL), 0.02)
    norm_mix = 1.0 + nrm(ks[5], (DEPTH, D_MODEL), 0.02)
    norm_ffn = 1.0 + nrm(ks[6], (DEPTH, D_MODEL), 0.02)
    w_in = nrm(ks[7], (DEPTH, D_MODEL, IN_PROJ_DIM), D_MODEL ** -0.5)
    ret_norm = 1.0 + nrm(ks[8], (DEPTH, RET_W), 0.02)
    hgrn_norm = 1.0 + nrm(ks[9], (DEPTH, HGRN_W), 0.02)
    hgrn_lb_logits = nrm(ks[10], (DEPTH, HGRN_HEADS * HGRN_DK), 1.0)
    gla_wa2 = nrm(ks[11], (DEPTH, GLA_GATE_RANK, GLA_QK), GLA_GATE_RANK ** -0.5)
    gla_ba = nrm(ks[12], (DEPTH, GLA_QK), 0.1)
    gla_norm = 1.0 + nrm(ks[13], (DEPTH, GLA_W), 0.02)
    w_out = nrm(ks[14], (DEPTH, D_MIX, D_MODEL), D_MIX ** -0.5)
    router_group_w = nrm(ks[15], (DEPTH, D_MODEL, N_GROUPS), D_MODEL ** -0.5)
    router_group_b = nrm(ks[16], (DEPTH, N_GROUPS), 0.01)
    router_expert_w = nrm(ks[17], (DEPTH, D_MODEL, N_EXPERTS), D_MODEL ** -0.5)
    router_expert_b = nrm(ks[18], (DEPTH, N_EXPERTS), 0.01)
    expert_w_gate = nrm(ks[19], (DEPTH, N_EXPERTS, D_MODEL, D_EXPERT), D_MODEL ** -0.5)
    expert_w_up = nrm(ks[20], (DEPTH, N_EXPERTS, D_MODEL, D_EXPERT), D_MODEL ** -0.5)
    expert_w_down = nrm(ks[21], (DEPTH, N_EXPERTS, D_EXPERT, D_MODEL), D_EXPERT ** -0.5)
    norm_final = 1.0 + nrm(ks[22], (D_MODEL,), 0.02)
    return {"x": x, "c": c, "positions": positions, "w_ada": w_ada, "b_ada": b_ada,
            "norm_mix": norm_mix, "norm_ffn": norm_ffn, "w_in": w_in, "ret_norm": ret_norm,
            "hgrn_norm": hgrn_norm, "hgrn_lb_logits": hgrn_lb_logits, "gla_wa2": gla_wa2,
            "gla_ba": gla_ba, "gla_norm": gla_norm, "w_out": w_out,
            "router_group_w": router_group_w, "router_group_b": router_group_b,
            "router_expert_w": router_expert_w, "router_expert_b": router_expert_b,
            "expert_w_gate": expert_w_gate, "expert_w_up": expert_w_up,
            "expert_w_down": expert_w_down, "norm_final": norm_final}

def first_block(x, c, positions, w_ada, b_ada, norm_mix, norm_ffn, w_in, ret_norm, hgrn_norm,
              hgrn_lb_logits, gla_wa2, gla_ba, gla_norm, w_out, router_group_w, router_group_b,
              router_expert_w, router_expert_b, expert_w_gate, expert_w_up, expert_w_down,
              norm_final):
    cos, sin = rope_tables(positions, HEAD_DIM)
    lb_w = jax.nn.softmax(hgrn_lb_logits.astype(jnp.float32), axis=0)
    lower_bounds = jnp.cumsum(lb_w, axis=0) - lb_w[0]
    c_act = jax.nn.silu(c)
    for layer in range(DEPTH):
        mod = c_act @ w_ada[layer] + b_ada[layer]
        shift_m, scale_m, gate_m, shift_f, scale_f, gate_f = [m[:, None, :] for m in jnp.split(mod, N_MOD, axis=-1)]
        h = rmsnorm(x, norm_mix[layer]) * (1.0 + scale_m) + shift_m
        x = x + gate_m * hybrid_mixer(h, cos, sin, w_in[layer], ret_norm[layer], hgrn_norm[layer],
                                      lower_bounds[layer], gla_wa2[layer], gla_ba[layer],
                                      gla_norm[layer], w_out[layer])
        h = rmsnorm(x, norm_ffn[layer]) * (1.0 + scale_f) + shift_f
        x = x + gate_f * hierarchical_moe(h, router_group_w[layer], router_group_b[layer],
                                          router_expert_w[layer], router_expert_b[layer],
                                          expert_w_gate[layer], expert_w_up[layer], expert_w_down[layer])
    return rmsnorm(x, norm_final)


DEPTH_2 = 2

SSM_EXPAND = 2
SSM_D_INNER = SSM_EXPAND * D_MODEL
SSM_HEAD_DIM = 64
SSM_HEADS = SSM_D_INNER // SSM_HEAD_DIM
SSM_GROUPS = 4
SSM_STATE = 128
SSM_CONV = 4
SSM_CHUNK = 128
SSM_CONV_DIM = SSM_D_INNER + 2 * SSM_GROUPS * SSM_STATE
ATT_HEAD_DIM = 64
ATT_KV_HEADS = D_MODEL // ATT_HEAD_DIM
ATT_PATTERNS = ((128, 1), (512, 4), (2048, 16))
ATT_GROUPS = len(ATT_PATTERNS)
ATT_Q_HEADS = ATT_GROUPS * ATT_KV_HEADS
ATT_WIDTH = ATT_KV_HEADS * ATT_HEAD_DIM
REL_BUCKETS = 32
REL_MAX_DIST = 2048
HY_SIZES = (SSM_D_INNER, SSM_CONV_DIM, SSM_HEADS, ATT_Q_HEADS * ATT_HEAD_DIM, ATT_WIDTH, ATT_WIDTH)
HY_SPLITS = tuple(int(v) for v in np.cumsum(HY_SIZES)[:-1])
HY_IN_DIM = sum(HY_SIZES)
HY_OUT_DIM = SSM_D_INNER + ATT_WIDTH
CONV_WIDTH = 31
FFN_HIDDEN = -(-8 * D_MODEL // (3 * 256)) * 256
N_EVEN = (DEPTH_2 + 1) // 2
N_ODD = DEPTH_2 // 2


def rms_norm(x, g):
    xf = x.astype(jnp.float32)
    y = xf * lax.rsqrt(jnp.mean(xf * xf, -1, keepdims=True) + EPS)
    return (y * g.astype(jnp.float32)).astype(x.dtype)

def layer_norm(x, g, b):
    xf = x.astype(jnp.float32)
    mu = jnp.mean(xf, -1, keepdims=True)
    var = jnp.mean(jnp.square(xf - mu), -1, keepdims=True)
    y = (xf - mu) * lax.rsqrt(var + EPS)
    return (y * g.astype(jnp.float32) + b.astype(jnp.float32)).astype(x.dtype)

def causal_depthwise_conv(x, w, b):
    k = w.shape[0]
    out = lax.conv_general_dilated(
        x, w[:, None, :].astype(x.dtype), window_strides=(1,), padding=[(k - 1, 0)],
        dimension_numbers=('NWC', 'WIO', 'NWC'), feature_group_count=x.shape[-1])
    return out + b

def t5_bucket(dist):
    max_exact = REL_BUCKETS // 2
    n = jnp.maximum(dist, 1).astype(jnp.float32)
    large = max_exact + jnp.log(n / max_exact) / math.log(REL_MAX_DIST / max_exact) * (REL_BUCKETS - max_exact)
    large = jnp.minimum(large.astype(jnp.int32), REL_BUCKETS - 1)
    return jnp.where(dist < max_exact, dist, large)

def ssd_chunked(x, dt, A, Bm, Cm):
    f32 = jnp.float32
    b_, s, h, p = x.shape
    g, n = Bm.shape[2], Bm.shape[3]
    r, q = h // g, SSM_CHUNK
    nc = s // q
    x = x.astype(f32).reshape(b_, nc, q, g, r, p)
    dt = dt.astype(f32).reshape(b_, nc, q, g, r)
    Bm = Bm.astype(f32).reshape(b_, nc, q, g, n)
    Cm = Cm.astype(f32).reshape(b_, nc, q, g, n)
    a_cs = jnp.cumsum(dt * A.astype(f32).reshape(g, r), axis=2)
    xdt = x * dt[..., None]
    seg = a_cs[:, :, :, None] - a_cs[:, :, None, :]
    causal = jnp.tril(jnp.ones((q, q), bool))[:, :, None, None]
    decay = jnp.exp(jnp.where(causal, seg, -jnp.inf))
    cb = jnp.einsum('bclgn,bcsgn->bclsg', Cm, Bm)
    y_diag = jnp.einsum('bclsgr,bcsgrp->bclgrp', cb[..., None] * decay, xdt)
    decay_end = jnp.exp(a_cs[:, :, -1:] - a_cs)
    states = jnp.einsum('bcsgn,bcsgrp->bcgrpn', Bm, xdt * decay_end[..., None])
    chunk_decay = jnp.exp(a_cs[:, :, -1])

    def step(hs, inp):
        st, dec = inp
        return dec[..., None, None] * hs + st, hs

    h0 = jnp.zeros((b_, g, r, p, n), f32)
    _, prev = lax.scan(step, h0, (jnp.moveaxis(states, 1, 0), jnp.moveaxis(chunk_decay, 1, 0)))
    prev = jnp.moveaxis(prev, 0, 1)
    y_off = jnp.einsum('bclgn,bcgrpn->bclgrp', Cm, prev) * jnp.exp(a_cs)[..., None]
    return (y_diag + y_off).reshape(b_, s, h, p)

def dilated_branch(q, k, v, bias_tab, window, dil):
    b_, s, h, dh = q.shape
    blk = window // dil
    L = s // dil
    nb = -(-L // blk)
    lp = nb * blk

    def blocks(t):
        t = t.reshape(b_, L, dil, h, dh)
        t = jnp.pad(t, ((0, 0), (0, lp - L), (0, 0), (0, 0), (0, 0)))
        return t.reshape(b_, nb, blk, dil, h, dh)

    def band_keys(t):
        prev = jnp.pad(t, ((0, 0), (1, 0), (0, 0), (0, 0), (0, 0), (0, 0)))[:, :-1]
        return jnp.concatenate([prev, t], axis=2)

    qb = blocks(q)
    kw, vw = band_keys(blocks(k)), band_keys(blocks(v))
    i = jnp.arange(blk)[:, None]
    j = jnp.arange(2 * blk)[None, :]
    delta = blk + i - j
    band = (delta >= 0) & (delta <= blk)
    kpos = jnp.arange(nb)[:, None] * blk + jnp.arange(2 * blk)[None, :] - blk
    mask = band[None] & (kpos >= 0)[:, None, :]
    bias = jnp.transpose(bias_tab[t5_bucket(jnp.maximum(delta, 0) * dil)], (2, 0, 1)).astype(jnp.float32)
    sc = jnp.einsum('bnirhd,bnjrhd->bnrhij', qb, kw).astype(jnp.float32) * (dh ** -0.5) + bias
    sc = jnp.where(mask[None, :, None, None], sc, -jnp.inf)
    m = jnp.max(sc, -1, keepdims=True)
    pr = jnp.exp(sc - m)
    l = jnp.sum(pr, -1, keepdims=True)
    o = jnp.einsum('bnrhij,bnjrhd->bnirhd', (pr / l).astype(v.dtype), vw)
    lse = jnp.transpose((m + jnp.log(l))[..., 0], (0, 1, 4, 2, 3))
    lse = lse.reshape(b_, lp, dil, h)[:, :L].reshape(b_, s, h)
    o = o.reshape(b_, lp, dil, h, dh)[:, :L].reshape(b_, s, h, dh)
    return o, lse

def dilated_attention(q, k, v, rel_table):
    b_, s, _, h, dh = q.shape
    outs, lses = [], []
    for gi, (w, d) in enumerate(ATT_PATTERNS):
        o, lse = dilated_branch(q[:, :, gi], k, v, rel_table[:, gi * h:(gi + 1) * h], w, d)
        outs.append(o)
        lses.append(lse)
    wgt = jax.nn.softmax(jnp.stack(lses, 0), axis=0)
    o = jnp.einsum('gbsh,gbshd->bshd', wgt.astype(outs[0].dtype), jnp.stack(outs, 0))
    return o.reshape(b_, s, h * dh)

def hybrid_mixer_2(h, w_in, conv_w, conv_b, dt_bias, a_log, d_skip, ssm_norm_g, w_out, rel_table):
    b_, s, _ = h.shape
    z, xbc, dt_raw, q, k, v = jnp.split(h @ w_in, HY_SPLITS, axis=-1)
    xbc = jax.nn.silu(causal_depthwise_conv(xbc, conv_w, conv_b))
    xs, bm, cm = jnp.split(xbc, (SSM_D_INNER, SSM_D_INNER + SSM_GROUPS * SSM_STATE), axis=-1)
    xs = xs.reshape(b_, s, SSM_HEADS, SSM_HEAD_DIM)
    dt = jax.nn.softplus((dt_raw + dt_bias).astype(jnp.float32))
    A = -jnp.exp(a_log.astype(jnp.float32))
    y = ssd_chunked(xs, dt, A, bm.reshape(b_, s, SSM_GROUPS, SSM_STATE), cm.reshape(b_, s, SSM_GROUPS, SSM_STATE))
    y = y + d_skip.astype(jnp.float32)[:, None] * xs.astype(jnp.float32)
    y = y.reshape(b_, s, SSM_D_INNER).astype(h.dtype)
    y = rms_norm(y * jax.nn.silu(z), ssm_norm_g)
    att = dilated_attention(q.reshape(b_, s, ATT_GROUPS, ATT_KV_HEADS, ATT_HEAD_DIM),
                            k.reshape(b_, s, ATT_KV_HEADS, ATT_HEAD_DIM),
                            v.reshape(b_, s, ATT_KV_HEADS, ATT_HEAD_DIM), rel_table)
    return jnp.concatenate([y, att.astype(y.dtype)], axis=-1) @ w_out

def conformer_conv(h, w1, b1, w_dw, b_dw, ln_g, ln_b, w2, b2):
    a, gt = jnp.split(h @ w1 + b1, 2, axis=-1)
    u = a * jax.nn.sigmoid(gt)
    u = causal_depthwise_conv(u, w_dw, b_dw)
    u = jax.nn.silu(layer_norm(u, ln_g, ln_b))
    return u @ w2 + b2

def swiglu(h, wg, wu, wd):
    return (jax.nn.silu(h @ wg) * (h @ wu)) @ wd

def second_inputs(seed: int = 0) -> dict:
    key = jax.random.key(seed)
    ks = iter(jax.random.split(key, 40))
    f32 = jnp.float32

    def nrm(shape, scale=1.0):
        return jax.random.normal(next(ks), shape, f32) * scale

    D = D_MODEL
    dt0 = jnp.exp(jax.random.uniform(next(ks), (N_EVEN, SSM_HEADS), f32, math.log(1e-3), math.log(1e-1)))
    return {
        "x": nrm((BATCH, SEQ, D)),
        "c": nrm((BATCH, D)),
        "ada_w": nrm((DEPTH_2, D, N_MOD * D), 0.5 * D ** -0.5),
        "ada_b": nrm((DEPTH_2, N_MOD * D), 0.02),
        "norm_mix_g": 1.0 + nrm((DEPTH_2, D), 0.05),
        "norm_ffn_g": 1.0 + nrm((DEPTH_2, D), 0.05),
        "hy_w_in": nrm((N_EVEN, D, HY_IN_DIM), D ** -0.5),
        "hy_conv_w": nrm((N_EVEN, SSM_CONV, SSM_CONV_DIM), SSM_CONV ** -0.5),
        "hy_conv_b": nrm((N_EVEN, SSM_CONV_DIM), 0.02),
        "hy_dt_bias": dt0 + jnp.log(-jnp.expm1(-dt0)),
        "hy_a_log": jnp.log(jax.random.uniform(next(ks), (N_EVEN, SSM_HEADS), f32, 1.0, 16.0)),
        "hy_d_skip": 1.0 + nrm((N_EVEN, SSM_HEADS), 0.1),
        "hy_ssm_norm_g": 1.0 + nrm((N_EVEN, SSM_D_INNER), 0.05),
        "hy_w_out": nrm((N_EVEN, HY_OUT_DIM, D), HY_OUT_DIM ** -0.5),
        "rel_table": nrm((REL_BUCKETS, ATT_Q_HEADS), 0.2),
        "cv_w_pw1": nrm((N_ODD, D, 2 * D), D ** -0.5),
        "cv_b_pw1": nrm((N_ODD, 2 * D), 0.02),
        "cv_w_dw": nrm((N_ODD, CONV_WIDTH, D), CONV_WIDTH ** -0.5),
        "cv_b_dw": nrm((N_ODD, D), 0.02),
        "cv_ln_g": 1.0 + nrm((N_ODD, D), 0.05),
        "cv_ln_b": nrm((N_ODD, D), 0.02),
        "cv_w_pw2": nrm((N_ODD, D, D), D ** -0.5),
        "cv_b_pw2": nrm((N_ODD, D), 0.02),
        "ffn_w_gate": nrm((DEPTH_2, D, FFN_HIDDEN), D ** -0.5),
        "ffn_w_up": nrm((DEPTH_2, D, FFN_HIDDEN), D ** -0.5),
        "ffn_w_down": nrm((DEPTH_2, FFN_HIDDEN, D), FFN_HIDDEN ** -0.5),
        "final_norm_g": 1.0 + nrm((D,), 0.05),
    }

def second_block(x, c, ada_w, ada_b, norm_mix_g, norm_ffn_g, hy_w_in, hy_conv_w, hy_conv_b, hy_dt_bias,
              hy_a_log, hy_d_skip, hy_ssm_norm_g, hy_w_out, rel_table, cv_w_pw1, cv_b_pw1, cv_w_dw,
              cv_b_dw, cv_ln_g, cv_ln_b, cv_w_pw2, cv_b_pw2, ffn_w_gate, ffn_w_up, ffn_w_down,
              final_norm_g):
    cs = jax.nn.silu(c)
    for i in range(DEPTH_2):
        mod = cs @ ada_w[i] + ada_b[i]
        sh1, sc1, g1, sh2, sc2, g2 = [m[:, None, :] for m in jnp.split(mod, N_MOD, axis=-1)]
        h = rms_norm(x, norm_mix_g[i]) * (1 + sc1) + sh1
        j = i // 2
        if i % 2 == 0:
            mix = hybrid_mixer_2(h, hy_w_in[j], hy_conv_w[j], hy_conv_b[j], hy_dt_bias[j], hy_a_log[j],
                               hy_d_skip[j], hy_ssm_norm_g[j], hy_w_out[j], rel_table)
        else:
            mix = conformer_conv(h, cv_w_pw1[j], cv_b_pw1[j], cv_w_dw[j], cv_b_dw[j], cv_ln_g[j],
                                 cv_ln_b[j], cv_w_pw2[j], cv_b_pw2[j])
        x = x + g1 * mix
        h = rms_norm(x, norm_ffn_g[i]) * (1 + sc2) + sh2
        x = x + g2 * swiglu(h, ffn_w_gate[i], ffn_w_up[i], ffn_w_down[i])
    return rms_norm(x, final_norm_g)


def setup_inputs(seed=0):
    out = dict(first_inputs(seed))
    for name, value in second_inputs(seed + 1).items():
        if name != "x":
            out[name + "_2"] = value
    return out


def reference(
    x, c, positions, w_ada, b_ada, norm_mix, norm_ffn, w_in, ret_norm, hgrn_norm,
    hgrn_lb_logits, gla_wa2, gla_ba, gla_norm, w_out, router_group_w, router_group_b,
    router_expert_w, router_expert_b, expert_w_gate, expert_w_up, expert_w_down, norm_final,
    c_2, ada_w_2, ada_b_2, norm_mix_g_2, norm_ffn_g_2, hy_w_in_2, hy_conv_w_2, hy_conv_b_2,
    hy_dt_bias_2, hy_a_log_2, hy_d_skip_2, hy_ssm_norm_g_2, hy_w_out_2, rel_table_2, cv_w_pw1_2,
    cv_b_pw1_2, cv_w_dw_2, cv_b_dw_2, cv_ln_g_2, cv_ln_b_2, cv_w_pw2_2, cv_b_pw2_2,
    ffn_w_gate_2, ffn_w_up_2, ffn_w_down_2, final_norm_g_2,
):
    x = first_block(
        x, c, positions, w_ada, b_ada, norm_mix, norm_ffn, w_in, ret_norm, hgrn_norm,
        hgrn_lb_logits, gla_wa2, gla_ba, gla_norm, w_out, router_group_w, router_group_b,
        router_expert_w, router_expert_b, expert_w_gate, expert_w_up, expert_w_down, norm_final,
    )
    return second_block(
        x, c_2, ada_w_2, ada_b_2, norm_mix_g_2, norm_ffn_g_2, hy_w_in_2, hy_conv_w_2,
        hy_conv_b_2, hy_dt_bias_2, hy_a_log_2, hy_d_skip_2, hy_ssm_norm_g_2, hy_w_out_2,
        rel_table_2, cv_w_pw1_2, cv_b_pw1_2, cv_w_dw_2, cv_b_dw_2, cv_ln_g_2, cv_ln_b_2,
        cv_w_pw2_2, cv_b_pw2_2, ffn_w_gate_2, ffn_w_up_2, ffn_w_down_2, final_norm_g_2,
    )


_drawn_inputs = setup_inputs


def setup_inputs(seed=0):
    import zlib

    import numpy as np

    out = dict(_drawn_inputs(seed))
    spreads = {}
    factors = {'norm_mix': 4.782,
     'norm_ffn': 4.519,
     'ret_norm': 6.799,
     'hgrn_norm': 8.0,
     'gla_wa2': 3.099,
     'gla_ba': 6.058,
     'gla_norm': 8.0,
     'router_group_b': 8.0,
     'router_expert_b': 6.1,
     'norm_mix_g_2': 2.903,
     'norm_ffn_g_2': 3.069,
     'hy_conv_b_2': 8.0,
     'hy_d_skip_2': 32.8,
     'hy_ssm_norm_g_2': 4.72,
     'rel_table_2': 8.0,
     'cv_b_pw1_2': 8.0,
     'cv_b_dw_2': 8.0,
     'cv_ln_g_2': 5.306,
     'cv_ln_b_2': 31.939,
     'cv_b_pw2_2': 23.661}
    for name, (base, spread) in spreads.items():
        noise = np.random.default_rng([zlib.crc32(name.encode()), seed]).standard_normal(out[name].shape)
        drawn = base * np.exp(spread * noise) if base else spread * noise
        out[name] = jnp.asarray(drawn.astype(out[name].dtype))
    for name, factor in factors.items():
        out[name] = (out[name] * factor).astype(out[name].dtype)
    return out
```

```python
from contextlib import ExitStack

import concourse.bass as bass
from concourse import mybir

F32 = mybir.dt.float32
I32 = mybir.dt.int32
ALU = mybir.AluOpType
ACT = mybir.ActivationFunctionType
AX = mybir.AxisListType
ds = bass.ds

P = 128
D = 1024
S = 256
TT = S // P
KT = D // P
HD = 64
CW = 256
RING = 6
EPS = 1e-6
F_MIN = 1e-30

RET_W, HGRN_W, GLA_W = 384, 384, 256
RET_H, HGRN_H, GLA_H, GLA_DK = 6, 6, 4, 32
HEADS = RET_H + HGRN_H + GLA_H
TAU = 16.0
RANK = 16
GROUPS, PER_GROUP, EXPERTS = 4, 8, 32
LEVELS = 8

SSM_IN, SSM_H, SSM_G, STATE, CONV = 2048, 32, 4, 128, 4
XBC = SSM_IN + 2 * SSM_G * STATE
XT = XBC // P
ATT_G, KV_H, BUCKETS = 3, 16, 32
TAPS = 31
FFN_CHUNKS = 2816 // CW
NEG = -1e30


class Marks:

    def __init__(self, sem):
        self.sem, self.n = sem, 0


def build(nc, t, out):
    top = ExitStack()
    with top:
        _program(nc, t, out, top)


def _program(nc, t, out, top):
    serial = [0]

    phase_sems = []

    def lasting_sem(name):
        return top.enter_context(nc.semaphore(name))

    def pool_dma_sem(name):
        serial[0] += 1
        return top.enter_context(nc.semaphore(f"{name}_{serial[0]}"))

    def sem(name):
        serial[0] += 1
        scope = ExitStack()
        s = scope.enter_context(nc.semaphore(f"{name}_{serial[0]}"))
        phase_sems.append((scope, s))
        return s

    def clear_phase_sems():
        with nc.Block() as block:
            @block.gpsimd
            def _(pool):
                for _, s in phase_sems:
                    pool.sem_clear(s)
        for scope, _ in reversed(phase_sems):
            scope.close()
        phase_sems.clear()

    def sb(scope, name, shape, dt=F32):
        serial[0] += 1
        return scope.enter_context(nc.sbuf_tensor(f"{name}_{serial[0]}", shape, dt))

    def bc(ap, axis, n):
        v = ap.unsqueeze(axis)
        shape = list(v.shape)
        shape[axis] = n
        return v.broadcast_to(shape)

    ring = sb(top, "ring", [P, RING, 8 * CW])
    X = sb(top, "X", [P, TT, D])
    HT = sb(top, "HT", [P, KT, S])
    ident = sb(top, "ident", [P, P])
    ones = sb(top, "ones", [P, P])
    pairs = sb(top, "pairs", [P, 384])
    mod = sb(top, "mod", [P, 4, KT])
    gate_a = sb(top, "gate_a", [P, D])
    gate_b = sb(top, "gate_b", [P, D])
    stat = sb(top, "stat", [P, 16])
    PS = top.enter_context(nc.psum_tensor("PS", [P, 8, 512], F32))

    landed = [lasting_sem(f"landed{i}") for i in range(RING)]
    used = lasting_sem("used")
    dve_step = Marks(lasting_sem("dve_step"))
    act_step = Marks(lasting_sem("act_step"))
    pool_step = Marks(lasting_sem("pool_step"))

    def stepper(eng, marks):
        def step(ins):
            marks.n += 1
            ins.then_inc(marks.sem, 1)
            eng.wait_ge(marks.sem, marks.n)
        return step

    def pk(w, c0):
        return w.rearrange("(p k) n -> p k n", k=KT)[:, :, ds(c0, CW)]

    def kp(w, c0):
        return w.rearrange("(k p) n -> p k n", p=P)[:, :, ds(c0, CW)]

    hy_groups = [t["hy_w_in"][0]]
    wi, hi = t["w_in"][0], hy_groups[0]
    HY_Z, HY_X, HY_DT, HY_Q = 0, SSM_IN, SSM_IN + XBC, SSM_IN + XBC + SSM_H
    HY_K = HY_Q + ATT_G * KV_H * HD
    HY_V = HY_K + KV_H * HD

    class Segment:
        def __init__(self, name, base, n):
            self.name, self.base, self.n = name, base, n

    stream = []
    segs = {}

    def segment(name, sources):
        segs[name] = Segment(name, len(stream), len(sources))
        stream.extend(sources)

    def expert_order(n):
        order = [("g", 0), ("u", 0)]
        for e in range(1, n):
            order += [("g", e), ("u", e), ("d", e - 1)]
        return order + [("d", n - 1)]

    def moe_source(kind, e):
        if kind == "d":
            return t["expert_w_down"][0][ds(e, 1)].rearrange("a (f p) n -> p (a f) n", p=P)
        w = t["expert_w_gate" if kind == "g" else "expert_w_up"][0]
        return w[ds(e, 1)].rearrange("a (p k) n -> p (a k) n", k=KT)

    def ffn_source(layer):
        def source(kind, e):
            if kind == "d":
                return t["ffn_w_down"][layer][ds(e * CW, CW), :].rearrange("(f p) n -> p f n", p=P)
            return pk(t["ffn_w_gate" if kind == "g" else "ffn_w_up"][layer], e * CW)
        return source

    segment("w_in", [pk(wi, c * CW) for c in range(15)])
    segment("w_out", [pk(t["w_out"][0], c * CW) for c in range(4)])
    segment("moe", [moe_source(k, e) for k, e in expert_order(EXPERTS)])
    segment("hy_x", [pk(hi, HY_X + c * CW) for c in range(12)])
    segment("hy_q", [pk(hi, HY_Q + c * CW) for c in range(12)])
    segment("hy_k", [pk(hi, HY_K + c * CW) for c in range(4)])
    segment("hy_z", [pk(hi, HY_Z + c * CW) for c in range(8)])
    segment("hy_v", [pk(hi, HY_V + c * CW) for c in range(4)])
    hy_out = t["hy_w_out"][0]
    segment("hy_out", [hy_out[g * D:(g + 1) * D, :].rearrange("(p k) n -> p k n", k=KT)[:, :, c * CW:(c + 1) * CW]
                       for c in range(4) for g in range(3)])
    segment("ffn0", [ffn_source(0)(k, e) for k, e in expert_order(FFN_CHUNKS)])
    segment("pw1", [pk(t["cv_w_pw1"][0], h * D + c * CW) for c in range(4) for h in range(2)])
    segment("pw2", [kp(t["cv_w_pw2"][0], c * CW) for c in range(4)])
    segment("ffn1", [ffn_source(1)(k, e) for k, e in expert_order(FFN_CHUNKS)])

    sent = [0]

    def send(sp, source, n):
        if n >= RING:
            sp.wait_ge(used, n - RING + 1)
        shape = source.shape
        dst = ring[:, n % RING, :].rearrange("p (a b) -> p a b", b=shape[2])
        sp.dma_start(dst, source).then_inc(landed[n % RING], 16)

    def send_until(sp, end):
        stop = min(end + RING, len(stream))
        while sent[0] < stop:
            send(sp, stream[sent[0]], sent[0])
            sent[0] += 1

    def arrive(pe, n):
        pe.wait_ge(landed[n % RING], 16 * (n // RING + 1))

    def w_slot(n, b=CW):
        return ring[:, n % RING, :].rearrange("p (a b) -> p a b", b=b)

    tok = lambda ap: ap.rearrange("(t p) n -> p t n", p=P)

    load0 = sem("load0")
    with nc.Block() as block:
        @block.sync
        def _(sp):
            sp.dma_start(X[:], tok(t["x"][0])).then_inc(load0, 16)
            sp.dma_start(ident[:], t["const_ident"]).then_inc(load0, 16)
            sp.dma_start(pairs[:], t["const_pairs"]).then_inc(load0, 16)
            send_until(sp, 0)
            sp.wait_ge(load0, 48)

        @block.vector
        def _(dve):
            dve.memset(ones[:], 1.0)

    def modulation(c_in, w, b, gain_mix, gain_ffn):
        NB, W = 6, 2048
        n_chunks = KT * (6 * D // W)
        with ExitStack() as scope:
            stage = sb(scope, "ada_stage", [P, NB, W])
            acc = sb(scope, "ada_acc", [P, 6 * D])
            cv = sb(scope, "ada_c", [P, KT])
            bias = sb(scope, "ada_b", [P, 6, KT])
            gains = sb(scope, "ada_gain", [P, 2, KT])
            small, zeroed, brow = sem("ada_small"), sem("ada_zeroed"), sem("ada_brow")
            arrived = [sem(f"ada_arrived{i}") for i in range(NB)]
            c_ready, summed, cols, rows, taken = (sem("ada_c_ready"), sem("ada_summed"), sem("ada_cols"),
                                                  sem("ada_rows"), sem("ada_taken"))
            wv = w.rearrange("(p k) (g n) -> p k g n", k=KT, n=W)
            with nc.Block() as block:
                @block.sync
                def _(sp):
                    sp.dma_start(cv[:], c_in[0].rearrange("(p k) -> p k", k=KT)).then_inc(small, 16)
                    sp.dma_start(bias[:], b.rearrange("(s p k) -> p s k", p=P, k=KT)).then_inc(small, 16)
                    sp.dma_start(gains[:, 0, :], gain_mix.rearrange("(p k) -> p k", k=KT)).then_inc(small, 16)
                    sp.dma_start(gains[:, 1, :], gain_ffn.rearrange("(p k) -> p k", k=KT)).then_inc(small, 16)
                    sp.wait_ge(zeroed, 1)
                    sp.dma_start(acc[0:1, :], b.rearrange("(a n) -> a n", a=1)).then_inc(brow, 16)
                    for n in range(n_chunks):
                        if n >= NB:
                            sp.wait_ge(summed, n - NB + 1)
                        sp.dma_start(stage[:, n % NB, :], wv[:, n % KT, n // KT, :]).then_inc(arrived[n % NB], 16)

                @block.gpsimd
                def _(pool):
                    pool.memset(acc[:], 0.0).then_inc(zeroed, 1)

                @block.scalar
                def _(act):
                    act.wait_ge(small, 64)
                    act.activation(cv[:], cv[:], ACT.Silu).then_inc(c_ready, 1)

                @block.vector
                def _(dve):
                    step = stepper(dve, dve_step)
                    dve.wait_ge(c_ready, 1)
                    dve.wait_ge(brow, 16)
                    for n in range(n_chunks):
                        dve.wait_ge(arrived[n % NB], 16 * (n // NB + 1))
                        if n % KT:
                            dve.wait_ge(summed, n)
                        a = acc[:, (n // KT) * W:(n // KT + 1) * W]
                        dve.scalar_tensor_tensor(out=a, in0=stage[:, n % NB, :], scalar=cv[:, n % KT:n % KT + 1],
                                                 in1=a, op0=ALU.mult, op1=ALU.add).then_inc(summed, 1)
                    dve.wait_ge(cols, 1)
                    cp = PS[:, 0, 0:4 * KT].rearrange("p (s k) -> p s k", k=KT)
                    for j in range(2):
                        dve.tensor_copy(mod[:, 2 * j, :], cp[:, 2 * j, :])
                        dve.scalar_tensor_tensor(out=mod[:, 2 * j + 1, :], in0=cp[:, 2 * j + 1, :], scalar=1.0,
                                                 in1=gains[:, j, :], op0=ALU.add, op1=ALU.mult)
                    dve.wait_ge(rows, 1)
                    dve.tensor_copy(gate_a[:], PS[:, 1:3, :])
                    dve.tensor_copy(gate_b[:], PS[:, 3:5, :])

                @block.tensor
                def _(pe):
                    pe.wait_ge(summed, n_chunks)
                    for s, seg in enumerate((0, 1, 3, 4)):
                        v = acc[:, seg * D:(seg + 1) * D].rearrange("p (m k) -> p k m", k=KT)
                        for k in range(KT):
                            mm = pe.matmul(PS[:, 0, s * KT + k:s * KT + k + 1], v[:, k, :], ones[:, 0:1],
                                           start=True, stop=True)
                    mm.then_inc(cols, 1)
                    for j, seg in enumerate((2, 5)):
                        for h in range(2):
                            mm = pe.matmul(PS[:, 1 + 2 * j + h, :], ones[:],
                                           acc[:, seg * D + h * 512:seg * D + (h + 1) * 512], start=True, stop=True)
                    mm.then_inc(rows, 1)

    def norm_block(scale, shift):
        squared, meaned, rooted, scaled, turned, evacuated = (sem("n_squared"), sem("n_meaned"), sem("n_rooted"),
                                                              sem("n_scaled"), sem("n_turned"), sem("n_evac"))
        with ExitStack() as scope:
            xn = sb(scope, "xn", [P, TT, D])
            with nc.Block() as block:
                @block.scalar
                def _(act):
                    for i in range(TT):
                        act.activation(xn[:, i, :], X[:, i, :], ACT.Square,
                                       accum_out=stat[:, i:i + 1]).then_inc(squared, 1)
                    act.wait_ge(meaned, 1)
                    act.activation(stat[:, 4:6], stat[:, 2:4], ACT.Sqrt).then_inc(rooted, 1)

                @block.vector
                def _(dve):
                    step = stepper(dve, dve_step)
                    dve.wait_ge(squared, TT)
                    dve.tensor_scalar(stat[:, 2:4], stat[:, 0:2], 1.0 / D, EPS, ALU.mult, ALU.add).then_inc(meaned, 1)
                    dve.wait_ge(rooted, 1)
                    step(dve.reciprocal(stat[:, 6:8], stat[:, 4:6]))
                    for i in range(TT):
                        dve.tensor_scalar(xn[:, i, :], X[:, i, :], stat[:, 6 + i:7 + i], None,
                                          ALU.mult).then_inc(scaled, 1)
                    for k in range(KT):
                        dve.wait_ge(turned, k + 1)
                        dve.tensor_scalar(HT[:, k, :], PS[:, k % 4, 0:S], scale[:, k:k + 1], shift[:, k:k + 1],
                                          ALU.mult, ALU.add).then_inc(evacuated, 1)

                @block.tensor
                def _(pe):
                    pe.wait_ge(scaled, TT)
                    for k in range(KT):
                        if k >= 4:
                            pe.wait_ge(evacuated, k - 3)
                        for i in range(TT):
                            mm = pe.transpose(PS[:, k % 4, i * P:(i + 1) * P],
                                              xn[:, i, :].rearrange("p (m k) -> p k m", k=KT)[:, k, :], ident[:])
                        mm.then_inc(turned, 1)

    def plain_norm(gain, result):
        with ExitStack() as scope:
            fg = sb(scope, "final_gain", [P, D])
            yo = sb(scope, "result", [P, TT, D])
            fin, squared, meaned, rooted, done, outs = (sem("f_gain"), sem("f_squared"), sem("f_meaned"), sem("f_rooted"),
                                                        sem("f_done"), sem("f_out"))
            with nc.Block() as block:
                @block.sync
                def _(sp):
                    sp.dma_start(fg[:], gain.partition_broadcast(P)).then_inc(fin, 16)
                    if result is not None:
                        for i in range(TT):
                            sp.wait_ge(done, i + 1)
                            sp.dma_start(result[0, i * P:(i + 1) * P, :], X[:, i, :]).then_inc(outs, 16)
                        sp.wait_ge(outs, 16 * TT)

                @block.scalar
                def _(act):
                    for i in range(TT):
                        act.activation(yo[:, i, :], X[:, i, :], ACT.Square, accum_out=stat[:, i:i + 1]).then_inc(squared, 1)
                    act.wait_ge(meaned, 1)
                    act.activation(stat[:, 4:6], stat[:, 2:4], ACT.Sqrt).then_inc(rooted, 1)

                @block.vector
                def _(dve):
                    step = stepper(dve, dve_step)
                    dve.wait_ge(squared, TT)
                    dve.tensor_scalar(stat[:, 2:4], stat[:, 0:2], 1.0 / D, EPS, ALU.mult, ALU.add).then_inc(meaned, 1)
                    dve.wait_ge(rooted, 1)
                    step(dve.reciprocal(stat[:, 6:8], stat[:, 4:6]))
                    dve.wait_ge(fin, 16)
                    for i in range(TT):
                        dve.scalar_tensor_tensor(out=X[:, i, :], in0=X[:, i, :], scalar=stat[:, 6 + i:7 + i], in1=fg[:],
                                                 op0=ALU.mult, op1=ALU.mult).then_inc(done, 1)

    def rows_chunk(pe, n, bank, src=None, start=True, stop=True):
        src = HT if src is None else src
        w = w_slot(n)
        for m in range(2):
            for k in range(KT):
                mm = pe.matmul(PS[:, bank, m * S:(m + 1) * S], w[:, k, m * P:(m + 1) * P], src[:, k, :],
                               start=(k == 0), stop=(k == KT - 1))
        return mm

    def tokens_chunk(pe, n, bank, src=None, k0=0, start=True, stop=True):
        src = HT if src is None else src
        w = w_slot(n)
        for i in range(TT):
            for k in range(KT):
                mm = pe.matmul(PS[:, bank, i * CW:(i + 1) * CW], src[:, k0 + k, i * P:(i + 1) * P], w[:, k, :],
                               start=(k == 0), stop=(k == KT - 1))
        return mm

    def project(parts, after=None):
        moved = sem("p_moved")
        todo = [(segs[s].base + c0 + j, kind, ev, j) for s, c0, n, kind, ev in parts for j in range(n)]
        with nc.Block() as block:
            @block.sync
            def _(sp):
                send_until(sp, todo[-1][0] + 1)

            @block.tensor
            def _(pe):
                for q, (n, kind, _, _) in enumerate(todo):
                    arrive(pe, n)
                    if q >= 4:
                        pe.wait_ge(moved, q - 3)
                    mm = (rows_chunk if kind == "rows" else tokens_chunk)(pe, n, q % 4)
                    mm.then_inc(used, 1)

            @block.scalar
            def _(act):
                for q, (n, kind, ev, j) in enumerate(todo):
                    act.wait_ge(used, n + 1)
                    ev(act, PS[:, q % 4, :].rearrange("p (a b) -> p a b", a=2), j).then_inc(moved, 1)

    def experts(name, source, count, combine, gate):
        base = segs[name].base
        hid_ready, weighted, silu_ready = sem("e_hid"), sem("e_weighted"), sem("e_silu")
        pairs_n = (count - 2) // 2
        left = (count - 2) % 2
        order = expert_order(count)
        B0 = base + 5
        with ExitStack() as scope:
            silu = sb(scope, "silu", [P, 2, 2, S])
            upc = sb(scope, "upc", [P, 2, 2, S])
            hid = sb(scope, "hid", [P, 2, 2, S])
            with nc.Block() as block:
                def bank(kind, par):
                    return 2 * par + (kind == "u")

                @block.sync
                def _(sp):
                    assert sent[0] == base + RING
                    with sp.Fori(0, pairs_n - 1) as i:
                        for j in range(6):
                            idx = RING + j
                            kind, e = order[idx]
                            sp.wait_ge(used, base + idx - RING + 1 + i * 6)
                            src = source(kind, e + i * 2)
                            n = base + idx
                            dst = ring[:, n % RING, :].rearrange("p (a b) -> p a b", b=src.shape[2])
                            sp.dma_start(dst, src).then_inc(landed[n % RING], 16)
                    sent[0] += 6 * (pairs_n - 1)
                    send_until(sp, base + len(order))

                @block.tensor
                def _(pe):
                    def up_gate(kind, n, par):
                        rows_chunk(pe, n, bank(kind, par)).then_inc(used, 1)

                    def down(n, par, first, last):
                        w = w_slot(n, D)
                        for f in range(2):
                            for i in range(TT):
                                for h in range(2):
                                    mm = pe.matmul(PS[:, 4 + 2 * i + h, :], hid[:, par, f, i * P:(i + 1) * P],
                                                   w[:, f, h * 512:(h + 1) * 512], start=first and f == 0,
                                                   stop=last and f == 1)
                        mm.then_inc(used, 1)

                    for idx in range(5):
                        kind, e = order[idx]
                        arrive(pe, base + idx)
                        if kind == "d":
                            pe.wait_ge(hid_ready, e + 1)
                            down(base + idx, e % 2, True, False)
                        else:
                            up_gate(kind, base + idx, e % 2)
                    with pe.Fori(0, pairs_n) as i:
                        for j in range(6):
                            kind, e = order[5 + j]
                            n = B0 + j
                            pe.wait_ge(landed[n % RING], i * 16 + 16 * (n // RING + 1))
                            if kind == "d":
                                pe.wait_ge(hid_ready, i * 2 + e + 1)
                                down(n, e % 2, False, False)
                            else:
                                up_gate(kind, n, e % 2)
                    for idx in range(5 + 6 * pairs_n, len(order)):
                        kind, e = order[idx]
                        arrive(pe, base + idx)
                        if kind == "d":
                            pe.wait_ge(hid_ready, e + 1)
                            down(base + idx, e % 2, False, e == count - 1)
                        else:
                            up_gate(kind, base + idx, e % 2)

                def up_done(e):
                    return base + (2 if e == 0 else 3 * e + 1)

                @block.scalar
                def _(act):
                    def one(par, gate_done):
                        act.wait_ge(used, gate_done)
                        act.activation(silu[:, par], PS[:, 2 * par, :].rearrange("p (a b) -> p a b", a=2),
                                       ACT.Silu).then_inc(silu_ready, 1)
                    one(0, up_done(0) - 1)
                    one(1, up_done(1) - 1)
                    with act.Fori(0, pairs_n) as i:
                        one(0, i * 6 + up_done(2) - 1)
                        one(1, i * 6 + up_done(3) - 1)
                    for e in range(2 + 2 * pairs_n, count):
                        one(e % 2, up_done(e) - 1)

                @block.vector
                def _(dve):
                    def one(par, up, e, nth):
                        dve.wait_ge(used, up)
                        u = PS[:, 2 * par + 1, :].rearrange("p (a b) -> p a b", a=2)
                        if combine is not None:
                            dve.tensor_tensor(upc[:, par], u, bc(combine(e), 1, 2), ALU.mult).then_inc(weighted, 1)
                            dve.wait_ge(weighted, nth)
                            u = upc[:, par]
                        dve.wait_ge(silu_ready, nth)
                        dve.tensor_tensor(hid[:, par], u, silu[:, par], ALU.mult).then_inc(hid_ready, 1)

                    one(0, up_done(0), 0, 1)
                    one(1, up_done(1), 1, 2)
                    with dve.Fori(0, pairs_n) as i:
                        one(0, i * 6 + up_done(2), i * 2 + 2, i * 2 + 3)
                        one(1, i * 6 + up_done(3), i * 2 + 3, i * 2 + 4)
                    for e in range(2 + 2 * pairs_n, count):
                        one(e % 2, up_done(e), e, e + 1)
                    dve.wait_ge(used, base + len(order))
                    step = stepper(dve, dve_step)
                    add_gated(dve, step, PS[:, 4:8, :].rearrange("p (i h) n -> p i (h n)", i=TT), gate, scope)

    def add_gated(dve, step, psum, gate, scope):
        tmp = sb(scope, "gated", [P, TT, D])
        step(dve.tensor_tensor(tmp[:], psum, bc(gate[:], 1, TT), ALU.mult))
        step(dve.tensor_tensor(X[:], X[:], tmp[:], ALU.add))

    def output_projection(seg, src, groups, gate, bias=None):
        base = segs[seg].base
        with ExitStack() as scope:
            tmp = sb(scope, "op_tmp", [P, 2, TT, CW])
            moved = sem("o_moved")
            with nc.Block() as block:
                @block.sync
                def _(sp):
                    send_until(sp, base + 4 * groups)

                @block.tensor
                def _(pe):
                    for c in range(4):
                        for i in range(TT):
                            if i == 0:
                                for g in range(groups):
                                    arrive(pe, base + c * groups + g)
                            if bias is not None:
                                pe.matmul(PS[:, c, i * CW:(i + 1) * CW], ones[0:1, :], bias[0:1, c * CW:(c + 1) * CW],
                                          start=True, stop=False)
                            for g in range(groups):
                                w = w_slot(base + c * groups + g)
                                for k in range(KT):
                                    mm = pe.matmul(PS[:, c, i * CW:(i + 1) * CW],
                                                   src[:, g * KT + k, i * P:(i + 1) * P], w[:, k, :],
                                                   start=(bias is None and g == 0 and k == 0),
                                                   stop=(g == groups - 1 and k == KT - 1))
                                if i == TT - 1:
                                    mm.then_inc(used, 1)

                @block.vector
                def _(dve):
                    step = stepper(dve, dve_step)
                    for c in range(4):
                        dve.wait_ge(used, base + (c + 1) * groups)
                        step(dve.tensor_tensor(tmp[:, c % 2], PS[:, c, :].rearrange("p (i n) -> p i n", i=TT),
                                               bc(gate[:, c * CW:(c + 1) * CW], 1, TT), ALU.mult))
                        xc = X[:, :, c * CW:(c + 1) * CW]
                        step(dve.tensor_tensor(xc, xc, tmp[:, c % 2], ALU.add))

    def turn_features(src, dst, groups, gain):
        turned, moved = sem("t_turned"), sem("t_moved")
        n = groups * KT
        with nc.Block() as block:
            @block.tensor
            def _(pe):
                for k in range(n):
                    if k >= 4:
                        pe.wait_ge(moved, k - 3)
                    for i in range(TT):
                        v = src[:, i, (k // KT) * D:(k // KT + 1) * D].rearrange("p (m k) -> p k m", k=KT)
                        mm = pe.transpose(PS[:, k % 4, i * P:(i + 1) * P], v[:, k % KT, :], ident[:])
                    mm.then_inc(turned, 1)

            @block.vector
            def _(dve):
                for k in range(n):
                    dve.wait_ge(turned, k + 1)
                    if gain is None:
                        dve.tensor_copy(dst[:, k, :], PS[:, k % 4, 0:S]).then_inc(moved, 1)
                    else:
                        dve.tensor_scalar(dst[:, k, :], PS[:, k % 4, 0:S], gain[:, k:k + 1], None,
                                          ALU.mult).then_inc(moved, 1)

    modulation(t["c"], t["w_ada"][0], t["b_ada"][0], t["norm_mix"][0], t["norm_ffn"][0])
    norm_block(mod[:, 1, :], mod[:, 0, :])

    with ExitStack() as scope:
        merged = sb(scope, "merged", [P, TT, D])
        mix_gain = sb(scope, "mix_gain", [P, KT])
        inner = ExitStack()
        RT = sb(inner, "ret_tok", [P, TT, 4 * RET_W])
        HG = sb(inner, "hgrn_tok", [P, TT, 2 * HGRN_W])
        GG = sb(inner, "gla_tok", [P, TT, 2 * GLA_W])
        HF = sb(inner, "hgrn_rows", [P, 6, S])
        GF = sb(inner, "gla_rows", [P, 2, S])
        gaT = sb(inner, "gla_rank", [RANK, S])
        decay = sb(inner, "ret_decay", [P, RET_H, 384])
        level_mask = sb(inner, "level_mask", [P, LEVELS, P])
        freq = sb(inner, "freq", [P, 32])
        pos = sb(inner, "pos", [P, TT], I32)
        posf = sb(inner, "posf", [P, TT])
        wga = sb(inner, "wga", [P, KT, RANK])
        wa2 = sb(inner, "wa2", [RANK, P])
        gba = sb(inner, "gba", [P, 1])
        lb = sb(inner, "lb", [P, 8, 3])
        small = pool_dma_sem("mix_small")

        def mover(dst, width):
            def ev(act, bank, j):
                return act.activation(dst[:, :, j * CW:(j + 1) * CW] if width == "tokens" else
                                      dst[:, 2 * j:2 * j + 2, :], bank, ACT.Copy)
            return ev

        with nc.allow_non_contiguous_dma(reason="a few small vectors"):
            with nc.Block() as block:
                @block.gpsimd
                def _(pool):
                    loads = [
                        (decay[:], t["const_decay"]), (level_mask[:], t["const_levels"]),
                        (freq[:], t["const_freq"]),
                        (pos[:], t["positions"][0].rearrange("(i p) -> p i", p=P)),
                        (wga[:], wi[:, 15 * CW:].rearrange("(p k) n -> p k n", k=KT)),
                        (wa2[:], t["gla_wa2"][0]), (gba[:], t["gla_ba"][0].rearrange("(p a) -> p a", a=1)),
                        (lb[:, 0, :], t["hgrn_lb_logits"][0].rearrange("(m p) -> p m", p=P)),
                        (mix_gain[0:48, :], t["ret_norm"][0].rearrange("(p k) -> p k", k=KT)),
                        (mix_gain[48:96, :], t["hgrn_norm"][0].rearrange("(p k) -> p k", k=KT)),
                        (mix_gain[96:128, :], t["gla_norm"][0].rearrange("(p k) -> p k", k=KT)),
                    ]
                    for dst, src in loads:
                        pool.dma_start(dst, src).then_inc(small, 16)
                    pool.wait_ge(small, 16 * len(loads))

        project([("w_in", 0, 6, "tokens", mover(RT, "tokens")), ("w_in", 6, 3, "rows", mover(HF, "rows")),
                 ("w_in", 9, 3, "tokens", mover(HG, "tokens")), ("w_in", 12, 1, "rows", mover(GF, "rows")),
                 ("w_in", 13, 2, "tokens", mover(GG, "tokens"))])

        qd = sb(inner, "gated_q", [P, 4, S])
        kd = sb(inner, "gated_k", [P, 4, S])
        ad = sb(inner, "gated_a", [P, 4, S])
        g_low, g_gate, g_sig, g_e = sem("g_low"), sem("g_gate"), sem("g_sig"), sem("g_e")
        lb_e, ang, trig, lowc = sem("lb_e"), sem("ang"), sem("trig"), sem("lowc")
        y_ready, ln_ready, e_ready = sem("y_ready"), sem("ln_ready"), sem("e_ready")
        narrow = ExitStack()
        w1 = sb(narrow, "gla_w", [P, 3, S])
        rot = sb(narrow, "rot", [P, 2, TT, 2 * RET_W])
        angle = sb(narrow, "angle", [P, 6, TT, 32])
        MAGIC = 12582912.0
        with nc.Block() as block:
            @block.tensor
            def _(pe):
                for k in range(KT):
                    mm = pe.matmul(PS[0:RANK, 0, 0:S], wga[:, k, :], HT[:, k, :], start=(k == 0), stop=(k == KT - 1))
                mm.then_inc(g_low, 1)
                pe.wait_ge(lowc, 1)
                pe.matmul(PS[:, 1, 0:S], wa2[:], gaT[:], start=True, stop=True).then_inc(g_gate, 1)

            @block.scalar
            def _(act):
                act.wait_ge(g_low, 1)
                act.activation(gaT[:], PS[0:RANK, 0, 0:S], ACT.Copy).then_inc(lowc, 1)
                act.activation(kd[:, 0:3, :], HF[:, 3:6, :], ACT.Sigmoid, scale=-1.0)
                act.activation(ad[:, 0:3, :], HF[:, 3:6, :], ACT.Sigmoid).then_inc(g_sig, 1)
                act.activation(qd[:, 0:3, :], HF[:, 0:3, :], ACT.Silu).then_inc(g_sig, 1)
                act.activation(RT[:, :, 3 * RET_W:], RT[:, :, 3 * RET_W:], ACT.Silu)
                act.activation(HG[:, :, HGRN_W:], HG[:, :, HGRN_W:], ACT.Silu)
                act.activation(GG[:, :, GLA_W:], GG[:, :, GLA_W:], ACT.Silu)
                act.wait_ge(lb_e, 1)
                act.activation(lb[:, 2, :], lb[:, 1, :], ACT.Exp).then_inc(lb_e, 1)
                act.wait_ge(y_ready, 1)
                act.activation(w1[:, 1, :], w1[:, 1, :], ACT.Exp).then_inc(e_ready, 1)
                act.wait_ge(e_ready, 1)
                act.activation(w1[:, 2, :], w1[:, 1, :], ACT.Ln, bias=1.0).then_inc(ln_ready, 1)
                act.wait_ge(y_ready, 2)
                act.activation(ad[:, 3, :], w1[:, 0, :], ACT.Exp, scale=1.0 / TAU)
                act.wait_ge(ang, 1)
                act.activation(angle[:, 4:6], angle[:, 2:4], ACT.Sin).then_inc(trig, 1)

            @block.vector
            def _(dve):
                step = stepper(dve, dve_step)
                dve.wait_ge(g_gate, 1)
                step(dve.tensor_scalar(w1[:, 0, :], PS[:, 1, 0:S], gba[:, 0:1], None, ALU.add))
                step(dve.tensor_scalar(w1[:, 2, :], w1[:, 0, :], -1.0, None, ALU.mult))
                dve.tensor_tensor(w1[:, 1, :], w1[:, 0, :], w1[:, 2, :], ALU.min).then_inc(y_ready, 1)
                dve.tensor_tensor(lb[:, 1, :], lb[:, 0, :], lb[:, 0, :], ALU.subtract).then_inc(lb_e, 1)
                dve.wait_ge(lb_e, 2)
                step(dve.reciprocal(lb[:, 3, :], lb[:, 2, :]))
                step(dve.tensor_tensor(lb[:, 4, :], lb[:, 2, :], lb[:, 3, :], ALU.mult))
                step(dve.tensor_tensor(lb[:, 5, :], lb[:, 4, :], lb[:, 4, :], ALU.subtract))
                step(dve.tensor_scalar(lb[:, 6, :], lb[:, 5, :], -1.0, 1.0, ALU.mult, ALU.add))
                step(dve.tensor_copy(posf[:], pos[:]))
                for i in range(TT):
                    step(dve.tensor_scalar(angle[:, 0, i, :], freq[:], posf[:, i:i + 1], None, ALU.mult))
                step(dve.tensor_scalar(angle[:, 1], angle[:, 0], 0.15915494309189535, MAGIC, ALU.mult, ALU.add))
                step(dve.tensor_scalar(angle[:, 1], angle[:, 1], -MAGIC, None, ALU.add))
                for piece in (6.28125, 1.93530321e-03, 6.283185307179586 - 6.28125 - 1.93530321e-03):
                    step(dve.scalar_tensor_tensor(out=angle[:, 0], in0=angle[:, 1], scalar=-piece, in1=angle[:, 0],
                                                  op0=ALU.mult, op1=ALU.add))
                step(dve.tensor_scalar(angle[:, 2], angle[:, 0], 3.1415925, -3.1415925, ALU.min, ALU.max))
                step(dve.tensor_scalar(angle[:, 4], angle[:, 2], -1.0, None, ALU.mult))
                step(dve.tensor_tensor(angle[:, 3], angle[:, 2], angle[:, 4], ALU.max))
                dve.tensor_scalar(angle[:, 3], angle[:, 3], -1.0, 1.5707963267948966, ALU.mult,
                                  ALU.add).then_inc(ang, 1)
                dve.wait_ge(g_sig, 2)
                for m in range(3):
                    dve.tensor_scalar(ad[:, m, :], ad[:, m, :], lb[:, 6, m:m + 1], lb[:, 5, m:m + 1], ALU.mult, ALU.add)
                    dve.tensor_scalar(kd[:, m, :], kd[:, m, :], lb[:, 6, m:m + 1], None, ALU.mult)
                step(dve.tensor_scalar(qd[:, 0:3, :], qd[:, 0:3, :], HD ** -0.5, None, ALU.mult))
                step(dve.tensor_scalar(ad[:, 0:3, :], ad[:, 0:3, :], F_MIN, None, ALU.max))
                dve.tensor_scalar(qd[:, 3, :], GF[:, 0, :], GLA_DK ** -0.5, None, ALU.mult)
                dve.tensor_copy(kd[:, 3, :], GF[:, 1, :])
                dve.wait_ge(ln_ready, 1)
                dve.scalar_tensor_tensor(out=w1[:, 0, :], in0=w1[:, 0, :], scalar=0.0, in1=w1[:, 2, :],
                                         op0=ALU.min, op1=ALU.subtract).then_inc(y_ready, 1)
                dve.wait_ge(trig, 1)
                for i in range(TT):
                    qk = RT[:, i, 0:2 * RET_W].rearrange("p (h a d) -> p h a d", a=2, d=32)
                    for j, tab in ((0, 5), (1, 4)):
                        for a in range(2):
                            last = dve.tensor_tensor(rot[:, j, i, :].rearrange("p (h a d) -> p h a d", a=2, d=32)[:, :, a, :],
                                              qk[:, :, a, :], bc(angle[:, tab, i, :], 1, 2 * RET_H), ALU.mult)
                    c4 = rot[:, 0, i, :].rearrange("p (h a d) -> p h a d", a=2, d=32)
                    s4 = rot[:, 1, i, :].rearrange("p (h a d) -> p h a d", a=2, d=32)
                    step(last)
                    dve.tensor_tensor(qk[:, :, 0, :], c4[:, :, 0, :], s4[:, :, 1, :], ALU.subtract)
                    dve.tensor_tensor(qk[:, :, 1, :], c4[:, :, 1, :], s4[:, :, 0, :], ALU.add)

        narrow.close()

        QT = sb(inner, "ret_T", [P, 6, S])
        SW = sb(inner, "ret_scores", [P, 2, 384])
        QL = sb(inner, "level_q", [P, LEVELS, 2, S])
        KL = sb(inner, "level_k", [P, LEVELS, 2, S])
        prefix = sb(inner, "prefix", [P, 2, S])
        suffix = sb(inner, "suffix", [P, 2, S])

        def o_cols(head, i):
            c = head * HD
            return PS[:, 4 + 2 * i + c // 512, c % 512:c % 512 + HD]

        def level_factors(pool, m0):
            step = stepper(pool, pool_step)
            qs, ks = qd[:, m0:m0 + 2, :], kd[:, m0:m0 + 2, :]
            pool.tensor_copy(prefix[:], ad[:, m0:m0 + 2, :])
            step(pool.memset(suffix[:], 1.0))
            for l in range(1, LEVELS + 1):
                b = 1 << (l - 1)
                pool.tensor_tensor(QL[:, l % LEVELS], qs, prefix[:], ALU.mult)
                step(pool.tensor_tensor(KL[:, l % LEVELS], ks, suffix[:], ALU.mult))
                if l < LEVELS:
                    n = 2 * S // (2 * b)
                    pv = prefix[:].rearrange("p m t -> p (m t)").rearrange("p (n h b) -> p n h b", h=2, b=b)
                    sv = suffix[:].rearrange("p m t -> p (m t)").rearrange("p (n h b) -> p n h b", h=2, b=b)
                    step(pool.tensor_tensor(sv[:, :, 0, :], sv[:, :, 0, :],
                                            pv[:, :, 1, b - 1:b].broadcast_to([P, n, b]), ALU.mult))
                    step(pool.tensor_tensor(pv[:, :, 1, :], pv[:, :, 1, :],
                                            pv[:, :, 0, b - 1:b].broadcast_to([P, n, b]), ALU.mult))

        turned, tmoved, r_sc, r_w = sem("r_turned"), sem("r_tmoved"), sem("r_scores"), sem("r_weights")
        with nc.Block() as block:
            @block.gpsimd
            def _(pool):
                level_factors(pool, 0)

            @block.tensor
            def _(pe):
                for j in range(6):
                    if j >= 4:
                        pe.wait_ge(tmoved, j - 3)
                    for i in range(TT):
                        mm = pe.transpose(PS[:, j % 4, i * P:(i + 1) * P], RT[:, i, j * P:(j + 1) * P], ident[:])
                    mm.then_inc(turned, 1)
                pe.wait_ge(tmoved, 6)

                def values(h):
                    pe.wait_ge(r_w, h + 1)
                    w = SW[:, h % 2, :]
                    v = RT[:, :, 2 * RET_W + h * HD:2 * RET_W + (h + 1) * HD]
                    pe.matmul(o_cols(h, 0), w[:, 0:P], v[:, 0, :], start=True, stop=True)
                    pe.matmul(o_cols(h, 1), w[:, P:2 * P], v[:, 0, :], start=True, stop=False)
                    pe.matmul(o_cols(h, 1), w[:, 2 * P:3 * P], v[:, 1, :], start=False, stop=True)

                for h in range(RET_H):
                    r0, m = HD * (h % 2), h // 2
                    q, k = QT[r0:r0 + HD, m, :], QT[r0:r0 + HD, 3 + m, :]
                    pe.matmul(PS[:, h % 4, 0:S], k[:, 0:P], q, start=True, stop=True)
                    pe.matmul(PS[:, h % 4, S:384], k[:, P:S], q[:, P:S], start=True, stop=True).then_inc(r_sc, 1)
                    if h:
                        values(h - 1)
                values(RET_H - 1)

            @block.vector
            def _(dve):
                for j in range(6):
                    dve.wait_ge(turned, j + 1)
                    dve.tensor_copy(QT[:, j, :], PS[:, j % 4, 0:S]).then_inc(tmoved, 1)
                for h in range(RET_H):
                    dve.wait_ge(r_sc, h + 1)
                    dve.scalar_tensor_tensor(out=SW[:, h % 2, :], in0=PS[:, h % 4, 0:384], scalar=HD ** -0.5,
                                             in1=decay[:, h, :], op0=ALU.mult, op1=ALU.mult).then_inc(r_w, 1)

        GWT = sb(inner, "gated_scores", [P, 2, LEVELS, P])
        CR = sb(inner, "cross", [P, 6, P])

        def cross_place(gated, c):
            r0 = gated[c][1]
            k = sum(g[1] == r0 for g in gated[:c])
            return PS[:, r0 // 32, k * P:(k + 1) * P]

        def gated_heads(gated, m0):
            g_sc, g_w, g_cr, g_crw = sem("g_scores"), sem("g_weights"), sem("g_cross"), sem("g_crossw")
            units = [(g, i) for g in gated for i in range(TT)]
            n = len(gated)
            with nc.Block() as block:
                @block.tensor
                def _(pe):
                    for c, (m, r0, dk, _, _, _) in enumerate(gated):
                        mm = pe.matmul(cross_place(gated, c), KL[r0:r0 + dk, 0, m - m0, 0:P],
                                       QL[r0:r0 + dk, 0, m - m0, P:S], start=True, stop=True)
                    mm.then_inc(g_cr, 1)
                    pe.wait_ge(g_crw, 1)

                    def scores(u):
                        (m, r0, dk, _, _, _), i = units[u]
                        for l in range(LEVELS):
                            q = (qd[r0:r0 + dk, m] if l == 0 else QL[r0:r0 + dk, l, m - m0])[:, i * P:(i + 1) * P]
                            k = (kd[r0:r0 + dk, m] if l == 0 else KL[r0:r0 + dk, l, m - m0])[:, i * P:(i + 1) * P]
                            mm = pe.matmul(PS[:, 2 * (u % 2) + l // 4, (l % 4) * P:(l % 4 + 1) * P], k, q,
                                           start=True, stop=True)
                        mm.then_inc(g_sc, 1)

                    def values(u):
                        (_, _, _, src, v0, head), i = units[u]
                        pe.wait_ge(g_w, u + 1)
                        for l in range(LEVELS):
                            pe.matmul(o_cols(head, i), GWT[:, u % 2, l, :], src[:, i, v0:v0 + HD], start=(l == 0),
                                      stop=(i == 0 and l == LEVELS - 1))
                        if i:
                            pe.matmul(o_cols(head, i), CR[:, u // 2, :], src[:, 0, v0:v0 + HD], start=False, stop=True)

                    for u in range(2 * n):
                        if u >= 2:
                            pe.wait_ge(g_w, u - 1)
                        scores(u)
                        if u:
                            values(u - 1)
                    values(2 * n - 1)

                @block.vector
                def _(dve):
                    dve.wait_ge(g_cr, 1)
                    for c in range(n):
                        last = dve.tensor_copy(CR[:, c, :], cross_place(gated, c))
                    last.then_inc(g_crw, 1)
                    for u in range(2 * n):
                        dve.wait_ge(g_sc, u + 1)
                        b = 2 * (u % 2)
                        dve.tensor_tensor(GWT[:, u % 2], PS[:, b:b + 2, :].rearrange("p a (l n) -> p (a l) n", n=P),
                                          level_mask[:], ALU.mult).then_inc(g_w, 1)

        gated = [(h // 2, HD * (h % 2), HD, HG, h * HD, RET_H + h) for h in range(HGRN_H)]
        gated += [(3, GLA_DK * h, GLA_DK, GG, h * HD, RET_H + HGRN_H + h) for h in range(GLA_H)]
        gated_heads(gated[:4], 0)
        with nc.Block() as block:
            @block.gpsimd
            def _(pool):
                level_factors(pool, 2)
        gated_heads(gated[4:], 2)

        hs = sb(inner, "head_sums", [P, 4, TT * HEADS])
        squared, meaned, rooted = sem("h_squared"), sem("h_meaned"), sem("h_rooted")
        O = PS[:, 4:8, :].rearrange("p (i b) n -> p i (b n)", i=TT)
        with nc.Block() as block:
            @block.scalar
            def _(act):
                act.activation(merged[:], O, ACT.Square).then_inc(squared, 1)
                act.wait_ge(meaned, 1)
                act.activation(hs[:, 2, :], hs[:, 1, :], ACT.Sqrt).then_inc(rooted, 1)

            @block.vector
            def _(dve):
                step = stepper(dve, dve_step)
                dve.wait_ge(squared, 1)
                step(dve.tensor_reduce(hs[:, 0, :], merged[:].rearrange("p i (h d) -> p (i h) d", d=HD), AX.X, ALU.add))
                dve.tensor_scalar(hs[:, 1, :], hs[:, 0, :], 1.0 / HD, EPS, ALU.mult, ALU.add).then_inc(meaned, 1)
                dve.wait_ge(rooted, 1)
                step(dve.reciprocal(hs[:, 3, :], hs[:, 2, :]))
                step(dve.tensor_tensor(merged[:].rearrange("p i (h d) -> p (i h) d", d=HD),
                                       PS[:, 4:8, :].rearrange("p b (h d) -> p (b h) d", d=HD),
                                       bc(hs[:, 3, :], 2, HD), ALU.mult))
                for c0, g in ((0, RT[:, :, 3 * RET_W:]), (RET_W, HG[:, :, HGRN_W:]),
                              (RET_W + HGRN_W, GG[:, :, GLA_W:])):
                    part = merged[:, :, c0:c0 + g.shape[2]]
                    dve.tensor_tensor(part, part, g, ALU.mult)
        inner.close()
        MT = sb(scope, "merged_T", [P, KT, S])
        turn_features(merged, MT, 1, mix_gain)
        output_projection("w_out", MT, 1, gate_a)

    clear_phase_sems()
    norm_block(mod[:, 3, :], mod[:, 2, :])

    with ExitStack() as scope:
        CB = sb(scope, "combine", [P, EXPERTS, S])
        route = ExitStack()
        NR = GROUPS + EXPERTS
        wr = sb(route, "w_router", [P, KT, NR])
        br = sb(route, "b_router", [P, NR])
        lg = sb(route, "logits", [P, TT, NR])
        order4 = sb(route, "order4", [P, 16])
        g4 = sb(route, "group_scratch", [P, 4, TT, GROUPS])
        e8 = sb(route, "expert_scratch", [P, 8, TT, PER_GROUP])
        s1 = sb(route, "scalars", [P, 16, TT])
        em = sb(route, "by_group", [P, TT, EXPERTS])
        cT = sb(route, "combine_T", [EXPERTS, S])
        small, lgm, xin, xout, cm, cev, stored, spread = (pool_dma_sem("r_small"), sem("r_logits"), sem("r_expin"),
                                                          sem("r_expout"), sem("r_comb"), sem("r_ct"),
                                                          pool_dma_sem("r_stored"), pool_dma_sem("r_spread"))
        rows_dram = nc.dram_tensor("combine_rows", (EXPERTS, S), F32, kind="Internal").ap()
        with nc.Block() as block:
            @block.gpsimd
            def _(pool):
                with nc.allow_non_contiguous_dma(reason="small router weights"):
                    pool.dma_start(wr[:, :, 0:GROUPS],
                                   t["router_group_w"][0].rearrange("(p k) n -> p k n", k=KT)).then_inc(small, 16)
                    pool.dma_start(wr[:, :, GROUPS:],
                                   t["router_expert_w"][0].rearrange("(p k) n -> p k n", k=KT)).then_inc(small, 16)
                pool.dma_start(br[:, 0:GROUPS], t["router_group_b"][0].partition_broadcast(P)).then_inc(small, 16)
                pool.dma_start(br[:, GROUPS:], t["router_expert_b"][0].partition_broadcast(P)).then_inc(small, 16)
                pool.dma_start(order4[:], t["const_order"]).then_inc(small, 16)
                pool.wait_ge(cev, 1)
                pool.dma_start(rows_dram, cT[:]).then_inc(stored, 16)
                pool.wait_ge(stored, 16)
                pool.dma_start(CB[:], rows_dram.partition_broadcast(P)).then_inc(spread, 16)
                pool.wait_ge(spread, 16)

            @block.tensor
            def _(pe):
                pe.wait_ge(small, 80)
                for i in range(TT):
                    for k in range(KT):
                        mm = pe.matmul(PS[:, i, 0:NR], HT[:, k, i * P:(i + 1) * P], wr[:, k, :],
                                       start=(k == 0), stop=(k == KT - 1))
                mm.then_inc(lgm, 1)
                pe.wait_ge(cm, 1)
                for i in range(TT):
                    mm = pe.transpose(PS[0:EXPERTS, 2, i * P:(i + 1) * P], em[:, i, :], ident[:])
                mm.then_inc(lgm, 1)

            @block.scalar
            def _(act):
                act.wait_ge(xin, 1)
                act.activation(g4[:, 0], g4[:, 0], ACT.Exp).then_inc(xout, 1)
                act.wait_ge(xin, 2)
                act.activation(s1[:, 6, :], s1[:, 6, :], ACT.Exp).then_inc(xout, 1)

            @block.vector
            def _(dve):
                step = stepper(dve, dve_step)
                dve.wait_ge(lgm, 1)
                step(dve.tensor_tensor(lg[:], PS[:, 0:2, 0:NR], bc(br[:], 1, TT), ALU.add))
                gl = lg[:, :, 0:GROUPS]
                step(dve.tensor_reduce(s1[:, 0, :], gl, AX.X, ALU.max))
                dve.tensor_tensor(g4[:, 0], gl, bc(s1[:, 0, :], 2, GROUPS), ALU.subtract).then_inc(xin, 1)

                def first_of_equals(x, top, n, tmp, best, onehot):
                    step(dve.tensor_tensor(tmp, x, bc(top, 2, n), ALU.is_equal))
                    step(dve.tensor_tensor(tmp, tmp, bc(order4[:, 0:n], 1, TT), ALU.mult))
                    step(dve.tensor_reduce(best, tmp, AX.X, ALU.max))
                    step(dve.tensor_tensor(onehot, tmp, bc(best, 2, n), ALU.is_equal))

                first_of_equals(gl, s1[:, 0, :], GROUPS, g4[:, 1], s1[:, 1, :], g4[:, 2])
                dve.wait_ge(xout, 1)
                step(dve.tensor_reduce(s1[:, 2, :], g4[:, 0], AX.X, ALU.add))
                step(dve.reciprocal(s1[:, 3, :], s1[:, 2, :]))
                for i in range(TT):
                    last = dve.tensor_tensor(em[:, i, :].rearrange("p (g e) -> p g e", g=GROUPS),
                                             lg[:, i, GROUPS:].rearrange("p (g e) -> p g e", g=GROUPS),
                                             bc(g4[:, 2, i, :], 2, PER_GROUP), ALU.mult)
                step(last)
                for i in range(TT):
                    last = dve.tensor_reduce(e8[:, 0, i, :], em[:, i, :].rearrange("p (g e) -> p e g", g=GROUPS),
                                             AX.X, ALU.add)
                step(last)
                step(dve.tensor_reduce(s1[:, 4, :], e8[:, 0], AX.X, ALU.max))
                first_of_equals(e8[:, 0], s1[:, 4, :], PER_GROUP, e8[:, 1], s1[:, 1, :], e8[:, 2])
                step(dve.scalar_tensor_tensor(out=e8[:, 3], in0=e8[:, 2], scalar=NEG, in1=e8[:, 0],
                                              op0=ALU.mult, op1=ALU.add))
                step(dve.tensor_reduce(s1[:, 5, :], e8[:, 3], AX.X, ALU.max))
                dve.tensor_tensor(s1[:, 6, :], s1[:, 5, :], s1[:, 4, :], ALU.subtract).then_inc(xin, 1)
                first_of_equals(e8[:, 3], s1[:, 5, :], PER_GROUP, e8[:, 1], s1[:, 1, :], e8[:, 4])
                dve.wait_ge(xout, 2)
                step(dve.tensor_scalar(s1[:, 7, :], s1[:, 6, :], 1.0, None, ALU.add))
                step(dve.reciprocal(s1[:, 8, :], s1[:, 7, :]))
                step(dve.tensor_tensor(s1[:, 9, :], s1[:, 8, :], s1[:, 3, :], ALU.mult))
                step(dve.tensor_tensor(s1[:, 10, :], s1[:, 9, :], s1[:, 6, :], ALU.mult))
                dve.tensor_tensor(e8[:, 5], e8[:, 2], bc(s1[:, 9, :], 2, PER_GROUP), ALU.mult)
                step(dve.tensor_tensor(e8[:, 6], e8[:, 4], bc(s1[:, 10, :], 2, PER_GROUP), ALU.mult))
                step(dve.tensor_tensor(e8[:, 7], e8[:, 5], e8[:, 6], ALU.add))
                for i in range(TT):
                    last = dve.tensor_tensor(em[:, i, :].rearrange("p (g e) -> p g e", g=GROUPS),
                                             bc(g4[:, 2, i, :], 2, PER_GROUP), bc(e8[:, 7, i, :], 1, GROUPS), ALU.mult)
                last.then_inc(cm, 1)
                dve.wait_ge(lgm, 2)
                dve.tensor_copy(cT[:], PS[0:EXPERTS, 2, 0:S]).then_inc(cev, 1)
        route.close()
        experts("moe", moe_source, EXPERTS, lambda e: CB[:, ds(e, 1), :], gate_b)

    plain_norm(t["norm_final"], None)

    clear_phase_sems()

    modulation(t["c_2"], t["ada_w"][0], t["ada_b"][0], t["norm_mix_g"][0], t["norm_ffn_g"][0])
    norm_block(mod[:, 1, :], mod[:, 0, :])

    with ExitStack() as scope:
        att = sb(scope, "att", [P, TT, KV_H * HD])
        y = sb(scope, "y", [P, TT, SSM_IN])
        ssm_gain = sb(scope, "ssm_gain", [P, 2 * KT])
        wide = ExitStack()
        ZV = sb(wide, "z_v", [P, TT, SSM_IN + KV_H * HD])
        XB = sb(wide, "xbc", [P, XT, S + CONV - 1])
        dt = sb(wide, "dt", [P, TT, SSM_H])
        convT = sb(wide, "conv_T", [P, (CONV + 1) * XT])
        rowc = sb(wide, "row_consts", [P, 3, SSM_H])

        inner = ExitStack()
        QT = sb(inner, "att_q", [P, ATT_G * KT, S])
        KTT = sb(inner, "att_k", [P, KT, S])
        wdt = sb(inner, "w_dt", [P, KT, SSM_H])
        rawc = sb(inner, "conv_raw", [P, P])
        table = sb(inner, "rel_table", [BUCKETS, ATT_G * KV_H])
        onehot = sb(inner, "bucket_onehot", [BUCKETS, 384])
        gsel = sb(inner, "group_select", [ATT_G, ATT_G * KV_H])
        gmask = sb(inner, "group_mask", [ATT_G, 384])
        flip = sb(inner, "flip", [P, P])
        bias_rows = sb(inner, "bias_rows", [ATT_G * KV_H, 384])
        bias_dram = nc.dram_tensor("bias_rows_dram", (ATT_G * KV_H, 384), F32, kind="Internal").ap()
        small, made, moved1, stored = pool_dma_sem("a_small"), sem("a_made"), sem("a_moved"), pool_dma_sem("a_stored")
        with nc.Block() as block:
            @block.gpsimd
            def _(pool):
                with nc.allow_non_contiguous_dma(reason="small vectors"):
                    loads = [
                        (wdt[:], hi[:, HY_DT:HY_DT + SSM_H].rearrange("(p k) n -> p k n", k=KT)),
                        (rawc[0:CONV * XT, :], t["hy_conv_w"][0].rearrange("j (m p) -> (j m) p", p=P)),
                        (rawc[CONV * XT:(CONV + 1) * XT, :], t["hy_conv_b"][0].rearrange("(m p) -> m p", p=P)),
                        (table[:], t["rel_table"]), (onehot[:], t["const_onehot"]), (gsel[:], t["const_gsel"]),
                        (gmask[:], t["const_gmask"]), (flip[:], t["const_flip"]),
                        (rowc[:, 0, :], t["hy_dt_bias"][0].partition_broadcast(P)),
                        (rowc[:, 1, :], t["hy_a_log"][0].partition_broadcast(P)),
                        (rowc[:, 2, :], t["hy_d_skip"][0].partition_broadcast(P)),
                        (ssm_gain[:, 0:KT], t["hy_ssm_norm_g"][0][0:D].rearrange("(p k) -> p k", k=KT)),
                        (ssm_gain[:, KT:], t["hy_ssm_norm_g"][0][D:].rearrange("(p k) -> p k", k=KT)),
                    ]
                    for dst, src in loads:
                        pool.dma_start(dst, src).then_inc(small, 16)
                pool.wait_ge(moved1, 1)
                pool.dma_start(bias_dram, bias_rows[:]).then_inc(stored, 16)
                pool.wait_ge(stored, 16)

            @block.tensor
            def _(pe):
                pe.wait_ge(small, 16 * 13)
                n = (CONV + 1) * XT
                pe.matmul(PS[0:ATT_G * KV_H, 1, 0:384], table[:], onehot[:], start=True, stop=False)
                pe.matmul(PS[0:ATT_G * KV_H, 1, 0:384], gsel[:], gmask[:], start=False, stop=True)
                pe.transpose(PS[:, 0, 0:n], rawc[0:n, :], ident[0:n, 0:n]).then_inc(made, 1)
                for i in range(TT):
                    for k in range(KT):
                        mm = pe.matmul(PS[:, 2, i * SSM_H:(i + 1) * SSM_H], HT[:, k, i * P:(i + 1) * P], wdt[:, k, :],
                                       start=(k == 0), stop=(k == KT - 1))
                mm.then_inc(made, 1)

            @block.vector
            def _(dve):
                dve.memset(XB[:, :, 0:CONV - 1], 0.0)
                dve.wait_ge(made, 1)
                dve.tensor_copy(bias_rows[:], PS[0:ATT_G * KV_H, 1, 0:384]).then_inc(moved1, 1)
                dve.tensor_copy(convT[:], PS[:, 0, 0:(CONV + 1) * XT])
                dve.wait_ge(made, 2)
                dve.tensor_tensor(dt[:], PS[:, 2, 0:TT * SSM_H].rearrange("p (i h) -> p i h", i=TT),
                                  bc(rowc[:, 0, :], 1, TT), ALU.add)

        def move_x(act, bank, j):
            return act.activation(XB[:, 2 * j:2 * j + 2, CONV - 1:], bank, ACT.Copy)

        def move_rows(dst):
            return lambda act, bank, j: act.activation(dst[:, 2 * j:2 * j + 2, :], bank, ACT.Copy)

        def move_q(act, bank, j):
            return act.activation(QT[:, 2 * j:2 * j + 2, :].rearrange("p a (i n) -> p (a i) n", n=P),
                                  bank.rearrange("p a (i n) -> p (a i) n", n=P)[:, :, ::-1], ACT.Copy)

        def move_tokens(dst, c0, func=ACT.Copy):
            return lambda act, bank, j: act.activation(dst[:, :, c0 + j * CW:c0 + (j + 1) * CW], bank, func)

        project([("hy_x", 0, 12, "rows", move_x), ("hy_q", 0, 12, "rows", move_q),
                 ("hy_k", 0, 4, "rows", move_rows(KTT)), ("hy_z", 0, 8, "tokens", move_tokens(ZV, 0, ACT.Silu)),
                 ("hy_v", 0, 4, "tokens", move_tokens(ZV, SSM_IN))])

        BT = sb(inner, "bias_tiles", [P, 2, ATT_G, S])
        SC = sb(inner, "att_scores", [P, 2, ATT_G, S])
        PT = sb(inner, "att_probs_T", [P, 2, S])
        nmax = sb(inner, "neg_max", [P, 4])
        zsum = sb(inner, "prob_sums", [P, 4])
        zinv = sb(inner, "prob_inv", [P, 4])
        FL = sb(inner, "flip_scaled", [P, 2, P])
        flipped = sem("a_flipped")
        bias_in = [pool_dma_sem("bias_in0"), pool_dma_sem("bias_in1")]
        scored, biased, maxed, exped, summed, copied, valued, normed = (
            sem("a_scored"), sem("a_biased"), sem("a_maxed"), sem("a_exped"), sem("a_summed"), sem("a_copied"),
            sem("a_valued"), sem("a_normed"))
        U = KV_H * TT
        with nc.Block() as block:
            @block.gpsimd
            def _(pool):
                for h in range(KV_H):
                    if h >= 2:
                        pool.wait_ge(biased, 2 * (h - 1))
                    pool.dma_start(BT[:, h % 2], bass.AP(tensor=bias_dram.tensor, offset=h * 384,
                                                         ap=[[1, P], [KV_H * 384, ATT_G], [1, S]]))\
                        .then_inc(bias_in[h % 2], 16)

            @block.tensor
            def _(pe):
                def score(u):
                    h, i = u // TT, u % TT
                    r0, n = HD * (h % 2), (i + 1) * P
                    for g in range(ATT_G):
                        b = 2 * (u % 2) + g // 2
                        mm = pe.matmul(PS[:, b, (g % 2) * S:(g % 2) * S + n],
                                       QT[r0:r0 + HD, g * KT + h // 2, i * P:(i + 1) * P],
                                       KTT[r0:r0 + HD, h // 2, 0:n], start=True, stop=True)
                    mm.then_inc(scored, 1)

                def add_groups(u):
                    i = u % TT
                    pe.wait_ge(flipped, u + 1)
                    for st in range(i + 1):
                        for g in range(ATT_G):
                            mm = pe.matmul(PS[:, 4 + u % 2, st * P:(st + 1) * P], SC[:, u % 2, g, st * P:(st + 1) * P],
                                           FL[:, u % 2, :], start=(g == 0), stop=(g == ATT_G - 1))
                    mm.then_inc(summed, 1)

                def value(u):
                    h, i = u // TT, u % TT
                    pe.wait_ge(copied, u + 1)
                    if u >= 2:
                        pe.wait_ge(normed, u - 1)
                    for st in range(i + 1):
                        mm = pe.matmul(PS[:, 6 + u % 2, 0:HD], PT[:, u % 2, st * P:(st + 1) * P],
                                       ZV[:, st, SSM_IN + h * HD:SSM_IN + (h + 1) * HD], start=(st == 0), stop=(st == i))
                    mm.then_inc(valued, 1)

                for u in range(U + 2):
                    if u < U:
                        if u >= 2:
                            pe.wait_ge(biased, u - 1)
                        score(u)
                    if 1 <= u <= U:
                        add_groups(u - 1)
                    if u >= 2:
                        value(u - 2)

            @block.vector
            def _(dve):
                step = stepper(dve, dve_step)
                for u in range(U + 2):
                    if u < U:
                        h, i = u // TT, u % TT
                        n = (i + 1) * P
                        dve.wait_ge(bias_in[h % 2], 16 * (h // 2 + 1))
                        dve.wait_ge(scored, u + 1)
                        if u >= 2:
                            dve.wait_ge(summed, u - 1)
                        ps = PS[:, 2 * (u % 2):2 * (u % 2) + 2, :].rearrange("p a (g s) -> p (a g) s", s=S)
                        dve.scalar_tensor_tensor(out=SC[:, u % 2, :, 0:n], in0=ps[:, 0:ATT_G, 0:n], scalar=HD ** -0.5,
                                                 in1=BT[:, h % 2, :, S - n:], op0=ALU.mult, op1=ALU.add)\
                            .then_inc(biased, 1)
                        dve.wait_ge(biased, u + 1)
                        dve.tensor_reduce(nmax[:, u % 4:u % 4 + 1], SC[:, u % 2, :, 0:n], AX.XY, ALU.max, negate=True)\
                            .then_inc(maxed, 1)
                    if 1 <= u <= U:
                        v = u - 1
                        dve.wait_ge(exped, v + 1)
                        step(dve.reciprocal(zinv[:, v % 4:v % 4 + 1], zsum[:, v % 4:v % 4 + 1]))
                        dve.tensor_scalar(FL[:, v % 2, :], flip[:], zinv[:, v % 4:v % 4 + 1], None,
                                          ALU.mult).then_inc(flipped, 1)
                    if u >= 2:
                        v = u - 2
                        h, i = v // TT, v % TT
                        dve.wait_ge(valued, v + 1)
                        dve.tensor_copy(att[:, i, h * HD:(h + 1) * HD], PS[:, 6 + v % 2, 0:HD]).then_inc(normed, 1)

            @block.scalar
            def _(act):
                for u in range(U + 1):
                    if u < U:
                        n = (u % TT + 1) * P
                        act.wait_ge(maxed, u + 1)
                        act.activation(SC[:, u % 2, :, 0:n], SC[:, u % 2, :, 0:n], ACT.Exp,
                                       bias=nmax[:, u % 4:u % 4 + 1], accum_out=zsum[:, u % 4:u % 4 + 1])\
                            .then_inc(exped, 1)
                    if u >= 1:
                        v = u - 1
                        n = (v % TT + 1) * P
                        act.wait_ge(summed, v + 1)
                        act.activation(PT[:, v % 2, 0:n], PS[:, 4 + v % 2, 0:n], ACT.Copy).then_inc(copied, 1)
        inner.close()

        inner = ExitStack()
        xs = sb(inner, "xs", [P, TT, SSM_IN])
        acc = sb(inner, "conv_acc", [P, 4, S])
        la = sb(inner, "dt_a", [P, TT, SSM_H])
        sp8 = sb(inner, "softplus", [P, 8, TT * SSM_H])
        conv, conved, xturned, xmoved = sem("s_conv"), sem("s_conved"), sem("s_turned"), sem("s_moved")
        e_in, e_out, scan_ps = sem("s_ein"), sem("s_eout"), sem("s_scan")
        with nc.Block() as block:
            @block.vector
            def _(dve):
                step = stepper(dve, dve_step)
                dtf = dt[:].rearrange("p i h -> p (i h)")
                step(dve.tensor_scalar(sp8[:, 0, :], dtf, -1.0, None, ALU.mult))
                dve.tensor_tensor(sp8[:, 1, :], sp8[:, 0, :], dtf, ALU.min).then_inc(e_in, 1)
                dve.wait_ge(e_out, 1)
                step(dve.tensor_scalar(sp8[:, 2, :], sp8[:, 1, :], 2.0, None, ALU.add))
                step(dve.reciprocal(sp8[:, 3, :], sp8[:, 2, :]))
                step(dve.tensor_tensor(sp8[:, 4, :], sp8[:, 1, :], sp8[:, 3, :], ALU.mult))
                step(dve.tensor_tensor(sp8[:, 5, :], sp8[:, 4, :], sp8[:, 4, :], ALU.mult))
                step(dve.tensor_scalar(sp8[:, 6, :], sp8[:, 5, :], 1.0 / 17, None, ALU.mult))
                for k in range(7, 0, -1):
                    step(dve.scalar_tensor_tensor(out=sp8[:, 6, :], in0=sp8[:, 6, :], scalar=1.0 / (2 * k + 1),
                                                  in1=sp8[:, 5, :], op0=ALU.add, op1=ALU.mult))
                step(dve.scalar_tensor_tensor(out=sp8[:, 6, :], in0=sp8[:, 6, :], scalar=1.0, in1=sp8[:, 4, :],
                                              op0=ALU.add, op1=ALU.mult))
                step(dve.tensor_scalar(sp8[:, 7, :], dtf, 0.0, None, ALU.max))
                step(dve.scalar_tensor_tensor(out=dtf, in0=sp8[:, 6, :], scalar=2.0, in1=sp8[:, 7, :],
                                              op0=ALU.mult, op1=ALU.add))
                dve.wait_ge(e_out, 2)
                step(dve.scalar_tensor_tensor(out=la[:], in0=dt[:], scalar=-1.0, in1=bc(rowc[:, 1, :], 1, TT),
                                              op0=ALU.mult, op1=ALU.mult))
                for m in range(XT):
                    a = acc[:, m % 4, :]
                    if m >= 4:
                        dve.wait_ge(conved, m - 3)
                    for j in range(CONV):
                        w = convT[:, j * XT + m:j * XT + m + 1]
                        if j == 0:
                            ins = dve.tensor_scalar(a, XB[:, m, 0:S], w, convT[:, CONV * XT + m:CONV * XT + m + 1],
                                                    ALU.mult, ALU.add)
                        else:
                            ins = dve.scalar_tensor_tensor(out=a, in0=XB[:, m, j:j + S], scalar=w, in1=a,
                                                           op0=ALU.mult, op1=ALU.add)
                        if j < CONV - 1:
                            step(ins)
                        else:
                            ins.then_inc(conv, 1)

            @block.scalar
            def _(act):
                act.wait_ge(e_in, 1)
                act.activation(sp8[:, 1, :], sp8[:, 1, :], ACT.Exp).then_inc(e_out, 1)
                act.activation(rowc[:, 1, :], rowc[:, 1, :], ACT.Exp).then_inc(e_out, 1)
                for m in range(XT):
                    act.wait_ge(conv, m + 1)
                    act.activation(XB[:, m, CONV - 1:], acc[:, m % 4, :], ACT.Silu).then_inc(conved, 1)
                    if m >= 1 and m - 1 < SSM_IN // P:
                        n = m - 1
                        act.wait_ge(xturned, n + 1)
                        act.activation(xs[:, :, n * P:(n + 1) * P],
                                       PS[:, n % 4, 0:S].rearrange("p (i n) -> p i n", i=TT), ACT.Copy)\
                            .then_inc(xmoved, 1)

            @block.tensor
            def _(pe):
                for m in range(SSM_IN // P):
                    pe.wait_ge(conved, m + 1)
                    if m >= 4:
                        pe.wait_ge(xmoved, m - 3)
                    for i in range(TT):
                        mm = pe.transpose(PS[:, m % 4, i * P:(i + 1) * P],
                                          XB[:, m, CONV - 1 + i * P:CONV - 1 + (i + 1) * P], ident[:])
                    mm.then_inc(xturned, 1)

        xdt = sb(inner, "xdt", [P, TT, SSM_IN])
        cbm = sb(inner, "cb_masked", [P, SSM_G, 384])
        cums = sb(inner, "cums", [P, TT, SSM_H])
        dd = sb(inner, "decays", [P, 2, 384])
        W = sb(inner, "ssm_weights", [P, 2, 384])
        cb_ps, cb_mv, cum_ps, bcast, diffed, exped, weighted, vdone, xready, ymoved, yinit = (
            sem("s_cb"), sem("s_cbm"), sem("s_cum"), sem("s_bcast"), sem("s_diff"), sem("s_exp"), sem("s_weight"),
            sem("s_value"), sem("s_xready"), sem("s_ymoved"), sem("s_yinit"))
        GH = SSM_H // SSM_G

        def move_y(dve, g):
            dve.wait_ge(vdone, (g + 1) * GH)
            dve.wait_ge(yinit, TT)
            c = slice(g * GH * HD, (g + 1) * GH * HD)
            b = 4 + 2 * (g % 2)
            dve.tensor_tensor(y[:, :, c], y[:, :, c], PS[:, b:b + 2, :], ALU.add).then_inc(ymoved, 1)

        with nc.Block() as block:
            @block.tensor
            def _(pe):
                pe.matmul(PS[:, 2, 0:SSM_H], pairs[:, 0:P], la[:, 0, :], start=True, stop=True)
                pe.matmul(PS[:, 2, SSM_H:2 * SSM_H], ones[:], la[:, 0, :], start=True, stop=False)
                pe.matmul(PS[:, 2, SSM_H:2 * SSM_H], pairs[:, 0:P], la[:, 1, :], start=False, stop=True)\
                    .then_inc(cum_ps, 1)
                for g in range(SSM_G):
                    B = XB[:, SSM_IN // P + g, CONV - 1:]
                    C = XB[:, SSM_IN // P + SSM_G + g, CONV - 1:]
                    if g >= 2:
                        pe.wait_ge(cb_mv, g - 1)
                    pe.matmul(PS[:, g % 2, 0:S], B[:, 0:P], C, start=True, stop=True)
                    pe.matmul(PS[:, g % 2, S:384], B[:, P:S], C[:, P:S], start=True, stop=True).then_inc(cb_ps, 1)
                pe.wait_ge(cb_mv, SSM_G)
                pe.wait_ge(xready, 1)

                def spread(h):
                    if h >= 2:
                        pe.wait_ge(diffed, h - 1)
                    pe.matmul(PS[:, h % 2, 0:S], la[:, 0, h:h + 1].broadcast_to([P, P]), pairs[:, 0:S],
                              start=True, stop=False)
                    pe.matmul(PS[:, h % 2, P:S], la[:, 1, h:h + 1].broadcast_to([P, P]), pairs[:, 0:P],
                              start=False, stop=True).then_inc(bcast, 1)

                def values(h):
                    g = h // GH
                    if g >= 2 and h % GH == 0:
                        pe.wait_ge(ymoved, g - 1)
                    pe.wait_ge(weighted, h + 1)
                    w = W[:, h % 2, :]
                    c = (h % GH) * HD
                    x = xdt[:, :, h * HD:(h + 1) * HD]
                    o = [PS[:, 4 + 2 * (g % 2) + i, c:c + HD] for i in range(TT)]
                    pe.matmul(o[0], w[:, 0:P], x[:, 0, :], start=True, stop=True)
                    pe.matmul(o[1], w[:, P:2 * P], x[:, 0, :], start=True, stop=False)
                    pe.matmul(o[1], w[:, 2 * P:3 * P], x[:, 1, :], start=False, stop=True).then_inc(vdone, 1)

                for h in range(SSM_H + 1):
                    if h < SSM_H:
                        spread(h)
                    if h >= 1:
                        values(h - 1)

            @block.vector
            def _(dve):
                dve.wait_ge(cum_ps, 1)
                dve.tensor_copy(cums[:], PS[:, 2, 0:2 * SSM_H].rearrange("p (i h) -> p i h", i=TT))
                for g in range(SSM_G):
                    dve.wait_ge(cb_ps, g + 1)
                    dve.tensor_tensor(cbm[:, g, :], PS[:, g % 2, 0:384], pairs[:], ALU.mult).then_inc(cb_mv, 1)
                dve.wait_ge(cb_mv, SSM_G)
                v4 = lambda ap: ap.rearrange("p i (h d) -> p (i h) d", d=HD)
                dve.tensor_tensor(v4(xdt[:]), v4(xs[:]), bc(dt[:].rearrange("p i h -> p (i h)"), 2, HD),
                                  ALU.mult).then_inc(xready, 1)
                for h in range(SSM_H):
                    dve.wait_ge(bcast, h + 1)
                    if h >= 2:
                        dve.wait_ge(weighted, h - 1)
                    dve.tensor_scalar(dd[:, h % 2, 0:S], PS[:, h % 2, 0:S], cums[:, 0, h:h + 1], 0.0,
                                      ALU.subtract, ALU.min)
                    dve.tensor_scalar(dd[:, h % 2, S:384], PS[:, h % 2, P:S], cums[:, 1, h:h + 1], 0.0,
                                      ALU.subtract, ALU.min).then_inc(diffed, 1)
                    if h % GH == 1 and h > GH:
                        move_y(dve, h // GH - 1)
                move_y(dve, SSM_G - 1)

            @block.scalar
            def _(act):
                for h in range(SSM_H):
                    act.wait_ge(diffed, h + 1)
                    act.activation(dd[:, h % 2, :], dd[:, h % 2, :], ACT.Exp).then_inc(exped, 1)

            @block.gpsimd
            def _(pool):
                for i in range(TT):
                    pool.tensor_tensor(y[:, i, :].rearrange("p (h d) -> p h d", d=HD),
                                       xs[:, i, :].rearrange("p (h d) -> p h d", d=HD),
                                       bc(rowc[:, 2, :], 2, HD), ALU.mult).then_inc(yinit, 1)
                for h in range(SSM_H):
                    pool.wait_ge(exped, h + 1)
                    if h >= 2:
                        pool.wait_ge(vdone, h - 1)
                    pool.tensor_tensor(W[:, h % 2, :], dd[:, h % 2, :], cbm[:, h // GH, :], ALU.mult)\
                        .then_inc(weighted, 1)

        squared, meaned, rooted = sem("y_squared"), sem("y_meaned"), sem("y_rooted")
        gated_y = sem("y_gated")
        with nc.Block() as block:
            @block.vector
            def _(dve):
                step = stepper(dve, dve_step)
                for i in range(TT):
                    dve.tensor_tensor(y[:, i, :], y[:, i, :], ZV[:, i, 0:SSM_IN], ALU.mult).then_inc(gated_y, 1)
                dve.wait_ge(squared, TT)
                dve.tensor_scalar(stat[:, 2:4], stat[:, 0:2], 1.0 / SSM_IN, EPS, ALU.mult, ALU.add).then_inc(meaned, 1)
                dve.wait_ge(rooted, 1)
                step(dve.reciprocal(stat[:, 6:8], stat[:, 4:6]))
                for i in range(TT):
                    dve.tensor_scalar(y[:, i, :], y[:, i, :], stat[:, 6 + i:7 + i], None, ALU.mult)

            @block.scalar
            def _(act):
                for i in range(TT):
                    act.wait_ge(gated_y, i + 1)
                    act.activation(xs[:, i, :], y[:, i, :], ACT.Square, accum_out=stat[:, i:i + 1]).then_inc(squared, 1)
                act.wait_ge(meaned, 1)
                act.activation(stat[:, 4:6], stat[:, 2:4], ACT.Sqrt).then_inc(rooted, 1)
        inner.close()
        wide.close()
        YT = sb(scope, "y_T", [P, 3 * KT, S])
        turn_features(y, YT[:, 0:2 * KT, :], 2, ssm_gain)
        turn_features(att, YT[:, 2 * KT:, :], 1, None)
        output_projection("hy_out", YT, 3, gate_a)

    norm_block(mod[:, 3, :], mod[:, 2, :])
    experts("ffn0", ffn_source(0), FFN_CHUNKS, None, gate_b)

    clear_phase_sems()

    modulation(t["c_2"], t["ada_w"][1], t["ada_b"][1], t["norm_mix_g"][1], t["norm_ffn_g"][1])
    norm_block(mod[:, 1, :], mod[:, 0, :])

    with ExitStack() as scope:
        U0 = TAPS - 1
        UP = sb(scope, "conv_in", [P, KT, S + U0])
        CA = sb(scope, "conv_out", [P, KT, S])
        SG = sb(scope, "conv_gate", [P, KT, S])
        SQ = sb(scope, "conv_sq", [P, KT, S])
        raw = sb(scope, "vec_raw", [P, 3, P])
        vec = sb(scope, "vec_T", [P, 3, P])
        b2 = sb(scope, "pw2_bias", [1, D])
        rstd = sb(scope, "ln_rstd", [P, 3, S])
        meanw = sb(scope, "mean_weights", [P, P])
        small, made, taken = pool_dma_sem("c_small"), sem("c_made"), sem("c_taken")
        HALF = TAPS * KT // 2
        with nc.Block() as block:
            @block.gpsimd
            def _(pool):
                taps = t["cv_w_dw"][0].rearrange("j (m p) -> (j m) p", p=P)
                loads = [(raw[0:HALF, 0, :], taps[0:HALF, :]), (raw[0:HALF, 1, :], taps[HALF:, :]),
                         (raw[0:16, 2, :], t["cv_b_pw1"][0].rearrange("(m p) -> m p", p=P)),
                         (raw[16:24, 2, :], t["cv_b_dw"][0].rearrange("(m p) -> m p", p=P)),
                         (raw[24:32, 2, :], t["cv_ln_g"][0].rearrange("(m p) -> m p", p=P)),
                         (raw[32:40, 2, :], t["cv_ln_b"][0].rearrange("(m p) -> m p", p=P)),
                         (b2[:], t["cv_b_pw2"][0].rearrange("(a n) -> a n", a=1))]
                for dst, src in loads:
                    pool.dma_start(dst, src).then_inc(small, 16)
                pool.wait_ge(small, 16 * len(loads))

            @block.tensor
            def _(pe):
                pe.wait_ge(small, 16 * 7)
                for j, n in enumerate((HALF, HALF, 40)):
                    mm = pe.transpose(PS[:, j, 0:n], raw[0:n, j, :], ident[0:n, 0:n])
                mm.then_inc(made, 1)

            @block.vector
            def _(dve):
                dve.memset(UP[:, :, 0:U0], 0.0)
                dve.memset(meanw[:], 1.0 / D)
                dve.wait_ge(made, 1)
                for j, n in enumerate((HALF, HALF, 40)):
                    dve.tensor_copy(vec[:, j, 0:n], PS[:, j, 0:n])

        vb = vec[:, 2, :]
        base = segs["pw1"].base
        moved, glu = sem("g_moved"), sem("g_glu")
        with nc.Block() as block:
            @block.sync
            def _(sp):
                send_until(sp, base + 8)

            @block.tensor
            def _(pe):
                for q in range(8):
                    arrive(pe, base + q)
                    if q >= 4:
                        pe.wait_ge(moved, 2 * (q - 3))
                    rows_chunk(pe, base + q, q % 4).then_inc(used, 1)

            @block.scalar
            def _(act):
                for q in range(8):
                    act.wait_ge(used, base + q + 1)
                    c, half = q // 2, q % 2
                    for m in range(2):
                        f = 2 * c + m
                        bank = PS[:, q % 4, m * S:(m + 1) * S]
                        if half:
                            act.activation(SG[:, f, :], bank, ACT.Sigmoid, bias=vb[:, 8 + f:9 + f]).then_inc(moved, 1)
                        else:
                            act.activation(CA[:, f, :], bank, ACT.Identity, bias=vb[:, f:f + 1]).then_inc(moved, 1)

            @block.vector
            def _(dve):
                for c in range(4):
                    dve.wait_ge(moved, 4 * (c + 1))
                    f = slice(2 * c, 2 * c + 2)
                    dve.tensor_tensor(UP[:, f, U0:], CA[:, f, :], SG[:, f, :], ALU.mult)

        tap, means, centred, sqd, vars_, rooted, rs = (sem("d_tap"), sem("d_mean"), sem("d_centred"), sem("d_sq"),
                                                       sem("d_var"), sem("d_rooted"), sem("d_rs"))
        var_ready = sem("d_vready")
        with nc.Block() as block:
            @block.vector
            def _(dve):
                step = stepper(dve, dve_step)
                for j in range(TAPS):
                    for m in range(KT):
                        c = j * KT + m
                        w = vec[:, c // HALF, c % HALF:c % HALF + 1]
                        if j == 0:
                            ins = dve.tensor_scalar(CA[:, m, :], UP[:, m, 0:S], w, vb[:, 16 + m:17 + m], ALU.mult, ALU.add)
                        else:
                            dve.wait_ge(tap, c - KT + 1)
                            ins = dve.scalar_tensor_tensor(out=CA[:, m, :], in0=UP[:, m, j:j + S], scalar=w,
                                                           in1=CA[:, m, :], op0=ALU.mult, op1=ALU.add)
                        ins.then_inc(tap, 1)
                dve.wait_ge(means, 1)
                dve.tensor_tensor(CA[:], CA[:], bc(PS[:, 0, 0:S], 1, KT), ALU.subtract).then_inc(centred, 1)
                dve.wait_ge(vars_, 1)
                dve.tensor_scalar(rstd[:, 0, :], PS[:, 1, 0:S], EPS, None, ALU.add).then_inc(var_ready, 1)
                dve.wait_ge(rooted, 1)
                step(dve.reciprocal(rstd[:, 2, :], rstd[:, 1, :]))
                dve.tensor_tensor(CA[:], CA[:], bc(rstd[:, 2, :], 1, KT), ALU.mult).then_inc(rs, 1)

            @block.tensor
            def _(pe):
                pe.wait_ge(tap, TAPS * KT)
                for m in range(KT):
                    mm = pe.matmul(PS[:, 0, 0:S], meanw[:], CA[:, m, :], start=(m == 0), stop=(m == KT - 1))
                mm.then_inc(means, 1)
                pe.wait_ge(sqd, 1)
                for m in range(KT):
                    mm = pe.matmul(PS[:, 1, 0:S], meanw[:], SQ[:, m, :], start=(m == 0), stop=(m == KT - 1))
                mm.then_inc(vars_, 1)

            @block.scalar
            def _(act):
                act.wait_ge(centred, 1)
                act.activation(SQ[:], CA[:], ACT.Square).then_inc(sqd, 1)
                act.wait_ge(var_ready, 1)
                act.activation(rstd[:, 1, :], rstd[:, 0, :], ACT.Sqrt).then_inc(rooted, 1)
                act.wait_ge(rs, 1)
                for m in range(KT):
                    act.activation(SQ[:, m, :], CA[:, m, :], ACT.Silu, scale=vb[:, 24 + m:25 + m],
                                   bias=vb[:, 32 + m:33 + m])
        output_projection("pw2", SQ, 1, gate_a, bias=b2)

    norm_block(mod[:, 3, :], mod[:, 2, :])
    experts("ffn1", ffn_source(1), FFN_CHUNKS, None, gate_b)

    plain_norm(t["final_norm_g"], out)


def _constants(np):
    p = np.arange(P)
    tri = (p[:, None] <= p[None, :]).astype(np.float32)
    pairs = np.concatenate([tri, np.ones((P, P), np.float32), tri], axis=1)
    levels = np.zeros((P, LEVELS, P), np.float32)
    levels[:, 0, :] = np.eye(P)
    for l in range(1, LEVELS):
        b = 1 << (l - 1)
        block, half = p // (2 * b), (p // b) % 2
        levels[:, l, :] = ((block[:, None] == block[None, :]) & (half[:, None] == 0) & (half[None, :] == 1))
    log_gamma = np.log1p(-np.exp2(-5.0 - np.arange(RET_H)))
    rel = np.concatenate([np.arange(S)[None, :] - p[:, None], p[None, :] - p[:, None]], axis=1)
    decay = np.where(rel[:, None, :] >= 0, np.exp(log_gamma[None, :, None] * np.maximum(rel, 0)[:, None, :]), 0.0)
    freq = np.float32(10000.0) ** (-np.arange(0, HD, 2, dtype=np.float32) / np.float32(HD))
    dist = 255 - np.arange(384)
    exact = BUCKETS // 2
    n = np.maximum(dist, 1).astype(np.float64)
    large = np.minimum((exact + np.log(n / exact) / np.log(2048 / exact) * (BUCKETS - exact)).astype(np.int64), BUCKETS - 1)
    bucket = np.where(dist < exact, np.maximum(dist, 0), large)
    onehot = (np.arange(BUCKETS)[:, None] == bucket[None, :]).astype(np.float32)
    gmask = np.stack([np.where((dist >= 0) & (dist % dil == 0) & (dist <= w), 0.0, NEG)
                      for w, dil in ((128, 1), (512, 4), (2048, 16))])
    gsel = np.repeat(np.eye(ATT_G), KV_H, axis=1)
    order = np.tile(16.0 - np.arange(16), (P, 1))
    out = {"ident": np.eye(P), "pairs": pairs, "levels": levels, "decay": decay, "freq": np.tile(freq, (P, 1)),
           "onehot": onehot, "gmask": gmask, "gsel": gsel, "order": order, "flip": np.eye(P)[::-1]}
    return {f"const_{k}": np.ascontiguousarray(v, dtype=np.float32) for k, v in out.items()}


_FIRST = ["x", "c", "positions", "w_ada", "b_ada", "norm_mix", "norm_ffn", "w_in", "ret_norm", "hgrn_norm",
          "hgrn_lb_logits", "gla_wa2", "gla_ba", "gla_norm", "w_out", "router_group_w", "router_group_b",
          "router_expert_w", "router_expert_b", "expert_w_gate", "expert_w_up", "expert_w_down",
          "norm_final"]
_SECOND = ["c_2", "ada_w_2", "ada_b_2", "norm_mix_g_2", "norm_ffn_g_2", "hy_w_in_2", "hy_conv_w_2", "hy_conv_b_2",
           "hy_dt_bias_2", "hy_a_log_2", "hy_d_skip_2", "hy_ssm_norm_g_2", "hy_w_out_2", "rel_table_2", "cv_w_pw1_2",
           "cv_b_pw1_2", "cv_w_dw_2", "cv_b_dw_2", "cv_ln_g_2", "cv_ln_b_2", "cv_w_pw2_2", "cv_b_pw2_2",
           "ffn_w_gate_2", "ffn_w_up_2", "ffn_w_down_2", "final_norm_g_2"]


def kernel(**inputs):
    import numpy as np
    import concourse.bacc as bacc
    from concourse.bass_utils import run_bass_kernel_spmd

    nc = bacc.Bacc("TRN2", target_bir_lowering=False, num_devices=1)
    arrays, t = {}, {}
    sources = {n: inputs[n] for n in _FIRST + _SECOND}
    sources.update(_constants(np))
    for name, value in sources.items():
        a = np.ascontiguousarray(value)
        arrays[f"in_{name}"] = a
        ap = nc.dram_tensor(f"in_{name}", a.shape, mybir.dt.from_np(a.dtype), kind="ExternalInput").ap()
        t[name if name == "c_2" or not name.endswith("_2") else name[:-2]] = ap
    out = nc.dram_tensor("out", (1, S, D), F32, kind="ExternalOutput").ap()
    build(nc, t, out)
    r = run_bass_kernel_spmd(nc, [arrays], core_ids=[0])
    return r.results[0]["out"]
```

```python
from contextlib import ExitStack

import concourse.bass as bass
from concourse import mybir

F32 = mybir.dt.float32
I32 = mybir.dt.int32
ALU = mybir.AluOpType
ACT = mybir.ActivationFunctionType
AX = mybir.AxisListType
ds = bass.ds

P = 128
D = 1024
S = 256
TT = S // P
KT = D // P
HD = 64
CW = 256
RING = 6
EPS = 1e-6
F_MIN = 1e-30

RET_W, HGRN_W, GLA_W = 384, 384, 256
RET_H, HGRN_H, GLA_H, GLA_DK = 6, 6, 4, 32
HEADS = RET_H + HGRN_H + GLA_H
TAU = 16.0
RANK = 16
GROUPS, PER_GROUP, EXPERTS, SLOTS = 4, 8, 32, 32
LEVELS = 8

SSM_IN, SSM_H, SSM_G, STATE, CONV = 2048, 32, 4, 128, 4
XBC = SSM_IN + 2 * SSM_G * STATE
XT = XBC // P
ATT_G, KV_H, BUCKETS = 3, 16, 32
TAPS = 31
FFN_CHUNKS = 2816 // CW
NEG = -1e30


class Marks:

    def __init__(self, sem):
        self.sem, self.n = sem, 0


def build(nc, t, out):
    top = ExitStack()
    with top:
        _program(nc, t, out, top)


def _program(nc, t, out, top):
    serial = [0]

    phase_sems = []

    def lasting_sem(name):
        return top.enter_context(nc.semaphore(name))

    def pool_dma_sem(name):
        serial[0] += 1
        return top.enter_context(nc.semaphore(f"{name}_{serial[0]}"))

    def sem(name):
        serial[0] += 1
        scope = ExitStack()
        s = scope.enter_context(nc.semaphore(f"{name}_{serial[0]}"))
        phase_sems.append((scope, s))
        return s

    def clear_phase_sems():
        with nc.Block() as block:
            @block.gpsimd
            def _(pool):
                for _, s in phase_sems:
                    pool.sem_clear(s)
        for scope, _ in reversed(phase_sems):
            scope.close()
        phase_sems.clear()

    def sb(scope, name, shape, dt=F32):
        serial[0] += 1
        return scope.enter_context(nc.sbuf_tensor(f"{name}_{serial[0]}", shape, dt))

    def bc(ap, axis, n):
        v = ap.unsqueeze(axis)
        shape = list(v.shape)
        shape[axis] = n
        return v.broadcast_to(shape)

    ring = sb(top, "ring", [P, RING, 8 * CW])
    X = sb(top, "X", [P, TT, D])
    HT = sb(top, "HT", [P, KT, S])
    ident = sb(top, "ident", [P, P])
    ones = sb(top, "ones", [P, P])
    pairs = sb(top, "pairs", [P, 384])
    mod = sb(top, "mod", [P, 4, KT])
    gate_a = sb(top, "gate_a", [P, D])
    gate_b = sb(top, "gate_b", [P, D])
    stat = sb(top, "stat", [P, 16])
    PS = top.enter_context(nc.psum_tensor("PS", [P, 8, 512], F32))

    landed = [lasting_sem(f"landed{i}") for i in range(RING)]
    used = lasting_sem("used")
    dve_step = Marks(lasting_sem("dve_step"))
    act_step = Marks(lasting_sem("act_step"))
    pool_step = Marks(lasting_sem("pool_step"))

    def stepper(eng, marks):
        def step(ins):
            marks.n += 1
            ins.then_inc(marks.sem, 1)
            eng.wait_ge(marks.sem, marks.n)
        return step

    def pk(w, c0):
        return w.rearrange("(p k) n -> p k n", k=KT)[:, :, ds(c0, CW)]

    def kp(w, c0):
        return w.rearrange("(k p) n -> p k n", p=P)[:, :, ds(c0, CW)]

    hy_groups = [t["hy_w_in"][0]]
    wi, hi = t["w_in"][0], hy_groups[0]
    HY_Z, HY_X, HY_DT, HY_Q = 0, SSM_IN, SSM_IN + XBC, SSM_IN + XBC + SSM_H
    HY_K = HY_Q + ATT_G * KV_H * HD
    HY_V = HY_K + KV_H * HD

    class Segment:
        def __init__(self, name, base, n):
            self.name, self.base, self.n = name, base, n

    stream = []
    segs = {}

    def segment(name, sources):
        segs[name] = Segment(name, len(stream), len(sources))
        stream.extend(sources)

    def expert_order(n):
        order = [("g", 0), ("u", 0)]
        for e in range(1, n):
            order += [("g", e), ("u", e), ("d", e - 1)]
        return order + [("d", n - 1)]

    QUAD = 4
    QUADS = EXPERTS // QUAD
    QUAD_ORDER = [("g", 0), ("u", 0), ("g", 1), ("u", 1), ("d", 0), ("g", 2), ("u", 2), ("d", 1),
                  ("g", 3), ("u", 3), ("d", 2), ("d", 3)]
    QC = len(QUAD_ORDER)

    def moe_source(kind, e):
        if kind == "d":
            return t["expert_w_down"][0][ds(e, 1)].rearrange("a (f p) n -> p (a f) n", p=P)
        w = t["expert_w_gate" if kind == "g" else "expert_w_up"][0]
        return w[ds(e, 1)].rearrange("a (p k) n -> p (a k) n", k=KT)

    def ffn_source(layer):
        def source(kind, e):
            if kind == "d":
                return t["ffn_w_down"][layer][ds(e * CW, CW), :].rearrange("(f p) n -> p f n", p=P)
            return pk(t["ffn_w_gate" if kind == "g" else "ffn_w_up"][layer], e * CW)
        return source

    segment("w_in", [pk(wi, c * CW) for c in range(15)])
    segment("w_out", [pk(t["w_out"][0], c * CW) for c in range(4)])
    segment("moe", [moe_source(k, QUAD * q + e) for q in range(QUADS) for k, e in QUAD_ORDER])
    segment("hy_x", [pk(hi, HY_X + c * CW) for c in range(12)])
    segment("hy_q", [pk(hi, HY_Q + c * CW) for c in range(12)])
    segment("hy_k", [pk(hi, HY_K + c * CW) for c in range(4)])
    segment("hy_z", [pk(hi, HY_Z + c * CW) for c in range(8)])
    segment("hy_v", [pk(hi, HY_V + c * CW) for c in range(4)])
    hy_out = t["hy_w_out"][0]
    segment("hy_out", [hy_out[g * D:(g + 1) * D, :].rearrange("(p k) n -> p k n", k=KT)[:, :, c * CW:(c + 1) * CW]
                       for c in range(4) for g in range(3)])
    segment("ffn0", [ffn_source(0)(k, e) for k, e in expert_order(FFN_CHUNKS)])
    segment("pw1", [pk(t["cv_w_pw1"][0], h * D + c * CW) for c in range(4) for h in range(2)])
    segment("pw2", [kp(t["cv_w_pw2"][0], c * CW) for c in range(4)])
    segment("ffn1", [ffn_source(1)(k, e) for k, e in expert_order(FFN_CHUNKS)])

    sent = [0]

    def send(sp, source, n):
        if n >= RING:
            sp.wait_ge(used, n - RING + 1)
        shape = source.shape
        dst = ring[:, n % RING, :].rearrange("p (a b) -> p a b", b=shape[2])
        sp.dma_start(dst, source).then_inc(landed[n % RING], 16)

    def send_until(sp, end):
        stop = min(end + RING, len(stream))
        while sent[0] < stop:
            send(sp, stream[sent[0]], sent[0])
            sent[0] += 1

    def arrive(pe, n, landed=landed):
        pe.wait_ge(landed[n % RING], 16 * (n // RING + 1))

    def w_slot(n, b=CW, ring=ring):
        return ring[:, n % RING, :].rearrange("p (a b) -> p a b", b=b)

    tok = lambda ap: ap.rearrange("(t p) n -> p t n", p=P)

    load0 = sem("load0")
    with nc.Block() as block:
        @block.sync
        def _(sp):
            sp.dma_start(X[:], tok(t["x"][0])).then_inc(load0, 16)
            sp.dma_start(ident[:], t["const_ident"]).then_inc(load0, 16)
            sp.dma_start(pairs[:], t["const_pairs"]).then_inc(load0, 16)
            send_until(sp, 0)
            sp.wait_ge(load0, 48)

        @block.vector
        def _(dve):
            dve.memset(ones[:], 1.0)

    def modulation(c_in, w, b, gain_mix, gain_ffn):
        NB, W = 6, 2048
        n_chunks = KT * (6 * D // W)
        with ExitStack() as scope:
            stage = sb(scope, "ada_stage", [P, NB, W])
            acc = sb(scope, "ada_acc", [P, 6 * D])
            cv = sb(scope, "ada_c", [P, KT])
            bias = sb(scope, "ada_b", [P, 6, KT])
            gains = sb(scope, "ada_gain", [P, 2, KT])
            small, zeroed, brow = sem("ada_small"), sem("ada_zeroed"), sem("ada_brow")
            arrived = [sem(f"ada_arrived{i}") for i in range(NB)]
            c_ready, summed, cols, rows, taken = (sem("ada_c_ready"), sem("ada_summed"), sem("ada_cols"),
                                                  sem("ada_rows"), sem("ada_taken"))
            wv = w.rearrange("(p k) (g n) -> p k g n", k=KT, n=W)
            with nc.Block() as block:
                @block.sync
                def _(sp):
                    sp.dma_start(cv[:], c_in[0].rearrange("(p k) -> p k", k=KT)).then_inc(small, 16)
                    sp.dma_start(bias[:], b.rearrange("(s p k) -> p s k", p=P, k=KT)).then_inc(small, 16)
                    sp.dma_start(gains[:, 0, :], gain_mix.rearrange("(p k) -> p k", k=KT)).then_inc(small, 16)
                    sp.dma_start(gains[:, 1, :], gain_ffn.rearrange("(p k) -> p k", k=KT)).then_inc(small, 16)
                    sp.wait_ge(zeroed, 1)
                    sp.dma_start(acc[0:1, :], b.rearrange("(a n) -> a n", a=1)).then_inc(brow, 16)
                    for n in range(n_chunks):
                        if n >= NB:
                            sp.wait_ge(summed, n - NB + 1)
                        sp.dma_start(stage[:, n % NB, :], wv[:, n % KT, n // KT, :]).then_inc(arrived[n % NB], 16)

                @block.gpsimd
                def _(pool):
                    pool.memset(acc[:], 0.0).then_inc(zeroed, 1)

                @block.scalar
                def _(act):
                    act.wait_ge(small, 64)
                    act.activation(cv[:], cv[:], ACT.Silu).then_inc(c_ready, 1)

                @block.vector
                def _(dve):
                    step = stepper(dve, dve_step)
                    dve.wait_ge(c_ready, 1)
                    dve.wait_ge(brow, 16)
                    for n in range(n_chunks):
                        dve.wait_ge(arrived[n % NB], 16 * (n // NB + 1))
                        if n % KT:
                            dve.wait_ge(summed, n)
                        a = acc[:, (n // KT) * W:(n // KT + 1) * W]
                        dve.scalar_tensor_tensor(out=a, in0=stage[:, n % NB, :], scalar=cv[:, n % KT:n % KT + 1],
                                                 in1=a, op0=ALU.mult, op1=ALU.add).then_inc(summed, 1)
                    dve.wait_ge(cols, 1)
                    cp = PS[:, 0, 0:4 * KT].rearrange("p (s k) -> p s k", k=KT)
                    for j in range(2):
                        dve.tensor_copy(mod[:, 2 * j, :], cp[:, 2 * j, :])
                        dve.scalar_tensor_tensor(out=mod[:, 2 * j + 1, :], in0=cp[:, 2 * j + 1, :], scalar=1.0,
                                                 in1=gains[:, j, :], op0=ALU.add, op1=ALU.mult)
                    dve.wait_ge(rows, 1)
                    dve.tensor_copy(gate_a[:], PS[:, 1:3, :])
                    dve.tensor_copy(gate_b[:], PS[:, 3:5, :])

                @block.tensor
                def _(pe):
                    pe.wait_ge(summed, n_chunks)
                    for s, seg in enumerate((0, 1, 3, 4)):
                        v = acc[:, seg * D:(seg + 1) * D].rearrange("p (m k) -> p k m", k=KT)
                        for k in range(KT):
                            mm = pe.matmul(PS[:, 0, s * KT + k:s * KT + k + 1], v[:, k, :], ones[:, 0:1],
                                           start=True, stop=True)
                    mm.then_inc(cols, 1)
                    for j, seg in enumerate((2, 5)):
                        for h in range(2):
                            mm = pe.matmul(PS[:, 1 + 2 * j + h, :], ones[:],
                                           acc[:, seg * D + h * 512:seg * D + (h + 1) * 512], start=True, stop=True)
                    mm.then_inc(rows, 1)

    def norm_block(scale, shift, xn=None):
        squared, meaned, rooted, scaled, turned, evacuated = (sem("n_squared"), sem("n_meaned"), sem("n_rooted"),
                                                              sem("n_scaled"), sem("n_turned"), sem("n_evac"))
        with ExitStack() as scope:
            xn = sb(scope, "xn", [P, TT, D]) if xn is None else xn
            with nc.Block() as block:
                @block.scalar
                def _(act):
                    for i in range(TT):
                        act.activation(xn[:, i, :], X[:, i, :], ACT.Square,
                                       accum_out=stat[:, i:i + 1]).then_inc(squared, 1)
                    act.wait_ge(meaned, 1)
                    act.activation(stat[:, 4:6], stat[:, 2:4], ACT.Sqrt).then_inc(rooted, 1)

                @block.vector
                def _(dve):
                    step = stepper(dve, dve_step)
                    dve.wait_ge(squared, TT)
                    dve.tensor_scalar(stat[:, 2:4], stat[:, 0:2], 1.0 / D, EPS, ALU.mult, ALU.add).then_inc(meaned, 1)
                    dve.wait_ge(rooted, 1)
                    step(dve.reciprocal(stat[:, 6:8], stat[:, 4:6]))
                    for i in range(TT):
                        dve.tensor_scalar(xn[:, i, :], X[:, i, :], stat[:, 6 + i:7 + i], None,
                                          ALU.mult).then_inc(scaled, 1)
                    for k in range(KT):
                        dve.wait_ge(turned, k + 1)
                        dve.tensor_scalar(HT[:, k, :], PS[:, k % 4, 0:S], scale[:, k:k + 1], shift[:, k:k + 1],
                                          ALU.mult, ALU.add).then_inc(evacuated, 1)

                @block.tensor
                def _(pe):
                    pe.wait_ge(scaled, TT)
                    for k in range(KT):
                        if k >= 4:
                            pe.wait_ge(evacuated, k - 3)
                        for i in range(TT):
                            mm = pe.transpose(PS[:, k % 4, i * P:(i + 1) * P],
                                              xn[:, i, :].rearrange("p (m k) -> p k m", k=KT)[:, k, :], ident[:])
                        mm.then_inc(turned, 1)

    def plain_norm(gain, result):
        with ExitStack() as scope:
            fg = sb(scope, "final_gain", [P, D])
            yo = sb(scope, "result", [P, TT, D])
            fin, squared, meaned, rooted, done, outs = (sem("f_gain"), sem("f_squared"), sem("f_meaned"), sem("f_rooted"),
                                                        sem("f_done"), sem("f_out"))
            with nc.Block() as block:
                @block.sync
                def _(sp):
                    sp.dma_start(fg[:], gain.partition_broadcast(P)).then_inc(fin, 16)
                    if result is not None:
                        for i in range(TT):
                            sp.wait_ge(done, i + 1)
                            sp.dma_start(result[0, i * P:(i + 1) * P, :], X[:, i, :]).then_inc(outs, 16)
                        sp.wait_ge(outs, 16 * TT)

                @block.scalar
                def _(act):
                    for i in range(TT):
                        act.activation(yo[:, i, :], X[:, i, :], ACT.Square, accum_out=stat[:, i:i + 1]).then_inc(squared, 1)
                    act.wait_ge(meaned, 1)
                    act.activation(stat[:, 4:6], stat[:, 2:4], ACT.Sqrt).then_inc(rooted, 1)

                @block.vector
                def _(dve):
                    step = stepper(dve, dve_step)
                    dve.wait_ge(squared, TT)
                    dve.tensor_scalar(stat[:, 2:4], stat[:, 0:2], 1.0 / D, EPS, ALU.mult, ALU.add).then_inc(meaned, 1)
                    dve.wait_ge(rooted, 1)
                    step(dve.reciprocal(stat[:, 6:8], stat[:, 4:6]))
                    dve.wait_ge(fin, 16)
                    for i in range(TT):
                        dve.scalar_tensor_tensor(out=X[:, i, :], in0=X[:, i, :], scalar=stat[:, 6 + i:7 + i], in1=fg[:],
                                                 op0=ALU.mult, op1=ALU.mult).then_inc(done, 1)

    def rows_chunk(pe, n, bank, src=None, ring=ring):
        src = HT if src is None else src
        w = w_slot(n, ring=ring)
        for m in range(2):
            for k in range(KT):
                mm = pe.matmul(PS[:, bank, m * S:(m + 1) * S], w[:, k, m * P:(m + 1) * P], src[:, k, :],
                               start=(k == 0), stop=(k == KT - 1))
        return mm

    def tokens_chunk(pe, n, bank, src=None, k0=0):
        src = HT if src is None else src
        w = w_slot(n)
        for i in range(TT):
            for k in range(KT):
                mm = pe.matmul(PS[:, bank, i * CW:(i + 1) * CW], src[:, k0 + k, i * P:(i + 1) * P], w[:, k, :],
                               start=(k == 0), stop=(k == KT - 1))
        return mm

    def project(parts, after=None):
        moved = sem("p_moved")
        todo = [(segs[s].base + c0 + j, kind, ev, j) for s, c0, n, kind, ev in parts for j in range(n)]
        with nc.Block() as block:
            @block.sync
            def _(sp):
                send_until(sp, todo[-1][0] + 1)

            @block.tensor
            def _(pe):
                for q, (n, kind, _, _) in enumerate(todo):
                    arrive(pe, n)
                    if q >= 4:
                        pe.wait_ge(moved, q - 3)
                    mm = (rows_chunk if kind == "rows" else tokens_chunk)(pe, n, q % 4)
                    mm.then_inc(used, 1)

            @block.scalar
            def _(act):
                for q, (n, kind, ev, j) in enumerate(todo):
                    act.wait_ge(used, n + 1)
                    ev(act, PS[:, q % 4, :].rearrange("p (a b) -> p a b", a=2), j).then_inc(moved, 1)

    def swiglu(name, source, count, gate):
        base = segs[name].base
        hid_ready, silu_ready = sem("e_hid"), sem("e_silu")
        pairs_n = (count - 2) // 2
        order = expert_order(count)
        B0 = base + 5
        with ExitStack() as scope:
            silu = sb(scope, "silu", [P, 2, 2, S])
            hid = sb(scope, "hid", [P, 2, 2, S])
            with nc.Block() as block:
                def bank(kind, par):
                    return 2 * par + (kind == "u")

                @block.sync
                def _(sp):
                    assert sent[0] == base + RING
                    with sp.Fori(0, pairs_n - 1) as i:
                        for j in range(6):
                            idx = RING + j
                            kind, e = order[idx]
                            sp.wait_ge(used, base + idx - RING + 1 + i * 6)
                            src = source(kind, e + i * 2)
                            n = base + idx
                            dst = ring[:, n % RING, :].rearrange("p (a b) -> p a b", b=src.shape[2])
                            sp.dma_start(dst, src).then_inc(landed[n % RING], 16)
                    sent[0] += 6 * (pairs_n - 1)
                    send_until(sp, base + len(order))

                @block.tensor
                def _(pe):
                    def up_gate(kind, n, par):
                        rows_chunk(pe, n, bank(kind, par)).then_inc(used, 1)

                    def down(n, par, first, last):
                        w = w_slot(n, D)
                        for f in range(2):
                            for i in range(TT):
                                for h in range(2):
                                    mm = pe.matmul(PS[:, 4 + 2 * i + h, :], hid[:, par, f, i * P:(i + 1) * P],
                                                   w[:, f, h * 512:(h + 1) * 512], start=first and f == 0,
                                                   stop=last and f == 1)
                        mm.then_inc(used, 1)

                    for idx in range(5):
                        kind, e = order[idx]
                        arrive(pe, base + idx)
                        if kind == "d":
                            pe.wait_ge(hid_ready, e + 1)
                            down(base + idx, e % 2, True, False)
                        else:
                            up_gate(kind, base + idx, e % 2)
                    with pe.Fori(0, pairs_n) as i:
                        for j in range(6):
                            kind, e = order[5 + j]
                            n = B0 + j
                            pe.wait_ge(landed[n % RING], i * 16 + 16 * (n // RING + 1))
                            if kind == "d":
                                pe.wait_ge(hid_ready, i * 2 + e + 1)
                                down(n, e % 2, False, False)
                            else:
                                up_gate(kind, n, e % 2)
                    for idx in range(5 + 6 * pairs_n, len(order)):
                        kind, e = order[idx]
                        arrive(pe, base + idx)
                        if kind == "d":
                            pe.wait_ge(hid_ready, e + 1)
                            down(base + idx, e % 2, False, e == count - 1)
                        else:
                            up_gate(kind, base + idx, e % 2)

                def up_done(e):
                    return base + (2 if e == 0 else 3 * e + 1)

                @block.scalar
                def _(act):
                    def one(par, gate_done):
                        act.wait_ge(used, gate_done)
                        act.activation(silu[:, par], PS[:, 2 * par, :].rearrange("p (a b) -> p a b", a=2),
                                       ACT.Silu).then_inc(silu_ready, 1)
                    one(0, up_done(0) - 1)
                    one(1, up_done(1) - 1)
                    with act.Fori(0, pairs_n) as i:
                        one(0, i * 6 + up_done(2) - 1)
                        one(1, i * 6 + up_done(3) - 1)
                    for e in range(2 + 2 * pairs_n, count):
                        one(e % 2, up_done(e) - 1)

                @block.vector
                def _(dve):
                    def one(par, up, nth):
                        dve.wait_ge(used, up)
                        u = PS[:, 2 * par + 1, :].rearrange("p (a b) -> p a b", a=2)
                        dve.wait_ge(silu_ready, nth)
                        dve.tensor_tensor(hid[:, par], u, silu[:, par], ALU.mult).then_inc(hid_ready, 1)

                    one(0, up_done(0), 1)
                    one(1, up_done(1), 2)
                    with dve.Fori(0, pairs_n) as i:
                        one(0, i * 6 + up_done(2), i * 2 + 3)
                        one(1, i * 6 + up_done(3), i * 2 + 4)
                    for e in range(2 + 2 * pairs_n, count):
                        one(e % 2, up_done(e), e + 1)
                    dve.wait_ge(used, base + len(order))
                    step = stepper(dve, dve_step)
                    add_gated(dve, step, PS[:, 4:8, :].rearrange("p (i h) n -> p i (h n)", i=TT), gate, scope)

    def routed_experts(pick, put, xn, sums):
        base = segs["moe"].base
        assert base + QC * QUADS == segs["hy_x"].base and QC % RING == 0
        scale, shift = mod[:, 3, :], mod[:, 2, :]
        with ExitStack() as scope:
            hs = sb(scope, "slot_rows", [P, KT, QUAD * SLOTS])
            silu = sb(scope, "silu", [P, 2, 2, SLOTS])
            hid = sb(scope, "hid", [P, 2, 2, SLOTS])
            ys = sb(scope, "slot_out", [P, D])
            put_now = sb(scope, "put_now", [P, S])
            gathered, hs_ready, silu_ready, hid_ready, scattered, added, y_moved, staged = (
                sem("m_gathered"), sem("m_hs"), sem("m_silu"), sem("m_hid"), sem("m_scattered"), sem("m_added"),
                sem("m_y"), sem("m_staged"))
            done_after = {item: pos + 1 for pos, item in enumerate(QUAD_ORDER)}

            def over_quads(eng, body):
                body(0, True, False)
                with eng.Fori(1, QUADS - 1) as q:
                    body(q, False, False)
                body(QUADS - 1, False, True)

            with nc.Block() as block:
                @block.sync
                def _(sp):
                    def quad(q, pos0, pos1, q_src):
                        for pos in range(pos0, pos1):
                            kind, e = QUAD_ORDER[pos]
                            n = base + pos
                            sp.wait_ge(used, q * QC + n - RING + 1)
                            src = moe_source(kind, q * QUAD + e)
                            dst = ring[:, n % RING, :].rearrange("p (a b) -> p a b", b=src.shape[2])
                            sp.dma_start(dst, src).then_inc(landed[n % RING], 16)
                    quad(0, RING, QC, 0)
                    with sp.Fori(1, QUADS) as q:
                        quad(q, 0, QC, q)
                    sent[0] = base + QC * QUADS
                    send_until(sp, sent[0])

                @block.tensor
                def _(pe):
                    def gather(q):
                        for half in range(2):
                            for k in range(4):
                                for i in range(TT):
                                    v = xn[:, i, :].rearrange("p (m k) -> p k m", k=KT)[:, 4 * half + k, :]
                                    mm = pe.matmul(PS[:, half, k * P:(k + 1) * P], v,
                                                   pick[:, i, ds(q * QUAD, QUAD), :].rearrange("p e s -> p (e s)"),
                                                   start=(i == 0), stop=(i == TT - 1))
                            mm.then_inc(gathered, 1)

                    def up_gate(e, q):
                        for j, kind in enumerate("gu"):
                            n = base + done_after[(kind, e)] - 1
                            pe.wait_ge(landed[n % RING], q * (16 * QC // RING) + 16 * (n // RING + 1))
                            w = w_slot(n)
                            for m in range(2):
                                for k in range(KT):
                                    mm = pe.matmul(PS[:, 2 + e % 2, (2 * j + m) * SLOTS:(2 * j + m + 1) * SLOTS],
                                                   w[:, k, m * P:(m + 1) * P], hs[:, k, e * SLOTS:(e + 1) * SLOTS],
                                                   start=(k == 0), stop=(k == KT - 1))
                            mm.then_inc(used, 1)

                    def down(e, q, first):
                        n = base + done_after[("d", e)] - 1
                        pe.wait_ge(landed[n % RING], q * (16 * QC // RING) + 16 * (n // RING + 1))
                        pe.wait_ge(hid_ready, q * QUAD + e + 1)
                        if e == 0 and not first:
                            pe.wait_ge(y_moved, q)
                        w = w_slot(n, D)
                        for h in range(2):
                            for f in range(2):
                                mm = pe.matmul(PS[e * SLOTS:(e + 1) * SLOTS, 4 + h, :], hid[:, e % 2, f, :],
                                               w[:, f, h * 512:(h + 1) * 512], start=(f == 0), stop=(f == 1))
                        mm.then_inc(used, 1)

                    def scatter(h, q, first):
                        pe.wait_ge(y_moved, q + 1)
                        pe.wait_ge(staged, q + 1)
                        if not (first and h == 0):
                            pe.wait_ge(added, q * 2 + h)
                        for i in range(TT):
                            mm = pe.matmul(PS[:, 6 + i, :], put_now[:, i * P:(i + 1) * P], ys[:, h * 512:(h + 1) * 512],
                                           start=True, stop=True)
                        mm.then_inc(scattered, 1)

                    def quad(q, first, last, second=False):
                        pe.wait_ge(hs_ready, q * 2 + 2)
                        up_gate(0, q)
                        if not first:
                            scatter(0, q - 1, second)
                        up_gate(1, q)
                        if not first:
                            scatter(1, q - 1, second)
                        down(0, q, first)
                        up_gate(2, q)
                        down(1, q, first)
                        up_gate(3, q)
                        down(2, q, first)
                        if not last:
                            gather(q + 1)
                        down(3, q, first)

                    gather(0)
                    quad(0, True, False)
                    quad(1, False, False, True)
                    with pe.Fori(2, QUADS - 1) as q:
                        quad(q, False, False)
                    quad(QUADS - 1, False, True)
                    scatter(0, QUADS - 1, False)
                    scatter(1, QUADS - 1, False)

                @block.scalar
                def _(act):
                    def quad(q, first, last):
                        for e in range(QUAD):
                            act.wait_ge(used, q * QC + base + done_after[("u", e)])
                            act.activation(silu[:, e % 2], PS[:, 2 + e % 2, 0:2 * SLOTS].rearrange(
                                "p (m s) -> p m s", m=2), ACT.Silu).then_inc(silu_ready, 1)
                        act.wait_ge(used, q * QC + base + QC)
                        act.activation(ys[:], PS[:, 4:6, :].rearrange("p b n -> p (b n)"), ACT.Copy).then_inc(y_moved, 1)
                    over_quads(act, quad)

                @block.gpsimd
                def _(pool):
                    def quad(q, first, last):
                        if not first:
                            pool.wait_ge(scattered, q * 2)
                        pool.tensor_copy(put_now[:], put[:, ds(q, 1), :].rearrange("p q n -> p (q n)")).then_inc(staged, 1)
                    over_quads(pool, quad)

                @block.vector
                def _(dve):
                    def make_rows(q):
                        for half in range(2):
                            dve.wait_ge(gathered, q * 2 + half + 1)
                            for k in range(4):
                                c = 4 * half + k
                                last = dve.tensor_scalar(hs[:, c, :], PS[:, half, k * P:(k + 1) * P], scale[:, c:c + 1],
                                                         shift[:, c:c + 1], ALU.mult, ALU.add)
                            last.then_inc(hs_ready, 1)

                    def activate(e, q):
                        dve.wait_ge(silu_ready, q * QUAD + e + 1)
                        dve.tensor_tensor(hid[:, e % 2], PS[:, 2 + e % 2, 2 * SLOTS:4 * SLOTS].rearrange(
                            "p (m s) -> p m s", m=2), silu[:, e % 2], ALU.mult).then_inc(hid_ready, 1)

                    def add(h, q):
                        dve.wait_ge(scattered, q * 2 + h + 1)
                        part = sums[:, :, h * 512:(h + 1) * 512]
                        dve.tensor_tensor(part, part, PS[:, 6:8, :], ALU.add).then_inc(added, 1)

                    def quad(q, first, last):
                        activate(0, q)
                        if not first:
                            add(0, q - 1)
                        activate(1, q)
                        if not first:
                            add(1, q - 1)
                        activate(2, q)
                        activate(3, q)
                        if not last:
                            make_rows(q + 1)

                    step = stepper(dve, dve_step)
                    step(dve.memset(sums[:], 0.0))
                    make_rows(0)
                    over_quads(dve, quad)
                    add(0, QUADS - 1)
                    add(1, QUADS - 1)

    def overflow_experts(rest, rows_dram, some_left, sums):
        with ExitStack() as scope:
            CB = sb(scope, "rest_rows", [P, EXPERTS, S])
            wb = sb(scope, "rest_w", [P, 3, 8 * CW])
            silu = sb(scope, "rest_silu", [P, 2, S])
            up = sb(scope, "rest_up", [P, 2, S])
            hid = sb(scope, "rest_hid", [P, 2, S])
            stored, spread = pool_dma_sem("o_stored"), pool_dma_sem("o_spread")
            arrived = [sem(f"o_arrived{j}") for j in range(3)]
            products, silu_ready, weighted, hid_ready, downs, added = (
                sem("o_products"), sem("o_silu"), sem("o_weighted"), sem("o_hid"), sem("o_downs"), sem("o_added"))

            def if_some(eng):
                return eng.If(eng.value_load(some_left[0:1, 0:1], min_val=0, max_val=1) > 0)

            with nc.Block() as block:
                @block.gpsimd
                def _(pool):
                    with if_some(pool):
                        pool.dma_start(rows_dram, rest[:]).then_inc(stored, 16)
                        pool.wait_ge(stored, 16)
                        pool.dma_start(CB[:], rows_dram.partition_broadcast(P)).then_inc(spread, 16)
                        pool.wait_ge(spread, 16)

                @block.sync
                def _(sp):
                    with if_some(sp):
                        with sp.Fori(0, EXPERTS) as e:
                            sp.wait_ge(downs, e + 1)
                            for j, kind in enumerate("gud"):
                                src = moe_source(kind, e)
                                sp.dma_start(wb[:, j, :].rearrange("p (a b) -> p a b", b=src.shape[2]), src)\
                                    .then_inc(arrived[j], 16)

                @block.tensor
                def _(pe):
                    with if_some(pe):
                        pe.sem_inc(downs, 1)
                        with pe.Fori(0, EXPERTS) as e:
                            for j in range(2):
                                pe.wait_ge(arrived[j], e * 16 + 16)
                                w = wb[:, j, :].rearrange("p (a b) -> p a b", b=CW)
                                for m in range(2):
                                    for k in range(KT):
                                        mm = pe.matmul(PS[:, j, m * S:(m + 1) * S], w[:, k, m * P:(m + 1) * P],
                                                       HT[:, k, :], start=(k == 0), stop=(k == KT - 1))
                            mm.then_inc(products, 1)
                            pe.wait_ge(arrived[2], e * 16 + 16)
                            pe.wait_ge(hid_ready, e + 1)
                            w = wb[:, 2, :].rearrange("p (a b) -> p a b", b=D)
                            for i in range(TT):
                                for h in range(2):
                                    for f in range(2):
                                        mm = pe.matmul(PS[:, 4 + 2 * i + h, :], hid[:, f, i * P:(i + 1) * P],
                                                       w[:, f, h * 512:(h + 1) * 512], start=(f == 0), stop=(f == 1))
                            mm.then_inc(downs, 1)
                            pe.wait_ge(added, e + 1)

                @block.scalar
                def _(act):
                    with if_some(act):
                        with act.Fori(0, EXPERTS) as e:
                            act.wait_ge(products, e + 1)
                            act.activation(silu[:], PS[:, 0, :].rearrange("p (m n) -> p m n", m=2), ACT.Silu)\
                                .then_inc(silu_ready, 1)

                @block.vector
                def _(dve):
                    with if_some(dve):
                        dve.wait_ge(spread, 16)
                        with dve.Fori(0, EXPERTS) as e:
                            dve.wait_ge(products, e + 1)
                            dve.tensor_tensor(up[:], PS[:, 1, :].rearrange("p (m n) -> p m n", m=2),
                                              CB[:, ds(e, 1), :].broadcast_to([P, 2, S]), ALU.mult).then_inc(weighted, 1)
                            dve.wait_ge(weighted, e + 1)
                            dve.wait_ge(silu_ready, e + 1)
                            dve.tensor_tensor(hid[:], up[:], silu[:], ALU.mult).then_inc(hid_ready, 1)
                            dve.wait_ge(downs, e + 2)
                            dve.tensor_tensor(sums[:], sums[:], PS[:, 4:8, :].rearrange("p (i h) n -> p i (h n)", i=TT),
                                              ALU.add).then_inc(added, 1)

    def add_gated(dve, step, psum, gate, scope):
        tmp = sb(scope, "gated", [P, TT, D])
        step(dve.tensor_tensor(tmp[:], psum, bc(gate[:], 1, TT), ALU.mult))
        step(dve.tensor_tensor(X[:], X[:], tmp[:], ALU.add))

    def output_projection(seg, src, groups, gate, bias=None):
        base = segs[seg].base
        with ExitStack() as scope:
            tmp = sb(scope, "op_tmp", [P, 2, TT, CW])
            moved = sem("o_moved")
            with nc.Block() as block:
                @block.sync
                def _(sp):
                    send_until(sp, base + 4 * groups)

                @block.tensor
                def _(pe):
                    for c in range(4):
                        for i in range(TT):
                            if i == 0:
                                for g in range(groups):
                                    arrive(pe, base + c * groups + g)
                            if bias is not None:
                                pe.matmul(PS[:, c, i * CW:(i + 1) * CW], ones[0:1, :], bias[0:1, c * CW:(c + 1) * CW],
                                          start=True, stop=False)
                            for g in range(groups):
                                w = w_slot(base + c * groups + g)
                                for k in range(KT):
                                    mm = pe.matmul(PS[:, c, i * CW:(i + 1) * CW],
                                                   src[:, g * KT + k, i * P:(i + 1) * P], w[:, k, :],
                                                   start=(bias is None and g == 0 and k == 0),
                                                   stop=(g == groups - 1 and k == KT - 1))
                                if i == TT - 1:
                                    mm.then_inc(used, 1)

                @block.vector
                def _(dve):
                    step = stepper(dve, dve_step)
                    for c in range(4):
                        dve.wait_ge(used, base + (c + 1) * groups)
                        step(dve.tensor_tensor(tmp[:, c % 2], PS[:, c, :].rearrange("p (i n) -> p i n", i=TT),
                                               bc(gate[:, c * CW:(c + 1) * CW], 1, TT), ALU.mult))
                        xc = X[:, :, c * CW:(c + 1) * CW]
                        step(dve.tensor_tensor(xc, xc, tmp[:, c % 2], ALU.add))

    def turn_features(src, dst, groups, gain):
        turned, moved = sem("t_turned"), sem("t_moved")
        n = groups * KT
        with nc.Block() as block:
            @block.tensor
            def _(pe):
                for k in range(n):
                    if k >= 4:
                        pe.wait_ge(moved, k - 3)
                    for i in range(TT):
                        v = src[:, i, (k // KT) * D:(k // KT + 1) * D].rearrange("p (m k) -> p k m", k=KT)
                        mm = pe.transpose(PS[:, k % 4, i * P:(i + 1) * P], v[:, k % KT, :], ident[:])
                    mm.then_inc(turned, 1)

            @block.vector
            def _(dve):
                for k in range(n):
                    dve.wait_ge(turned, k + 1)
                    if gain is None:
                        dve.tensor_copy(dst[:, k, :], PS[:, k % 4, 0:S]).then_inc(moved, 1)
                    else:
                        dve.tensor_scalar(dst[:, k, :], PS[:, k % 4, 0:S], gain[:, k:k + 1], None,
                                          ALU.mult).then_inc(moved, 1)

    modulation(t["c"], t["w_ada"][0], t["b_ada"][0], t["norm_mix"][0], t["norm_ffn"][0])
    norm_block(mod[:, 1, :], mod[:, 0, :])

    with ExitStack() as scope:
        merged = sb(scope, "merged", [P, TT, D])
        mix_gain = sb(scope, "mix_gain", [P, KT])
        inner = ExitStack()
        RT = sb(inner, "ret_tok", [P, TT, 4 * RET_W])
        HG = sb(inner, "hgrn_tok", [P, TT, 2 * HGRN_W])
        GG = sb(inner, "gla_tok", [P, TT, 2 * GLA_W])
        HF = sb(inner, "hgrn_rows", [P, 6, S])
        GF = sb(inner, "gla_rows", [P, 2, S])
        gaT = sb(inner, "gla_rank", [RANK, S])
        decay = sb(inner, "ret_decay", [P, RET_H, 384])
        level_mask = sb(inner, "level_mask", [P, LEVELS, P])
        freq = sb(inner, "freq", [P, 32])
        pos = sb(inner, "pos", [P, TT], I32)
        posf = sb(inner, "posf", [P, TT])
        wga = sb(inner, "wga", [P, KT, RANK])
        wa2 = sb(inner, "wa2", [RANK, P])
        gba = sb(inner, "gba", [P, 1])
        lb = sb(inner, "lb", [P, 8, 3])
        small = pool_dma_sem("mix_small")

        def mover(dst, width):
            def ev(act, bank, j):
                return act.activation(dst[:, :, j * CW:(j + 1) * CW] if width == "tokens" else
                                      dst[:, 2 * j:2 * j + 2, :], bank, ACT.Copy)
            return ev

        with nc.allow_non_contiguous_dma(reason="a few small vectors"):
            with nc.Block() as block:
                @block.gpsimd
                def _(pool):
                    loads = [
                        (decay[:], t["const_decay"]), (level_mask[:], t["const_levels"]),
                        (freq[:], t["const_freq"]),
                        (pos[:], t["positions"][0].rearrange("(i p) -> p i", p=P)),
                        (wga[:], wi[:, 15 * CW:].rearrange("(p k) n -> p k n", k=KT)),
                        (wa2[:], t["gla_wa2"][0]), (gba[:], t["gla_ba"][0].rearrange("(p a) -> p a", a=1)),
                        (lb[:, 0, :], t["hgrn_lb_logits"][0].rearrange("(m p) -> p m", p=P)),
                        (mix_gain[0:48, :], t["ret_norm"][0].rearrange("(p k) -> p k", k=KT)),
                        (mix_gain[48:96, :], t["hgrn_norm"][0].rearrange("(p k) -> p k", k=KT)),
                        (mix_gain[96:128, :], t["gla_norm"][0].rearrange("(p k) -> p k", k=KT)),
                    ]
                    for dst, src in loads:
                        pool.dma_start(dst, src).then_inc(small, 16)
                    pool.wait_ge(small, 16 * len(loads))

        project([("w_in", 0, 6, "tokens", mover(RT, "tokens")), ("w_in", 6, 3, "rows", mover(HF, "rows")),
                 ("w_in", 9, 3, "tokens", mover(HG, "tokens")), ("w_in", 12, 1, "rows", mover(GF, "rows")),
                 ("w_in", 13, 2, "tokens", mover(GG, "tokens"))])

        qd = sb(inner, "gated_q", [P, 4, S])
        kd = sb(inner, "gated_k", [P, 4, S])
        ad = sb(inner, "gated_a", [P, 4, S])
        g_low, g_gate, g_sig, g_e = sem("g_low"), sem("g_gate"), sem("g_sig"), sem("g_e")
        lb_e, ang, trig, lowc = sem("lb_e"), sem("ang"), sem("trig"), sem("lowc")
        y_ready, ln_ready, e_ready = sem("y_ready"), sem("ln_ready"), sem("e_ready")
        narrow = ExitStack()
        w1 = sb(narrow, "gla_w", [P, 3, S])
        rot = sb(narrow, "rot", [P, 2, TT, 2 * RET_W])
        angle = sb(narrow, "angle", [P, 6, TT, 32])
        MAGIC = 12582912.0
        with nc.Block() as block:
            @block.tensor
            def _(pe):
                for k in range(KT):
                    mm = pe.matmul(PS[0:RANK, 0, 0:S], wga[:, k, :], HT[:, k, :], start=(k == 0), stop=(k == KT - 1))
                mm.then_inc(g_low, 1)
                pe.wait_ge(lowc, 1)
                pe.matmul(PS[:, 1, 0:S], wa2[:], gaT[:], start=True, stop=True).then_inc(g_gate, 1)

            @block.scalar
            def _(act):
                act.wait_ge(g_low, 1)
                act.activation(gaT[:], PS[0:RANK, 0, 0:S], ACT.Copy).then_inc(lowc, 1)
                act.activation(kd[:, 0:3, :], HF[:, 3:6, :], ACT.Sigmoid, scale=-1.0)
                act.activation(ad[:, 0:3, :], HF[:, 3:6, :], ACT.Sigmoid).then_inc(g_sig, 1)
                act.activation(qd[:, 0:3, :], HF[:, 0:3, :], ACT.Silu).then_inc(g_sig, 1)
                act.activation(RT[:, :, 3 * RET_W:], RT[:, :, 3 * RET_W:], ACT.Silu)
                act.activation(HG[:, :, HGRN_W:], HG[:, :, HGRN_W:], ACT.Silu)
                act.activation(GG[:, :, GLA_W:], GG[:, :, GLA_W:], ACT.Silu)
                act.wait_ge(lb_e, 1)
                act.activation(lb[:, 2, :], lb[:, 1, :], ACT.Exp).then_inc(lb_e, 1)
                act.wait_ge(y_ready, 1)
                act.activation(w1[:, 1, :], w1[:, 1, :], ACT.Exp).then_inc(e_ready, 1)
                act.wait_ge(e_ready, 1)
                act.activation(w1[:, 2, :], w1[:, 1, :], ACT.Ln, bias=1.0).then_inc(ln_ready, 1)
                act.wait_ge(y_ready, 2)
                act.activation(ad[:, 3, :], w1[:, 0, :], ACT.Exp, scale=1.0 / TAU)
                act.wait_ge(ang, 1)
                act.activation(angle[:, 4:6], angle[:, 2:4], ACT.Sin).then_inc(trig, 1)

            @block.vector
            def _(dve):
                step = stepper(dve, dve_step)
                dve.wait_ge(g_gate, 1)
                step(dve.tensor_scalar(w1[:, 0, :], PS[:, 1, 0:S], gba[:, 0:1], None, ALU.add))
                step(dve.tensor_scalar(w1[:, 2, :], w1[:, 0, :], -1.0, None, ALU.mult))
                dve.tensor_tensor(w1[:, 1, :], w1[:, 0, :], w1[:, 2, :], ALU.min).then_inc(y_ready, 1)
                dve.tensor_tensor(lb[:, 1, :], lb[:, 0, :], lb[:, 0, :], ALU.subtract).then_inc(lb_e, 1)
                dve.wait_ge(lb_e, 2)
                step(dve.reciprocal(lb[:, 3, :], lb[:, 2, :]))
                step(dve.tensor_tensor(lb[:, 4, :], lb[:, 2, :], lb[:, 3, :], ALU.mult))
                step(dve.tensor_tensor(lb[:, 5, :], lb[:, 4, :], lb[:, 4, :], ALU.subtract))
                step(dve.tensor_scalar(lb[:, 6, :], lb[:, 5, :], -1.0, 1.0, ALU.mult, ALU.add))
                step(dve.tensor_copy(posf[:], pos[:]))
                for i in range(TT):
                    step(dve.tensor_scalar(angle[:, 0, i, :], freq[:], posf[:, i:i + 1], None, ALU.mult))
                step(dve.tensor_scalar(angle[:, 1], angle[:, 0], 0.15915494309189535, MAGIC, ALU.mult, ALU.add))
                step(dve.tensor_scalar(angle[:, 1], angle[:, 1], -MAGIC, None, ALU.add))
                for piece in (6.28125, 1.93530321e-03, 6.283185307179586 - 6.28125 - 1.93530321e-03):
                    step(dve.scalar_tensor_tensor(out=angle[:, 0], in0=angle[:, 1], scalar=-piece, in1=angle[:, 0],
                                                  op0=ALU.mult, op1=ALU.add))
                step(dve.tensor_scalar(angle[:, 2], angle[:, 0], 3.1415925, -3.1415925, ALU.min, ALU.max))
                step(dve.tensor_scalar(angle[:, 4], angle[:, 2], -1.0, None, ALU.mult))
                step(dve.tensor_tensor(angle[:, 3], angle[:, 2], angle[:, 4], ALU.max))
                dve.tensor_scalar(angle[:, 3], angle[:, 3], -1.0, 1.5707963267948966, ALU.mult,
                                  ALU.add).then_inc(ang, 1)
                dve.wait_ge(g_sig, 2)
                for m in range(3):
                    dve.tensor_scalar(ad[:, m, :], ad[:, m, :], lb[:, 6, m:m + 1], lb[:, 5, m:m + 1], ALU.mult, ALU.add)
                    dve.tensor_scalar(kd[:, m, :], kd[:, m, :], lb[:, 6, m:m + 1], None, ALU.mult)
                step(dve.tensor_scalar(qd[:, 0:3, :], qd[:, 0:3, :], HD ** -0.5, None, ALU.mult))
                step(dve.tensor_scalar(ad[:, 0:3, :], ad[:, 0:3, :], F_MIN, None, ALU.max))
                dve.tensor_scalar(qd[:, 3, :], GF[:, 0, :], GLA_DK ** -0.5, None, ALU.mult)
                dve.tensor_copy(kd[:, 3, :], GF[:, 1, :])
                dve.wait_ge(ln_ready, 1)
                dve.scalar_tensor_tensor(out=w1[:, 0, :], in0=w1[:, 0, :], scalar=0.0, in1=w1[:, 2, :],
                                         op0=ALU.min, op1=ALU.subtract).then_inc(y_ready, 1)
                dve.wait_ge(trig, 1)
                for i in range(TT):
                    qk = RT[:, i, 0:2 * RET_W].rearrange("p (h a d) -> p h a d", a=2, d=32)
                    for j, tab in ((0, 5), (1, 4)):
                        for a in range(2):
                            last = dve.tensor_tensor(rot[:, j, i, :].rearrange("p (h a d) -> p h a d", a=2, d=32)[:, :, a, :],
                                              qk[:, :, a, :], bc(angle[:, tab, i, :], 1, 2 * RET_H), ALU.mult)
                    c4 = rot[:, 0, i, :].rearrange("p (h a d) -> p h a d", a=2, d=32)
                    s4 = rot[:, 1, i, :].rearrange("p (h a d) -> p h a d", a=2, d=32)
                    step(last)
                    dve.tensor_tensor(qk[:, :, 0, :], c4[:, :, 0, :], s4[:, :, 1, :], ALU.subtract)
                    dve.tensor_tensor(qk[:, :, 1, :], c4[:, :, 1, :], s4[:, :, 0, :], ALU.add)

        narrow.close()

        QT = sb(inner, "ret_T", [P, 6, S])
        SW = sb(inner, "ret_scores", [P, 2, 384])
        QL = sb(inner, "level_q", [P, LEVELS, 2, S])
        KL = sb(inner, "level_k", [P, LEVELS, 2, S])
        prefix = sb(inner, "prefix", [P, 2, S])
        suffix = sb(inner, "suffix", [P, 2, S])

        def o_cols(head, i):
            c = head * HD
            return PS[:, 4 + 2 * i + c // 512, c % 512:c % 512 + HD]

        def level_factors(pool, m0):
            step = stepper(pool, pool_step)
            qs, ks = qd[:, m0:m0 + 2, :], kd[:, m0:m0 + 2, :]
            pool.tensor_copy(prefix[:], ad[:, m0:m0 + 2, :])
            step(pool.memset(suffix[:], 1.0))
            for l in range(1, LEVELS + 1):
                b = 1 << (l - 1)
                pool.tensor_tensor(QL[:, l % LEVELS], qs, prefix[:], ALU.mult)
                step(pool.tensor_tensor(KL[:, l % LEVELS], ks, suffix[:], ALU.mult))
                if l < LEVELS:
                    n = 2 * S // (2 * b)
                    pv = prefix[:].rearrange("p m t -> p (m t)").rearrange("p (n h b) -> p n h b", h=2, b=b)
                    sv = suffix[:].rearrange("p m t -> p (m t)").rearrange("p (n h b) -> p n h b", h=2, b=b)
                    step(pool.tensor_tensor(sv[:, :, 0, :], sv[:, :, 0, :],
                                            pv[:, :, 1, b - 1:b].broadcast_to([P, n, b]), ALU.mult))
                    step(pool.tensor_tensor(pv[:, :, 1, :], pv[:, :, 1, :],
                                            pv[:, :, 0, b - 1:b].broadcast_to([P, n, b]), ALU.mult))

        turned, tmoved, r_sc, r_w = sem("r_turned"), sem("r_tmoved"), sem("r_scores"), sem("r_weights")
        with nc.Block() as block:
            @block.gpsimd
            def _(pool):
                level_factors(pool, 0)

            @block.tensor
            def _(pe):
                for j in range(6):
                    if j >= 4:
                        pe.wait_ge(tmoved, j - 3)
                    for i in range(TT):
                        mm = pe.transpose(PS[:, j % 4, i * P:(i + 1) * P], RT[:, i, j * P:(j + 1) * P], ident[:])
                    mm.then_inc(turned, 1)
                pe.wait_ge(tmoved, 6)

                def values(h):
                    pe.wait_ge(r_w, h + 1)
                    w = SW[:, h % 2, :]
                    v = RT[:, :, 2 * RET_W + h * HD:2 * RET_W + (h + 1) * HD]
                    pe.matmul(o_cols(h, 0), w[:, 0:P], v[:, 0, :], start=True, stop=True)
                    pe.matmul(o_cols(h, 1), w[:, P:2 * P], v[:, 0, :], start=True, stop=False)
                    pe.matmul(o_cols(h, 1), w[:, 2 * P:3 * P], v[:, 1, :], start=False, stop=True)

                for h in range(RET_H):
                    r0, m = HD * (h % 2), h // 2
                    q, k = QT[r0:r0 + HD, m, :], QT[r0:r0 + HD, 3 + m, :]
                    pe.matmul(PS[:, h % 4, 0:S], k[:, 0:P], q, start=True, stop=True)
                    pe.matmul(PS[:, h % 4, S:384], k[:, P:S], q[:, P:S], start=True, stop=True).then_inc(r_sc, 1)
                    if h:
                        values(h - 1)
                values(RET_H - 1)

            @block.vector
            def _(dve):
                for j in range(6):
                    dve.wait_ge(turned, j + 1)
                    dve.tensor_copy(QT[:, j, :], PS[:, j % 4, 0:S]).then_inc(tmoved, 1)
                for h in range(RET_H):
                    dve.wait_ge(r_sc, h + 1)
                    dve.scalar_tensor_tensor(out=SW[:, h % 2, :], in0=PS[:, h % 4, 0:384], scalar=HD ** -0.5,
                                             in1=decay[:, h, :], op0=ALU.mult, op1=ALU.mult).then_inc(r_w, 1)

        GWT = sb(inner, "gated_scores", [P, 2, LEVELS, P])
        CR = sb(inner, "cross", [P, 6, P])

        def cross_place(gated, c):
            r0 = gated[c][1]
            k = sum(g[1] == r0 for g in gated[:c])
            return PS[:, r0 // 32, k * P:(k + 1) * P]

        def gated_heads(gated, m0):
            g_sc, g_w, g_cr, g_crw = sem("g_scores"), sem("g_weights"), sem("g_cross"), sem("g_crossw")
            units = [(g, i) for g in gated for i in range(TT)]
            n = len(gated)
            with nc.Block() as block:
                @block.tensor
                def _(pe):
                    for c, (m, r0, dk, _, _, _) in enumerate(gated):
                        mm = pe.matmul(cross_place(gated, c), KL[r0:r0 + dk, 0, m - m0, 0:P],
                                       QL[r0:r0 + dk, 0, m - m0, P:S], start=True, stop=True)
                    mm.then_inc(g_cr, 1)
                    pe.wait_ge(g_crw, 1)

                    def scores(u):
                        (m, r0, dk, _, _, _), i = units[u]
                        for l in range(LEVELS):
                            q = (qd[r0:r0 + dk, m] if l == 0 else QL[r0:r0 + dk, l, m - m0])[:, i * P:(i + 1) * P]
                            k = (kd[r0:r0 + dk, m] if l == 0 else KL[r0:r0 + dk, l, m - m0])[:, i * P:(i + 1) * P]
                            mm = pe.matmul(PS[:, 2 * (u % 2) + l // 4, (l % 4) * P:(l % 4 + 1) * P], k, q,
                                           start=True, stop=True)
                        mm.then_inc(g_sc, 1)

                    def values(u):
                        (_, _, _, src, v0, head), i = units[u]
                        pe.wait_ge(g_w, u + 1)
                        for l in range(LEVELS):
                            pe.matmul(o_cols(head, i), GWT[:, u % 2, l, :], src[:, i, v0:v0 + HD], start=(l == 0),
                                      stop=(i == 0 and l == LEVELS - 1))
                        if i:
                            pe.matmul(o_cols(head, i), CR[:, u // 2, :], src[:, 0, v0:v0 + HD], start=False, stop=True)

                    for u in range(2 * n):
                        if u >= 2:
                            pe.wait_ge(g_w, u - 1)
                        scores(u)
                        if u:
                            values(u - 1)
                    values(2 * n - 1)

                @block.vector
                def _(dve):
                    dve.wait_ge(g_cr, 1)
                    for c in range(n):
                        last = dve.tensor_copy(CR[:, c, :], cross_place(gated, c))
                    last.then_inc(g_crw, 1)
                    for u in range(2 * n):
                        dve.wait_ge(g_sc, u + 1)
                        b = 2 * (u % 2)
                        dve.tensor_tensor(GWT[:, u % 2], PS[:, b:b + 2, :].rearrange("p a (l n) -> p (a l) n", n=P),
                                          level_mask[:], ALU.mult).then_inc(g_w, 1)

        gated = [(h // 2, HD * (h % 2), HD, HG, h * HD, RET_H + h) for h in range(HGRN_H)]
        gated += [(3, GLA_DK * h, GLA_DK, GG, h * HD, RET_H + HGRN_H + h) for h in range(GLA_H)]
        gated_heads(gated[:4], 0)
        with nc.Block() as block:
            @block.gpsimd
            def _(pool):
                level_factors(pool, 2)
        gated_heads(gated[4:], 2)

        hs = sb(inner, "head_sums", [P, 4, TT * HEADS])
        squared, meaned, rooted = sem("h_squared"), sem("h_meaned"), sem("h_rooted")
        O = PS[:, 4:8, :].rearrange("p (i b) n -> p i (b n)", i=TT)
        with nc.Block() as block:
            @block.scalar
            def _(act):
                act.activation(merged[:], O, ACT.Square).then_inc(squared, 1)
                act.wait_ge(meaned, 1)
                act.activation(hs[:, 2, :], hs[:, 1, :], ACT.Sqrt).then_inc(rooted, 1)

            @block.vector
            def _(dve):
                step = stepper(dve, dve_step)
                dve.wait_ge(squared, 1)
                step(dve.tensor_reduce(hs[:, 0, :], merged[:].rearrange("p i (h d) -> p (i h) d", d=HD), AX.X, ALU.add))
                dve.tensor_scalar(hs[:, 1, :], hs[:, 0, :], 1.0 / HD, EPS, ALU.mult, ALU.add).then_inc(meaned, 1)
                dve.wait_ge(rooted, 1)
                step(dve.reciprocal(hs[:, 3, :], hs[:, 2, :]))
                step(dve.tensor_tensor(merged[:].rearrange("p i (h d) -> p (i h) d", d=HD),
                                       PS[:, 4:8, :].rearrange("p b (h d) -> p (b h) d", d=HD),
                                       bc(hs[:, 3, :], 2, HD), ALU.mult))
                for c0, g in ((0, RT[:, :, 3 * RET_W:]), (RET_W, HG[:, :, HGRN_W:]),
                              (RET_W + HGRN_W, GG[:, :, GLA_W:])):
                    part = merged[:, :, c0:c0 + g.shape[2]]
                    dve.tensor_tensor(part, part, g, ALU.mult)
        inner.close()
        MT = sb(scope, "merged_T", [P, KT, S])
        turn_features(merged, MT, 1, mix_gain)
        output_projection("w_out", MT, 1, gate_a)

    clear_phase_sems()

    with ExitStack() as scope:
        xn = sb(scope, "normed", [P, TT, D])
        pick = sb(scope, "pick", [P, TT, EXPERTS, SLOTS])
        put = sb(scope, "put", [P, QUADS, S])
        rest = sb(scope, "rest_T", [EXPERTS, S])
        some_left = sb(scope, "some_left", [P, 1], I32)
        norm_block(mod[:, 3, :], mod[:, 2, :], xn)
        route = ExitStack()
        NR = GROUPS + EXPERTS
        wr = sb(route, "w_router", [P, KT, NR])
        br = sb(route, "b_router", [P, NR])
        lg = sb(route, "logits", [P, TT, NR])
        order4 = sb(route, "order4", [P, 16])
        g4 = sb(route, "group_scratch", [P, 4, TT, GROUPS])
        e8 = sb(route, "expert_scratch", [P, 8, TT, PER_GROUP])
        s1 = sb(route, "scalars", [P, 16, TT])
        em = sb(route, "by_group", [P, TT, EXPERTS])
        slots = sb(route, "slot_numbers", [P, SLOTS])
        member = sb(route, "member", [P, TT, EXPERTS])
        place = sb(route, "place", [P, TT, EXPERTS])
        keep = sb(route, "past_slots", [P, TT, EXPERTS])
        heavy = sb(route, "weighted_pick", [P, TT, EXPERTS, SLOTS])
        most = sb(route, "most", [P, 2])
        ranked, rank_ready, heavied, turned, moved, restd = (sem("r_ranked"), sem("r_rank"), sem("r_heavy"),
                                                             sem("r_turned"), sem("r_moved"), sem("r_rest"))
        small, lgm, xin, xout = pool_dma_sem("r_small"), sem("r_logits"), sem("r_expin"), sem("r_expout")
        rows_dram = nc.dram_tensor("combine_rows", (EXPERTS, S), F32, kind="Internal").ap()
        with nc.Block() as block:
            @block.gpsimd
            def _(pool):
                with nc.allow_non_contiguous_dma(reason="small router weights"):
                    pool.dma_start(wr[:, :, 0:GROUPS],
                                   t["router_group_w"][0].rearrange("(p k) n -> p k n", k=KT)).then_inc(small, 16)
                    pool.dma_start(wr[:, :, GROUPS:],
                                   t["router_expert_w"][0].rearrange("(p k) n -> p k n", k=KT)).then_inc(small, 16)
                pool.dma_start(br[:, 0:GROUPS], t["router_group_b"][0].partition_broadcast(P)).then_inc(small, 16)
                pool.dma_start(br[:, GROUPS:], t["router_expert_b"][0].partition_broadcast(P)).then_inc(small, 16)
                pool.dma_start(order4[:], t["const_order"]).then_inc(small, 16)
                pool.dma_start(slots[:], t["const_slots"]).then_inc(small, 16)

            @block.tensor
            def _(pe):
                pe.wait_ge(small, 96)
                for i in range(TT):
                    for k in range(KT):
                        mm = pe.matmul(PS[:, i, 0:NR], HT[:, k, i * P:(i + 1) * P], wr[:, k, :],
                                       start=(k == 0), stop=(k == KT - 1))
                mm.then_inc(lgm, 1)
                pe.wait_ge(ranked, 1)
                pe.matmul(PS[:, 2, 0:EXPERTS], pairs[:, 0:P], member[:, 0, :], start=True, stop=True)
                pe.matmul(PS[:, 2, EXPERTS:2 * EXPERTS], ones[:], member[:, 0, :], start=True, stop=False)
                pe.matmul(PS[:, 2, EXPERTS:2 * EXPERTS], pairs[:, 0:P], member[:, 1, :], start=False, stop=True)
                pe.matmul(PS[:, 3, 0:EXPERTS], ones[:], member[:, 0, :], start=True, stop=False)
                pe.matmul(PS[:, 3, 0:EXPERTS], ones[:], member[:, 1, :], start=False, stop=True).then_inc(rank_ready, 1)
                pe.wait_ge(restd, 1)
                for i in range(TT):
                    mm = pe.transpose(PS[0:EXPERTS, 0, i * P:(i + 1) * P], keep[:, i, :], ident[:])
                mm.then_inc(lgm, 1)
                pe.wait_ge(heavied, TT)
                for q in range(QUADS):
                    if q >= 4:
                        pe.wait_ge(moved, q - 3)
                    for i in range(TT):
                        mm = pe.transpose(PS[:, 4 + q % 4, i * P:(i + 1) * P],
                                          heavy[:, i, q * QUAD:(q + 1) * QUAD, :].rearrange("p e s -> p (e s)"), ident[:])
                    mm.then_inc(turned, 1)

            @block.scalar
            def _(act):
                act.wait_ge(xin, 1)
                act.activation(g4[:, 0], g4[:, 0], ACT.Exp).then_inc(xout, 1)
                act.wait_ge(xin, 2)
                act.activation(s1[:, 6, :], s1[:, 6, :], ACT.Exp).then_inc(xout, 1)
                for q in range(QUADS):
                    act.wait_ge(turned, q + 1)
                    act.activation(put[:, q, :], PS[:, 4 + q % 4, 0:S], ACT.Copy).then_inc(moved, 1)

            @block.vector
            def _(dve):
                step = stepper(dve, dve_step)
                dve.wait_ge(lgm, 1)
                step(dve.tensor_tensor(lg[:], PS[:, 0:2, 0:NR], bc(br[:], 1, TT), ALU.add))
                gl = lg[:, :, 0:GROUPS]
                step(dve.tensor_reduce(s1[:, 0, :], gl, AX.X, ALU.max))
                dve.tensor_tensor(g4[:, 0], gl, bc(s1[:, 0, :], 2, GROUPS), ALU.subtract).then_inc(xin, 1)

                def first_of_equals(x, top, n, tmp, best, onehot):
                    step(dve.tensor_tensor(tmp, x, bc(top, 2, n), ALU.is_equal))
                    step(dve.tensor_tensor(tmp, tmp, bc(order4[:, 0:n], 1, TT), ALU.mult))
                    step(dve.tensor_reduce(best, tmp, AX.X, ALU.max))
                    step(dve.tensor_tensor(onehot, tmp, bc(best, 2, n), ALU.is_equal))

                first_of_equals(gl, s1[:, 0, :], GROUPS, g4[:, 1], s1[:, 1, :], g4[:, 2])
                dve.wait_ge(xout, 1)
                step(dve.tensor_reduce(s1[:, 2, :], g4[:, 0], AX.X, ALU.add))
                step(dve.reciprocal(s1[:, 3, :], s1[:, 2, :]))
                for i in range(TT):
                    last = dve.tensor_tensor(em[:, i, :].rearrange("p (g e) -> p g e", g=GROUPS),
                                             lg[:, i, GROUPS:].rearrange("p (g e) -> p g e", g=GROUPS),
                                             bc(g4[:, 2, i, :], 2, PER_GROUP), ALU.mult)
                step(last)
                for i in range(TT):
                    last = dve.tensor_reduce(e8[:, 0, i, :], em[:, i, :].rearrange("p (g e) -> p e g", g=GROUPS),
                                             AX.X, ALU.add)
                step(last)
                step(dve.tensor_reduce(s1[:, 4, :], e8[:, 0], AX.X, ALU.max))
                first_of_equals(e8[:, 0], s1[:, 4, :], PER_GROUP, e8[:, 1], s1[:, 1, :], e8[:, 2])
                step(dve.scalar_tensor_tensor(out=e8[:, 3], in0=e8[:, 2], scalar=NEG, in1=e8[:, 0],
                                              op0=ALU.mult, op1=ALU.add))
                step(dve.tensor_reduce(s1[:, 5, :], e8[:, 3], AX.X, ALU.max))
                dve.tensor_tensor(s1[:, 6, :], s1[:, 5, :], s1[:, 4, :], ALU.subtract).then_inc(xin, 1)
                first_of_equals(e8[:, 3], s1[:, 5, :], PER_GROUP, e8[:, 1], s1[:, 1, :], e8[:, 4])
                dve.wait_ge(xout, 2)
                step(dve.tensor_scalar(s1[:, 7, :], s1[:, 6, :], 1.0, None, ALU.add))
                step(dve.reciprocal(s1[:, 8, :], s1[:, 7, :]))
                step(dve.tensor_tensor(s1[:, 9, :], s1[:, 8, :], s1[:, 3, :], ALU.mult))
                step(dve.tensor_tensor(s1[:, 10, :], s1[:, 9, :], s1[:, 6, :], ALU.mult))
                dve.tensor_tensor(e8[:, 5], e8[:, 2], bc(s1[:, 9, :], 2, PER_GROUP), ALU.mult)
                step(dve.tensor_tensor(e8[:, 6], e8[:, 4], bc(s1[:, 10, :], 2, PER_GROUP), ALU.mult))
                step(dve.tensor_tensor(e8[:, 7], e8[:, 5], e8[:, 6], ALU.add))
                for i in range(TT):
                    last = dve.tensor_tensor(em[:, i, :].rearrange("p (g e) -> p g e", g=GROUPS),
                                             bc(g4[:, 2, i, :], 2, PER_GROUP), bc(e8[:, 7, i, :], 1, GROUPS), ALU.mult)
                step(last)
                step(dve.tensor_tensor(e8[:, 5], e8[:, 2], e8[:, 4], ALU.add))
                for i in range(TT):
                    last = dve.tensor_tensor(member[:, i, :].rearrange("p (g e) -> p g e", g=GROUPS),
                                             bc(g4[:, 2, i, :], 2, PER_GROUP), bc(e8[:, 5, i, :], 1, GROUPS), ALU.mult)
                last.then_inc(ranked, 1)
                dve.wait_ge(rank_ready, 1)
                step(dve.tensor_tensor(place[:], PS[:, 2, 0:2 * EXPERTS].rearrange("p (i e) -> p i e", i=TT), member[:],
                                       ALU.mult))
                step(dve.tensor_scalar(place[:], place[:], -1.0, None, ALU.add))
                step(dve.tensor_scalar(keep[:], place[:], float(SLOTS), None, ALU.is_ge))
                dve.tensor_tensor(keep[:], keep[:], em[:], ALU.mult).then_inc(restd, 1)
                step(dve.tensor_reduce(most[:, 0:1], PS[:, 3, 0:EXPERTS], AX.X, ALU.max))
                step(dve.tensor_scalar(most[:, 1:2], most[:, 0:1], float(SLOTS), None, ALU.is_gt))
                dve.tensor_copy(some_left[:], most[:, 1:2])
                for i in range(TT):
                    step(dve.tensor_tensor(pick[:, i], bc(place[:, i, :], 2, SLOTS), bc(slots[:], 1, EXPERTS),
                                           ALU.is_equal))
                    dve.tensor_tensor(heavy[:, i], pick[:, i], bc(em[:, i, :], 2, SLOTS), ALU.mult).then_inc(heavied, 1)
                dve.wait_ge(lgm, 2)
                dve.tensor_copy(rest[:], PS[0:EXPERTS, 0, 0:S])
        route.close()
        sums = sb(scope, "expert_sums", [P, TT, D])
        routed_experts(pick, put, xn, sums)
        overflow_experts(rest, rows_dram, some_left, sums)
        with nc.Block() as block:
            @block.vector
            def _(dve):
                step = stepper(dve, dve_step)
                step(dve.tensor_tensor(sums[:], sums[:], bc(gate_b[:], 1, TT), ALU.mult))
                dve.tensor_tensor(X[:], X[:], sums[:], ALU.add)

    plain_norm(t["norm_final"], None)

    clear_phase_sems()

    modulation(t["c_2"], t["ada_w"][0], t["ada_b"][0], t["norm_mix_g"][0], t["norm_ffn_g"][0])
    norm_block(mod[:, 1, :], mod[:, 0, :])

    with ExitStack() as scope:
        att = sb(scope, "att", [P, TT, KV_H * HD])
        y = sb(scope, "y", [P, TT, SSM_IN])
        ssm_gain = sb(scope, "ssm_gain", [P, 2 * KT])
        wide = ExitStack()
        ZV = sb(wide, "z_v", [P, TT, SSM_IN + KV_H * HD])
        XB = sb(wide, "xbc", [P, XT, S + CONV - 1])
        dt = sb(wide, "dt", [P, TT, SSM_H])
        convT = sb(wide, "conv_T", [P, (CONV + 1) * XT])
        rowc = sb(wide, "row_consts", [P, 3, SSM_H])

        inner = ExitStack()
        QT = sb(inner, "att_q", [P, ATT_G * KT, S])
        KTT = sb(inner, "att_k", [P, KT, S])
        wdt = sb(inner, "w_dt", [P, KT, SSM_H])
        rawc = sb(inner, "conv_raw", [P, P])
        table = sb(inner, "rel_table", [BUCKETS, ATT_G * KV_H])
        onehot = sb(inner, "bucket_onehot", [BUCKETS, 384])
        gsel = sb(inner, "group_select", [ATT_G, ATT_G * KV_H])
        gmask = sb(inner, "group_mask", [ATT_G, 384])
        flip = sb(inner, "flip", [P, P])
        bias_rows = sb(inner, "bias_rows", [ATT_G * KV_H, 384])
        bias_dram = nc.dram_tensor("bias_rows_dram", (ATT_G * KV_H, 384), F32, kind="Internal").ap()
        small, made, moved1, stored = pool_dma_sem("a_small"), sem("a_made"), sem("a_moved"), pool_dma_sem("a_stored")
        with nc.Block() as block:
            @block.gpsimd
            def _(pool):
                with nc.allow_non_contiguous_dma(reason="small vectors"):
                    loads = [
                        (wdt[:], hi[:, HY_DT:HY_DT + SSM_H].rearrange("(p k) n -> p k n", k=KT)),
                        (rawc[0:CONV * XT, :], t["hy_conv_w"][0].rearrange("j (m p) -> (j m) p", p=P)),
                        (rawc[CONV * XT:(CONV + 1) * XT, :], t["hy_conv_b"][0].rearrange("(m p) -> m p", p=P)),
                        (table[:], t["rel_table"]), (onehot[:], t["const_onehot"]), (gsel[:], t["const_gsel"]),
                        (gmask[:], t["const_gmask"]), (flip[:], t["const_flip"]),
                        (rowc[:, 0, :], t["hy_dt_bias"][0].partition_broadcast(P)),
                        (rowc[:, 1, :], t["hy_a_log"][0].partition_broadcast(P)),
                        (rowc[:, 2, :], t["hy_d_skip"][0].partition_broadcast(P)),
                        (ssm_gain[:, 0:KT], t["hy_ssm_norm_g"][0][0:D].rearrange("(p k) -> p k", k=KT)),
                        (ssm_gain[:, KT:], t["hy_ssm_norm_g"][0][D:].rearrange("(p k) -> p k", k=KT)),
                    ]
                    for dst, src in loads:
                        pool.dma_start(dst, src).then_inc(small, 16)
                pool.wait_ge(moved1, 1)
                pool.dma_start(bias_dram, bias_rows[:]).then_inc(stored, 16)
                pool.wait_ge(stored, 16)

            @block.tensor
            def _(pe):
                pe.wait_ge(small, 16 * 13)
                n = (CONV + 1) * XT
                pe.matmul(PS[0:ATT_G * KV_H, 1, 0:384], table[:], onehot[:], start=True, stop=False)
                pe.matmul(PS[0:ATT_G * KV_H, 1, 0:384], gsel[:], gmask[:], start=False, stop=True)
                pe.transpose(PS[:, 0, 0:n], rawc[0:n, :], ident[0:n, 0:n]).then_inc(made, 1)
                for i in range(TT):
                    for k in range(KT):
                        mm = pe.matmul(PS[:, 2, i * SSM_H:(i + 1) * SSM_H], HT[:, k, i * P:(i + 1) * P], wdt[:, k, :],
                                       start=(k == 0), stop=(k == KT - 1))
                mm.then_inc(made, 1)

            @block.vector
            def _(dve):
                dve.memset(XB[:, :, 0:CONV - 1], 0.0)
                dve.wait_ge(made, 1)
                dve.tensor_copy(bias_rows[:], PS[0:ATT_G * KV_H, 1, 0:384]).then_inc(moved1, 1)
                dve.tensor_copy(convT[:], PS[:, 0, 0:(CONV + 1) * XT])
                dve.wait_ge(made, 2)
                dve.tensor_tensor(dt[:], PS[:, 2, 0:TT * SSM_H].rearrange("p (i h) -> p i h", i=TT),
                                  bc(rowc[:, 0, :], 1, TT), ALU.add)

        def move_x(act, bank, j):
            return act.activation(XB[:, 2 * j:2 * j + 2, CONV - 1:], bank, ACT.Copy)

        def move_rows(dst):
            return lambda act, bank, j: act.activation(dst[:, 2 * j:2 * j + 2, :], bank, ACT.Copy)

        def move_q(act, bank, j):
            return act.activation(QT[:, 2 * j:2 * j + 2, :].rearrange("p a (i n) -> p (a i) n", n=P),
                                  bank.rearrange("p a (i n) -> p (a i) n", n=P)[:, :, ::-1], ACT.Copy)

        def move_tokens(dst, c0, func=ACT.Copy):
            return lambda act, bank, j: act.activation(dst[:, :, c0 + j * CW:c0 + (j + 1) * CW], bank, func)

        project([("hy_x", 0, 12, "rows", move_x), ("hy_q", 0, 12, "rows", move_q),
                 ("hy_k", 0, 4, "rows", move_rows(KTT)), ("hy_z", 0, 8, "tokens", move_tokens(ZV, 0, ACT.Silu)),
                 ("hy_v", 0, 4, "tokens", move_tokens(ZV, SSM_IN))])

        BT = sb(inner, "bias_tiles", [P, 2, ATT_G, S])
        SC = sb(inner, "att_scores", [P, 2, ATT_G, S])
        PT = sb(inner, "att_probs_T", [P, 2, S])
        nmax = sb(inner, "neg_max", [P, 4])
        zsum = sb(inner, "prob_sums", [P, 4])
        zinv = sb(inner, "prob_inv", [P, 4])
        FL = sb(inner, "flip_scaled", [P, 2, P])
        flipped = sem("a_flipped")
        bias_in = [pool_dma_sem("bias_in0"), pool_dma_sem("bias_in1")]
        scored, biased, maxed, exped, summed, copied, valued, normed = (
            sem("a_scored"), sem("a_biased"), sem("a_maxed"), sem("a_exped"), sem("a_summed"), sem("a_copied"),
            sem("a_valued"), sem("a_normed"))
        U = KV_H * TT
        with nc.Block() as block:
            @block.gpsimd
            def _(pool):
                for h in range(KV_H):
                    if h >= 2:
                        pool.wait_ge(biased, 2 * (h - 1))
                    pool.dma_start(BT[:, h % 2], bass.AP(tensor=bias_dram.tensor, offset=h * 384,
                                                         ap=[[1, P], [KV_H * 384, ATT_G], [1, S]]))\
                        .then_inc(bias_in[h % 2], 16)

            @block.tensor
            def _(pe):
                def score(u):
                    h, i = u // TT, u % TT
                    r0, n = HD * (h % 2), (i + 1) * P
                    for g in range(ATT_G):
                        b = 2 * (u % 2) + g // 2
                        mm = pe.matmul(PS[:, b, (g % 2) * S:(g % 2) * S + n],
                                       QT[r0:r0 + HD, g * KT + h // 2, i * P:(i + 1) * P],
                                       KTT[r0:r0 + HD, h // 2, 0:n], start=True, stop=True)
                    mm.then_inc(scored, 1)

                def add_groups(u):
                    i = u % TT
                    pe.wait_ge(flipped, u + 1)
                    for st in range(i + 1):
                        for g in range(ATT_G):
                            mm = pe.matmul(PS[:, 4 + u % 2, st * P:(st + 1) * P], SC[:, u % 2, g, st * P:(st + 1) * P],
                                           FL[:, u % 2, :], start=(g == 0), stop=(g == ATT_G - 1))
                    mm.then_inc(summed, 1)

                def value(u):
                    h, i = u // TT, u % TT
                    pe.wait_ge(copied, u + 1)
                    if u >= 2:
                        pe.wait_ge(normed, u - 1)
                    for st in range(i + 1):
                        mm = pe.matmul(PS[:, 6 + u % 2, 0:HD], PT[:, u % 2, st * P:(st + 1) * P],
                                       ZV[:, st, SSM_IN + h * HD:SSM_IN + (h + 1) * HD], start=(st == 0), stop=(st == i))
                    mm.then_inc(valued, 1)

                for u in range(U + 2):
                    if u < U:
                        if u >= 2:
                            pe.wait_ge(biased, u - 1)
                        score(u)
                    if 1 <= u <= U:
                        add_groups(u - 1)
                    if u >= 2:
                        value(u - 2)

            @block.vector
            def _(dve):
                step = stepper(dve, dve_step)
                for u in range(U + 2):
                    if u < U:
                        h, i = u // TT, u % TT
                        n = (i + 1) * P
                        dve.wait_ge(bias_in[h % 2], 16 * (h // 2 + 1))
                        dve.wait_ge(scored, u + 1)
                        if u >= 2:
                            dve.wait_ge(summed, u - 1)
                        ps = PS[:, 2 * (u % 2):2 * (u % 2) + 2, :].rearrange("p a (g s) -> p (a g) s", s=S)
                        dve.scalar_tensor_tensor(out=SC[:, u % 2, :, 0:n], in0=ps[:, 0:ATT_G, 0:n], scalar=HD ** -0.5,
                                                 in1=BT[:, h % 2, :, S - n:], op0=ALU.mult, op1=ALU.add)\
                            .then_inc(biased, 1)
                        dve.wait_ge(biased, u + 1)
                        dve.tensor_reduce(nmax[:, u % 4:u % 4 + 1], SC[:, u % 2, :, 0:n], AX.XY, ALU.max, negate=True)\
                            .then_inc(maxed, 1)
                    if 1 <= u <= U:
                        v = u - 1
                        dve.wait_ge(exped, v + 1)
                        step(dve.reciprocal(zinv[:, v % 4:v % 4 + 1], zsum[:, v % 4:v % 4 + 1]))
                        dve.tensor_scalar(FL[:, v % 2, :], flip[:], zinv[:, v % 4:v % 4 + 1], None,
                                          ALU.mult).then_inc(flipped, 1)
                    if u >= 2:
                        v = u - 2
                        h, i = v // TT, v % TT
                        dve.wait_ge(valued, v + 1)
                        dve.tensor_copy(att[:, i, h * HD:(h + 1) * HD], PS[:, 6 + v % 2, 0:HD]).then_inc(normed, 1)

            @block.scalar
            def _(act):
                for u in range(U + 1):
                    if u < U:
                        n = (u % TT + 1) * P
                        act.wait_ge(maxed, u + 1)
                        act.activation(SC[:, u % 2, :, 0:n], SC[:, u % 2, :, 0:n], ACT.Exp,
                                       bias=nmax[:, u % 4:u % 4 + 1], accum_out=zsum[:, u % 4:u % 4 + 1])\
                            .then_inc(exped, 1)
                    if u >= 1:
                        v = u - 1
                        n = (v % TT + 1) * P
                        act.wait_ge(summed, v + 1)
                        act.activation(PT[:, v % 2, 0:n], PS[:, 4 + v % 2, 0:n], ACT.Copy).then_inc(copied, 1)
        inner.close()

        inner = ExitStack()
        xs = sb(inner, "xs", [P, TT, SSM_IN])
        acc = sb(inner, "conv_acc", [P, 4, S])
        la = sb(inner, "dt_a", [P, TT, SSM_H])
        sp8 = sb(inner, "softplus", [P, 8, TT * SSM_H])
        conv, conved, xturned, xmoved = sem("s_conv"), sem("s_conved"), sem("s_turned"), sem("s_moved")
        e_in, e_out, scan_ps = sem("s_ein"), sem("s_eout"), sem("s_scan")
        with nc.Block() as block:
            @block.vector
            def _(dve):
                step = stepper(dve, dve_step)
                dtf = dt[:].rearrange("p i h -> p (i h)")
                step(dve.tensor_scalar(sp8[:, 0, :], dtf, -1.0, None, ALU.mult))
                dve.tensor_tensor(sp8[:, 1, :], sp8[:, 0, :], dtf, ALU.min).then_inc(e_in, 1)
                dve.wait_ge(e_out, 1)
                step(dve.tensor_scalar(sp8[:, 2, :], sp8[:, 1, :], 2.0, None, ALU.add))
                step(dve.reciprocal(sp8[:, 3, :], sp8[:, 2, :]))
                step(dve.tensor_tensor(sp8[:, 4, :], sp8[:, 1, :], sp8[:, 3, :], ALU.mult))
                step(dve.tensor_tensor(sp8[:, 5, :], sp8[:, 4, :], sp8[:, 4, :], ALU.mult))
                step(dve.tensor_scalar(sp8[:, 6, :], sp8[:, 5, :], 1.0 / 17, None, ALU.mult))
                for k in range(7, 0, -1):
                    step(dve.scalar_tensor_tensor(out=sp8[:, 6, :], in0=sp8[:, 6, :], scalar=1.0 / (2 * k + 1),
                                                  in1=sp8[:, 5, :], op0=ALU.add, op1=ALU.mult))
                step(dve.scalar_tensor_tensor(out=sp8[:, 6, :], in0=sp8[:, 6, :], scalar=1.0, in1=sp8[:, 4, :],
                                              op0=ALU.add, op1=ALU.mult))
                step(dve.tensor_scalar(sp8[:, 7, :], dtf, 0.0, None, ALU.max))
                step(dve.scalar_tensor_tensor(out=dtf, in0=sp8[:, 6, :], scalar=2.0, in1=sp8[:, 7, :],
                                              op0=ALU.mult, op1=ALU.add))
                dve.wait_ge(e_out, 2)
                step(dve.scalar_tensor_tensor(out=la[:], in0=dt[:], scalar=-1.0, in1=bc(rowc[:, 1, :], 1, TT),
                                              op0=ALU.mult, op1=ALU.mult))
                for m in range(XT):
                    a = acc[:, m % 4, :]
                    if m >= 4:
                        dve.wait_ge(conved, m - 3)
                    for j in range(CONV):
                        w = convT[:, j * XT + m:j * XT + m + 1]
                        if j == 0:
                            ins = dve.tensor_scalar(a, XB[:, m, 0:S], w, convT[:, CONV * XT + m:CONV * XT + m + 1],
                                                    ALU.mult, ALU.add)
                        else:
                            ins = dve.scalar_tensor_tensor(out=a, in0=XB[:, m, j:j + S], scalar=w, in1=a,
                                                           op0=ALU.mult, op1=ALU.add)
                        if j < CONV - 1:
                            step(ins)
                        else:
                            ins.then_inc(conv, 1)

            @block.scalar
            def _(act):
                act.wait_ge(e_in, 1)
                act.activation(sp8[:, 1, :], sp8[:, 1, :], ACT.Exp).then_inc(e_out, 1)
                act.activation(rowc[:, 1, :], rowc[:, 1, :], ACT.Exp).then_inc(e_out, 1)
                for m in range(XT):
                    act.wait_ge(conv, m + 1)
                    act.activation(XB[:, m, CONV - 1:], acc[:, m % 4, :], ACT.Silu).then_inc(conved, 1)
                    if m >= 1 and m - 1 < SSM_IN // P:
                        n = m - 1
                        act.wait_ge(xturned, n + 1)
                        act.activation(xs[:, :, n * P:(n + 1) * P],
                                       PS[:, n % 4, 0:S].rearrange("p (i n) -> p i n", i=TT), ACT.Copy)\
                            .then_inc(xmoved, 1)

            @block.tensor
            def _(pe):
                for m in range(SSM_IN // P):
                    pe.wait_ge(conved, m + 1)
                    if m >= 4:
                        pe.wait_ge(xmoved, m - 3)
                    for i in range(TT):
                        mm = pe.transpose(PS[:, m % 4, i * P:(i + 1) * P],
                                          XB[:, m, CONV - 1 + i * P:CONV - 1 + (i + 1) * P], ident[:])
                    mm.then_inc(xturned, 1)

        xdt = sb(inner, "xdt", [P, TT, SSM_IN])
        cbm = sb(inner, "cb_masked", [P, SSM_G, 384])
        cums = sb(inner, "cums", [P, TT, SSM_H])
        dd = sb(inner, "decays", [P, 2, 384])
        W = sb(inner, "ssm_weights", [P, 2, 384])
        cb_ps, cb_mv, cum_ps, bcast, diffed, exped, weighted, vdone, xready, ymoved, yinit = (
            sem("s_cb"), sem("s_cbm"), sem("s_cum"), sem("s_bcast"), sem("s_diff"), sem("s_exp"), sem("s_weight"),
            sem("s_value"), sem("s_xready"), sem("s_ymoved"), sem("s_yinit"))
        GH = SSM_H // SSM_G

        def move_y(dve, g):
            dve.wait_ge(vdone, (g + 1) * GH)
            dve.wait_ge(yinit, TT)
            c = slice(g * GH * HD, (g + 1) * GH * HD)
            b = 4 + 2 * (g % 2)
            dve.tensor_tensor(y[:, :, c], y[:, :, c], PS[:, b:b + 2, :], ALU.add).then_inc(ymoved, 1)

        with nc.Block() as block:
            @block.tensor
            def _(pe):
                pe.matmul(PS[:, 2, 0:SSM_H], pairs[:, 0:P], la[:, 0, :], start=True, stop=True)
                pe.matmul(PS[:, 2, SSM_H:2 * SSM_H], ones[:], la[:, 0, :], start=True, stop=False)
                pe.matmul(PS[:, 2, SSM_H:2 * SSM_H], pairs[:, 0:P], la[:, 1, :], start=False, stop=True)\
                    .then_inc(cum_ps, 1)
                for g in range(SSM_G):
                    B = XB[:, SSM_IN // P + g, CONV - 1:]
                    C = XB[:, SSM_IN // P + SSM_G + g, CONV - 1:]
                    if g >= 2:
                        pe.wait_ge(cb_mv, g - 1)
                    pe.matmul(PS[:, g % 2, 0:S], B[:, 0:P], C, start=True, stop=True)
                    pe.matmul(PS[:, g % 2, S:384], B[:, P:S], C[:, P:S], start=True, stop=True).then_inc(cb_ps, 1)
                pe.wait_ge(cb_mv, SSM_G)
                pe.wait_ge(xready, 1)

                def spread(h):
                    if h >= 2:
                        pe.wait_ge(diffed, h - 1)
                    pe.matmul(PS[:, h % 2, 0:S], la[:, 0, h:h + 1].broadcast_to([P, P]), pairs[:, 0:S],
                              start=True, stop=False)
                    pe.matmul(PS[:, h % 2, P:S], la[:, 1, h:h + 1].broadcast_to([P, P]), pairs[:, 0:P],
                              start=False, stop=True).then_inc(bcast, 1)

                def values(h):
                    g = h // GH
                    if g >= 2 and h % GH == 0:
                        pe.wait_ge(ymoved, g - 1)
                    pe.wait_ge(weighted, h + 1)
                    w = W[:, h % 2, :]
                    c = (h % GH) * HD
                    x = xdt[:, :, h * HD:(h + 1) * HD]
                    o = [PS[:, 4 + 2 * (g % 2) + i, c:c + HD] for i in range(TT)]
                    pe.matmul(o[0], w[:, 0:P], x[:, 0, :], start=True, stop=True)
                    pe.matmul(o[1], w[:, P:2 * P], x[:, 0, :], start=True, stop=False)
                    pe.matmul(o[1], w[:, 2 * P:3 * P], x[:, 1, :], start=False, stop=True).then_inc(vdone, 1)

                for h in range(SSM_H + 1):
                    if h < SSM_H:
                        spread(h)
                    if h >= 1:
                        values(h - 1)

            @block.vector
            def _(dve):
                dve.wait_ge(cum_ps, 1)
                dve.tensor_copy(cums[:], PS[:, 2, 0:2 * SSM_H].rearrange("p (i h) -> p i h", i=TT))
                for g in range(SSM_G):
                    dve.wait_ge(cb_ps, g + 1)
                    dve.tensor_tensor(cbm[:, g, :], PS[:, g % 2, 0:384], pairs[:], ALU.mult).then_inc(cb_mv, 1)
                dve.wait_ge(cb_mv, SSM_G)
                v4 = lambda ap: ap.rearrange("p i (h d) -> p (i h) d", d=HD)
                dve.tensor_tensor(v4(xdt[:]), v4(xs[:]), bc(dt[:].rearrange("p i h -> p (i h)"), 2, HD),
                                  ALU.mult).then_inc(xready, 1)
                for h in range(SSM_H):
                    dve.wait_ge(bcast, h + 1)
                    if h >= 2:
                        dve.wait_ge(weighted, h - 1)
                    dve.tensor_scalar(dd[:, h % 2, 0:S], PS[:, h % 2, 0:S], cums[:, 0, h:h + 1], 0.0,
                                      ALU.subtract, ALU.min)
                    dve.tensor_scalar(dd[:, h % 2, S:384], PS[:, h % 2, P:S], cums[:, 1, h:h + 1], 0.0,
                                      ALU.subtract, ALU.min).then_inc(diffed, 1)
                    if h % GH == 1 and h > GH:
                        move_y(dve, h // GH - 1)
                move_y(dve, SSM_G - 1)

            @block.scalar
            def _(act):
                for h in range(SSM_H):
                    act.wait_ge(diffed, h + 1)
                    act.activation(dd[:, h % 2, :], dd[:, h % 2, :], ACT.Exp).then_inc(exped, 1)

            @block.gpsimd
            def _(pool):
                for i in range(TT):
                    pool.tensor_tensor(y[:, i, :].rearrange("p (h d) -> p h d", d=HD),
                                       xs[:, i, :].rearrange("p (h d) -> p h d", d=HD),
                                       bc(rowc[:, 2, :], 2, HD), ALU.mult).then_inc(yinit, 1)
                for h in range(SSM_H):
                    pool.wait_ge(exped, h + 1)
                    if h >= 2:
                        pool.wait_ge(vdone, h - 1)
                    pool.tensor_tensor(W[:, h % 2, :], dd[:, h % 2, :], cbm[:, h // GH, :], ALU.mult)\
                        .then_inc(weighted, 1)

        squared, meaned, rooted = sem("y_squared"), sem("y_meaned"), sem("y_rooted")
        gated_y = sem("y_gated")
        with nc.Block() as block:
            @block.vector
            def _(dve):
                step = stepper(dve, dve_step)
                for i in range(TT):
                    dve.tensor_tensor(y[:, i, :], y[:, i, :], ZV[:, i, 0:SSM_IN], ALU.mult).then_inc(gated_y, 1)
                dve.wait_ge(squared, TT)
                dve.tensor_scalar(stat[:, 2:4], stat[:, 0:2], 1.0 / SSM_IN, EPS, ALU.mult, ALU.add).then_inc(meaned, 1)
                dve.wait_ge(rooted, 1)
                step(dve.reciprocal(stat[:, 6:8], stat[:, 4:6]))
                for i in range(TT):
                    dve.tensor_scalar(y[:, i, :], y[:, i, :], stat[:, 6 + i:7 + i], None, ALU.mult)

            @block.scalar
            def _(act):
                for i in range(TT):
                    act.wait_ge(gated_y, i + 1)
                    act.activation(xs[:, i, :], y[:, i, :], ACT.Square, accum_out=stat[:, i:i + 1]).then_inc(squared, 1)
                act.wait_ge(meaned, 1)
                act.activation(stat[:, 4:6], stat[:, 2:4], ACT.Sqrt).then_inc(rooted, 1)
        inner.close()
        wide.close()
        YT = sb(scope, "y_T", [P, 3 * KT, S])
        turn_features(y, YT[:, 0:2 * KT, :], 2, ssm_gain)
        turn_features(att, YT[:, 2 * KT:, :], 1, None)
        output_projection("hy_out", YT, 3, gate_a)

    norm_block(mod[:, 3, :], mod[:, 2, :])
    swiglu("ffn0", ffn_source(0), FFN_CHUNKS, gate_b)

    clear_phase_sems()

    modulation(t["c_2"], t["ada_w"][1], t["ada_b"][1], t["norm_mix_g"][1], t["norm_ffn_g"][1])
    norm_block(mod[:, 1, :], mod[:, 0, :])

    with ExitStack() as scope:
        U0 = TAPS - 1
        UP = sb(scope, "conv_in", [P, KT, S + U0])
        CA = sb(scope, "conv_out", [P, KT, S])
        SG = sb(scope, "conv_gate", [P, KT, S])
        SQ = sb(scope, "conv_sq", [P, KT, S])
        raw = sb(scope, "vec_raw", [P, 3, P])
        vec = sb(scope, "vec_T", [P, 3, P])
        b2 = sb(scope, "pw2_bias", [1, D])
        rstd = sb(scope, "ln_rstd", [P, 3, S])
        meanw = sb(scope, "mean_weights", [P, P])
        small, made, taken = pool_dma_sem("c_small"), sem("c_made"), sem("c_taken")
        HALF = TAPS * KT // 2
        with nc.Block() as block:
            @block.gpsimd
            def _(pool):
                taps = t["cv_w_dw"][0].rearrange("j (m p) -> (j m) p", p=P)
                loads = [(raw[0:HALF, 0, :], taps[0:HALF, :]), (raw[0:HALF, 1, :], taps[HALF:, :]),
                         (raw[0:16, 2, :], t["cv_b_pw1"][0].rearrange("(m p) -> m p", p=P)),
                         (raw[16:24, 2, :], t["cv_b_dw"][0].rearrange("(m p) -> m p", p=P)),
                         (raw[24:32, 2, :], t["cv_ln_g"][0].rearrange("(m p) -> m p", p=P)),
                         (raw[32:40, 2, :], t["cv_ln_b"][0].rearrange("(m p) -> m p", p=P)),
                         (b2[:], t["cv_b_pw2"][0].rearrange("(a n) -> a n", a=1))]
                for dst, src in loads:
                    pool.dma_start(dst, src).then_inc(small, 16)
                pool.wait_ge(small, 16 * len(loads))

            @block.tensor
            def _(pe):
                pe.wait_ge(small, 16 * 7)
                for j, n in enumerate((HALF, HALF, 40)):
                    mm = pe.transpose(PS[:, j, 0:n], raw[0:n, j, :], ident[0:n, 0:n])
                mm.then_inc(made, 1)

            @block.vector
            def _(dve):
                dve.memset(UP[:, :, 0:U0], 0.0)
                dve.memset(meanw[:], 1.0 / D)
                dve.wait_ge(made, 1)
                for j, n in enumerate((HALF, HALF, 40)):
                    dve.tensor_copy(vec[:, j, 0:n], PS[:, j, 0:n])

        vb = vec[:, 2, :]
        base = segs["pw1"].base
        moved, glu = sem("g_moved"), sem("g_glu")
        with nc.Block() as block:
            @block.sync
            def _(sp):
                send_until(sp, base + 8)

            @block.tensor
            def _(pe):
                for q in range(8):
                    arrive(pe, base + q)
                    if q >= 4:
                        pe.wait_ge(moved, 2 * (q - 3))
                    rows_chunk(pe, base + q, q % 4).then_inc(used, 1)

            @block.scalar
            def _(act):
                for q in range(8):
                    act.wait_ge(used, base + q + 1)
                    c, half = q // 2, q % 2
                    for m in range(2):
                        f = 2 * c + m
                        bank = PS[:, q % 4, m * S:(m + 1) * S]
                        if half:
                            act.activation(SG[:, f, :], bank, ACT.Sigmoid, bias=vb[:, 8 + f:9 + f]).then_inc(moved, 1)
                        else:
                            act.activation(CA[:, f, :], bank, ACT.Identity, bias=vb[:, f:f + 1]).then_inc(moved, 1)

            @block.vector
            def _(dve):
                for c in range(4):
                    dve.wait_ge(moved, 4 * (c + 1))
                    f = slice(2 * c, 2 * c + 2)
                    dve.tensor_tensor(UP[:, f, U0:], CA[:, f, :], SG[:, f, :], ALU.mult)

        tap, means, centred, sqd, vars_, rooted, rs = (sem("d_tap"), sem("d_mean"), sem("d_centred"), sem("d_sq"),
                                                       sem("d_var"), sem("d_rooted"), sem("d_rs"))
        var_ready = sem("d_vready")
        with nc.Block() as block:
            @block.vector
            def _(dve):
                step = stepper(dve, dve_step)
                for j in range(TAPS):
                    for m in range(KT):
                        c = j * KT + m
                        w = vec[:, c // HALF, c % HALF:c % HALF + 1]
                        if j == 0:
                            ins = dve.tensor_scalar(CA[:, m, :], UP[:, m, 0:S], w, vb[:, 16 + m:17 + m], ALU.mult, ALU.add)
                        else:
                            dve.wait_ge(tap, c - KT + 1)
                            ins = dve.scalar_tensor_tensor(out=CA[:, m, :], in0=UP[:, m, j:j + S], scalar=w,
                                                           in1=CA[:, m, :], op0=ALU.mult, op1=ALU.add)
                        ins.then_inc(tap, 1)
                dve.wait_ge(means, 1)
                dve.tensor_tensor(CA[:], CA[:], bc(PS[:, 0, 0:S], 1, KT), ALU.subtract).then_inc(centred, 1)
                dve.wait_ge(vars_, 1)
                dve.tensor_scalar(rstd[:, 0, :], PS[:, 1, 0:S], EPS, None, ALU.add).then_inc(var_ready, 1)
                dve.wait_ge(rooted, 1)
                step(dve.reciprocal(rstd[:, 2, :], rstd[:, 1, :]))
                dve.tensor_tensor(CA[:], CA[:], bc(rstd[:, 2, :], 1, KT), ALU.mult).then_inc(rs, 1)

            @block.tensor
            def _(pe):
                pe.wait_ge(tap, TAPS * KT)
                for m in range(KT):
                    mm = pe.matmul(PS[:, 0, 0:S], meanw[:], CA[:, m, :], start=(m == 0), stop=(m == KT - 1))
                mm.then_inc(means, 1)
                pe.wait_ge(sqd, 1)
                for m in range(KT):
                    mm = pe.matmul(PS[:, 1, 0:S], meanw[:], SQ[:, m, :], start=(m == 0), stop=(m == KT - 1))
                mm.then_inc(vars_, 1)

            @block.scalar
            def _(act):
                act.wait_ge(centred, 1)
                act.activation(SQ[:], CA[:], ACT.Square).then_inc(sqd, 1)
                act.wait_ge(var_ready, 1)
                act.activation(rstd[:, 1, :], rstd[:, 0, :], ACT.Sqrt).then_inc(rooted, 1)
                act.wait_ge(rs, 1)
                for m in range(KT):
                    act.activation(SQ[:, m, :], CA[:, m, :], ACT.Silu, scale=vb[:, 24 + m:25 + m],
                                   bias=vb[:, 32 + m:33 + m])
        output_projection("pw2", SQ, 1, gate_a, bias=b2)

    norm_block(mod[:, 3, :], mod[:, 2, :])
    swiglu("ffn1", ffn_source(1), FFN_CHUNKS, gate_b)

    plain_norm(t["final_norm_g"], out)


def _constants(np):
    p = np.arange(P)
    tri = (p[:, None] <= p[None, :]).astype(np.float32)
    pairs = np.concatenate([tri, np.ones((P, P), np.float32), tri], axis=1)
    levels = np.zeros((P, LEVELS, P), np.float32)
    levels[:, 0, :] = np.eye(P)
    for l in range(1, LEVELS):
        b = 1 << (l - 1)
        block, half = p // (2 * b), (p // b) % 2
        levels[:, l, :] = ((block[:, None] == block[None, :]) & (half[:, None] == 0) & (half[None, :] == 1))
    log_gamma = np.log1p(-np.exp2(-5.0 - np.arange(RET_H)))
    rel = np.concatenate([np.arange(S)[None, :] - p[:, None], p[None, :] - p[:, None]], axis=1)
    decay = np.where(rel[:, None, :] >= 0, np.exp(log_gamma[None, :, None] * np.maximum(rel, 0)[:, None, :]), 0.0)
    freq = np.float32(10000.0) ** (-np.arange(0, HD, 2, dtype=np.float32) / np.float32(HD))
    dist = 255 - np.arange(384)
    exact = BUCKETS // 2
    n = np.maximum(dist, 1).astype(np.float64)
    large = np.minimum((exact + np.log(n / exact) / np.log(2048 / exact) * (BUCKETS - exact)).astype(np.int64), BUCKETS - 1)
    bucket = np.where(dist < exact, np.maximum(dist, 0), large)
    onehot = (np.arange(BUCKETS)[:, None] == bucket[None, :]).astype(np.float32)
    gmask = np.stack([np.where((dist >= 0) & (dist % dil == 0) & (dist <= w), 0.0, NEG)
                      for w, dil in ((128, 1), (512, 4), (2048, 16))])
    gsel = np.repeat(np.eye(ATT_G), KV_H, axis=1)
    order = np.tile(16.0 - np.arange(16), (P, 1))
    out = {"ident": np.eye(P), "pairs": pairs, "levels": levels, "decay": decay, "freq": np.tile(freq, (P, 1)),
           "onehot": onehot, "gmask": gmask, "gsel": gsel, "order": order, "flip": np.eye(P)[::-1],
           "slots": np.tile(np.arange(SLOTS), (P, 1))}
    return {f"const_{k}": np.ascontiguousarray(v, dtype=np.float32) for k, v in out.items()}


_FIRST = ["x", "c", "positions", "w_ada", "b_ada", "norm_mix", "norm_ffn", "w_in", "ret_norm", "hgrn_norm",
          "hgrn_lb_logits", "gla_wa2", "gla_ba", "gla_norm", "w_out", "router_group_w", "router_group_b",
          "router_expert_w", "router_expert_b", "expert_w_gate", "expert_w_up", "expert_w_down",
          "norm_final"]
_SECOND = ["c_2", "ada_w_2", "ada_b_2", "norm_mix_g_2", "norm_ffn_g_2", "hy_w_in_2", "hy_conv_w_2", "hy_conv_b_2",
           "hy_dt_bias_2", "hy_a_log_2", "hy_d_skip_2", "hy_ssm_norm_g_2", "hy_w_out_2", "rel_table_2", "cv_w_pw1_2",
           "cv_b_pw1_2", "cv_w_dw_2", "cv_b_dw_2", "cv_ln_g_2", "cv_ln_b_2", "cv_w_pw2_2", "cv_b_pw2_2",
           "ffn_w_gate_2", "ffn_w_up_2", "ffn_w_down_2", "final_norm_g_2"]


def kernel(**inputs):
    import numpy as np
    import concourse.bacc as bacc
    from concourse.bass_utils import run_bass_kernel_spmd

    nc = bacc.Bacc("TRN2", target_bir_lowering=False, num_devices=1)
    arrays, t = {}, {}
    sources = {n: inputs[n] for n in _FIRST + _SECOND}
    sources.update(_constants(np))
    for name, value in sources.items():
        a = np.ascontiguousarray(value)
        arrays[f"in_{name}"] = a
        ap = nc.dram_tensor(f"in_{name}", a.shape, mybir.dt.from_np(a.dtype), kind="ExternalInput").ap()
        t[name if name == "c_2" or not name.endswith("_2") else name[:-2]] = ap
    out = nc.dram_tensor("out", (1, S, D), F32, kind="ExternalOutput").ap()
    build(nc, t, out)
    r = run_bass_kernel_spmd(nc, [arrays], core_ids=[0])
    return r.results[0]["out"]
```

```python
from contextlib import ExitStack

import concourse.bass as bass
from concourse import mybir

F32 = mybir.dt.float32
I32 = mybir.dt.int32
ALU = mybir.AluOpType
ACT = mybir.ActivationFunctionType
AX = mybir.AxisListType
ds = bass.ds

P = 128
D = 1024
S = 256
TT = S // P
KT = D // P
HD = 64
CW = 256
RING = 6
EPS = 1e-6
F_MIN = 1e-30

RET_W, HGRN_W, GLA_W = 384, 384, 256
RET_H, HGRN_H, GLA_H, GLA_DK = 6, 6, 4, 32
HEADS = RET_H + HGRN_H + GLA_H
TAU = 16.0
RANK = 16
GROUPS, PER_GROUP, EXPERTS, SLOTS = 4, 8, 32, 32
LEVELS = 8

SSM_IN, SSM_H, SSM_G, STATE, CONV = 2048, 32, 4, 128, 4
XBC = SSM_IN + 2 * SSM_G * STATE
XT = XBC // P
ATT_G, KV_H, BUCKETS = 3, 16, 32
TAPS = 31
FFN_CHUNKS = 2816 // CW
NEG = -1e30


class Marks:

    def __init__(self, sem):
        self.sem, self.n = sem, 0


def build(nc, t, out):
    top = ExitStack()
    with top:
        _program(nc, t, out, top)


def _program(nc, t, out, top):
    serial = [0]

    phase_sems = []

    def lasting_sem(name):
        return top.enter_context(nc.semaphore(name))

    def pool_dma_sem(name):
        serial[0] += 1
        return top.enter_context(nc.semaphore(f"{name}_{serial[0]}"))

    def sem(name):
        serial[0] += 1
        scope = ExitStack()
        s = scope.enter_context(nc.semaphore(f"{name}_{serial[0]}"))
        phase_sems.append((scope, s))
        return s

    def clear_phase_sems():
        with nc.Block() as block:
            @block.gpsimd
            def _(pool):
                for _, s in phase_sems:
                    pool.sem_clear(s)
        for scope, _ in reversed(phase_sems):
            scope.close()
        phase_sems.clear()

    def sb(scope, name, shape, dt=F32):
        serial[0] += 1
        return scope.enter_context(nc.sbuf_tensor(f"{name}_{serial[0]}", shape, dt))

    def bc(ap, axis, n):
        v = ap.unsqueeze(axis)
        shape = list(v.shape)
        shape[axis] = n
        return v.broadcast_to(shape)

    ring = sb(top, "ring", [P, RING, 8 * CW])
    X = sb(top, "X", [P, TT, D])
    HT = sb(top, "HT", [P, KT, S])
    ident = sb(top, "ident", [P, P])
    ones = sb(top, "ones", [P, P])
    pairs = sb(top, "pairs", [P, 384])
    mod = sb(top, "mod", [P, 4, KT])
    gate_a = sb(top, "gate_a", [P, D])
    gate_b = sb(top, "gate_b", [P, D])
    mod_next = sb(top, "mod_next", [P, 2, KT])
    stat = sb(top, "stat", [P, 16])
    PS = top.enter_context(nc.psum_tensor("PS", [P, 8, 512], F32))

    landed = [lasting_sem(f"landed{i}") for i in range(RING)]
    used = lasting_sem("used")
    dve_step = Marks(lasting_sem("dve_step"))
    pool_step = Marks(lasting_sem("pool_step"))

    def stepper(eng, marks):
        def step(ins):
            marks.n += 1
            ins.then_inc(marks.sem, 1)
            eng.wait_ge(marks.sem, marks.n)
        return step

    def pk(w, c0):
        return w.rearrange("(p k) n -> p k n", k=KT)[:, :, ds(c0, CW)]

    def kp(w, c0):
        return w.rearrange("(k p) n -> p k n", p=P)[:, :, ds(c0, CW)]

    hy_groups = [t["hy_w_in"][0]]
    wi, hi = t["w_in"][0], hy_groups[0]
    HY_Z, HY_X, HY_DT, HY_Q = 0, SSM_IN, SSM_IN + XBC, SSM_IN + XBC + SSM_H
    HY_K = HY_Q + ATT_G * KV_H * HD
    HY_V = HY_K + KV_H * HD

    class Segment:
        def __init__(self, name, base, n):
            self.name, self.base, self.n = name, base, n

    stream = []
    segs = {}

    def segment(name, sources):
        segs[name] = Segment(name, len(stream), len(sources))
        stream.extend(sources)

    def expert_order(n):
        order = [("g", 0), ("u", 0)]
        for e in range(1, n):
            order += [("g", e), ("u", e), ("d", e - 1)]
        return order + [("d", n - 1)]

    QUAD = 4
    QUADS = EXPERTS // QUAD
    QUAD_ORDER = [(kind, e) for e in range(QUAD) for kind in "gu"] + [("d", e) for e in range(QUAD)]
    QC = len(QUAD_ORDER)

    def moe_source(kind, e):
        if kind == "d":
            return t["expert_w_down"][0][ds(e, 1)].rearrange("a (f p) n -> p (a f) n", p=P)
        w = t["expert_w_gate" if kind == "g" else "expert_w_up"][0]
        return w[ds(e, 1)].rearrange("a (p k) n -> p (a k) n", k=KT)

    def ffn_source(layer):
        def source(kind, e):
            if kind == "d":
                return t["ffn_w_down"][layer][ds(e * CW, CW), :].rearrange("(f p) n -> p f n", p=P)
            return pk(t["ffn_w_gate" if kind == "g" else "ffn_w_up"][layer], e * CW)
        return source

    segment("w_in", [pk(wi, c * CW) for c in range(15)])
    segment("w_out", [pk(t["w_out"][0], c * CW) for c in range(4)])
    segment("moe", [moe_source(k, QUAD * q + e) for q in range(QUADS) for k, e in QUAD_ORDER])
    segment("hy_x", [pk(hi, HY_X + c * CW) for c in range(12)])
    segment("hy_q", [pk(hi, HY_Q + c * CW) for c in range(12)])
    segment("hy_k", [pk(hi, HY_K + c * CW) for c in range(4)])
    segment("hy_z", [pk(hi, HY_Z + c * CW) for c in range(8)])
    segment("hy_v", [pk(hi, HY_V + c * CW) for c in range(4)])
    hy_out = t["hy_w_out"][0]
    segment("hy_out", [hy_out[g * D:(g + 1) * D, :].rearrange("(p k) n -> p k n", k=KT)[:, :, c * CW:(c + 1) * CW]
                       for c in range(4) for g in range(3)])
    segment("ffn0", [ffn_source(0)(k, e) for k, e in expert_order(FFN_CHUNKS)])
    segment("pw1", [pk(t["cv_w_pw1"][0], h * D + c * CW) for c in range(4) for h in range(2)])
    segment("pw2", [kp(t["cv_w_pw2"][0], c * CW) for c in range(4)])
    segment("ffn1", [ffn_source(1)(k, e) for k, e in expert_order(FFN_CHUNKS)])

    sent = [0]

    def send(sp, source, n):
        if n >= RING:
            sp.wait_ge(used, n - RING + 1)
        shape = source.shape
        dst = ring[:, n % RING, :].rearrange("p (a b) -> p a b", b=shape[2])
        sp.dma_start(dst, source).then_inc(landed[n % RING], 16)

    def send_until(sp, end):
        stop = min(end + RING, len(stream))
        while sent[0] < stop:
            send(sp, stream[sent[0]], sent[0])
            sent[0] += 1

    def arrive(pe, n, landed=landed):
        pe.wait_ge(landed[n % RING], 16 * (n // RING + 1))

    def w_slot(n, b=CW, ring=ring):
        return ring[:, n % RING, :].rearrange("p (a b) -> p a b", b=b)

    tok = lambda ap: ap.rearrange("(t p) n -> p t n", p=P)

    load0 = sem("load0")
    with nc.Block() as block:
        @block.sync
        def _(sp):
            sp.dma_start(X[:], tok(t["x"][0])).then_inc(load0, 16)
            sp.dma_start(ident[:], t["const_ident"]).then_inc(load0, 16)
            sp.dma_start(pairs[:], t["const_pairs"]).then_inc(load0, 16)
            sp.wait_ge(load0, 48)

        @block.vector
        def _(dve):
            dve.memset(ones[:], 1.0)

    class Ada:

        def __init__(self, scope, c_in, w, b, gain_mix, gain_ffn, groups, per_step):
            self.groups, self.per_step = groups, per_step
            self.steps = KT * len(groups) // per_step
            self.rows_per_step = per_step // len(groups)
            self.wv = w.rearrange("(p k) (g n) -> p k g n", k=KT, n=2 * D)
            self.acc = sb(scope, "ada_acc", [P, len(groups), 2 * D])
            self.cv = sb(scope, "ada_c", [P, KT])
            self.gains = sb(scope, "ada_gain", [P, 2, KT])
            self.arrived = [pool_dma_sem(f"ada_arrived{j}") for j in range(per_step)]
            self.summed = sem("ada_summed")
            small, biased, zeroed = sem("ada_small"), sem("ada_biased"), sem("ada_zeroed")
            with nc.Block() as block:
                @block.sync
                def _(sp):
                    sp.dma_start(self.cv[:], c_in[0].rearrange("(p k) -> p k", k=KT)).then_inc(small, 16)
                    sp.dma_start(self.gains[:, 0, :], gain_mix.rearrange("(p k) -> p k", k=KT)).then_inc(small, 16)
                    sp.dma_start(self.gains[:, 1, :], gain_ffn.rearrange("(p k) -> p k", k=KT)).then_inc(small, 16)
                    sp.wait_ge(zeroed, 1)
                    for j, g in enumerate(groups):
                        sp.dma_start(self.acc[0:1, j, :],
                                     b[g * 2 * D:(g + 1) * 2 * D].rearrange("(a n) -> a n", a=1)).then_inc(biased, 16)
                    sp.wait_ge(biased, 16 * len(groups))

                @block.gpsimd
                def _(pool):
                    pool.memset(self.acc[:], 0.0).then_inc(zeroed, 1)

                @block.scalar
                def _(act):
                    act.wait_ge(small, 48)
                    act.activation(self.cv[:], self.cv[:], ACT.Silu)

        def fetch(self, pool, stage, i, first=False):
            for j in range(self.per_step):
                k, g = i * self.rows_per_step + j // len(self.groups), self.groups[j % len(self.groups)]
                if not first:
                    pool.wait_ge(self.summed, i * self.per_step + (j + 1 - self.per_step))
                pool.dma_start(stage[:, j:j + 1, :], self.wv[:, ds(k, 1), g, :]).then_inc(self.arrived[j], 16)

        def fetch_all(self, pool, stage):
            self.fetch(pool, stage, 0, True)
            with pool.Fori(1, self.steps) as i:
                self.fetch(pool, stage, i)

        def add(self, dve, stage, i, j0, j1, first=False):
            G = len(self.groups)
            for j in range(j0, j1):
                dve.wait_ge(self.arrived[j], i * 16 + 16)
                if not (first and j < G):
                    dve.wait_ge(self.summed, i * self.per_step + (j + 1 - G))
                dve.scalar_tensor_tensor(out=self.acc[:, j % G, :], in0=stage[:, j, :],
                                         scalar=self.cv[:, ds(i * self.rows_per_step + j // G, 1)],
                                         in1=self.acc[:, j % G, :], op0=ALU.mult, op1=ALU.add).then_inc(self.summed, 1)

        def add_all(self, dve, stage):
            self.add(dve, stage, 0, 0, self.per_step, True)
            with dve.Fori(1, self.steps) as i:
                self.add(dve, stage, i, 0, self.per_step)

        def finish(self, mod=mod):
            part = {2 * g + h: self.acc[:, j, h * D:(h + 1) * D] for j, g in enumerate(self.groups) for h in range(2)}
            columns = [(n, seg) for n, seg in enumerate((0, 1, 3, 4)) if seg in part]
            gates = [(n, seg) for n, seg in enumerate((2, 5)) if seg in part]
            cols, rows = sem("ada_cols"), sem("ada_rows")
            with nc.Block() as block:
                @block.tensor
                def _(pe):
                    for n, seg in columns:
                        v = part[seg].rearrange("p (m k) -> p k m", k=KT)
                        for k in range(KT):
                            mm = pe.matmul(PS[:, 0, n * KT + k:n * KT + k + 1], v[:, k, :], ones[:, 0:1],
                                           start=True, stop=True)
                    mm.then_inc(cols, 1)
                    for n, seg in gates:
                        for h in range(2):
                            pe.matmul(PS[:, 1 + 2 * n + h, :], ones[:], part[seg][:, h * 512:(h + 1) * 512],
                                      start=True, stop=True).then_inc(rows, 1)

                @block.vector
                def _(dve):
                    dve.wait_ge(cols, 1)
                    for n, seg in columns:
                        c = PS[:, 0, n * KT:(n + 1) * KT]
                        if n % 2:
                            dve.scalar_tensor_tensor(out=mod[:, n, :], in0=c, scalar=1.0, in1=self.gains[:, n // 2, :],
                                                     op0=ALU.add, op1=ALU.mult)
                        else:
                            dve.tensor_copy(mod[:, n, :], c)
                    for at, (n, seg) in enumerate(gates):
                        dve.wait_ge(rows, 2 * at + 2)
                        dve.tensor_copy((gate_a, gate_b)[n][:], PS[:, 1 + 2 * n:3 + 2 * n, :])

    def norm_block(scale, shift, xn=None):
        squared, meaned, rooted, scaled, turned, evacuated = (sem("n_squared"), sem("n_meaned"), sem("n_rooted"),
                                                              sem("n_scaled"), sem("n_turned"), sem("n_evac"))
        with ExitStack() as scope:
            xn = sb(scope, "xn", [P, TT, D]) if xn is None else xn
            with nc.Block() as block:
                @block.scalar
                def _(act):
                    for i in range(TT):
                        act.activation(xn[:, i, :], X[:, i, :], ACT.Square,
                                       accum_out=stat[:, i:i + 1]).then_inc(squared, 1)
                    act.wait_ge(meaned, 1)
                    act.activation(stat[:, 4:6], stat[:, 2:4], ACT.Sqrt).then_inc(rooted, 1)

                @block.vector
                def _(dve):
                    step = stepper(dve, dve_step)
                    dve.wait_ge(squared, TT)
                    dve.tensor_scalar(stat[:, 2:4], stat[:, 0:2], 1.0 / D, EPS, ALU.mult, ALU.add).then_inc(meaned, 1)
                    dve.wait_ge(rooted, 1)
                    step(dve.reciprocal(stat[:, 6:8], stat[:, 4:6]))
                    for i in range(TT):
                        dve.tensor_scalar(xn[:, i, :], X[:, i, :], stat[:, 6 + i:7 + i], None,
                                          ALU.mult).then_inc(scaled, 1)
                    for k in range(KT):
                        dve.wait_ge(turned, k + 1)
                        dve.tensor_scalar(HT[:, k, :], PS[:, k % 4, 0:S], scale[:, k:k + 1], shift[:, k:k + 1],
                                          ALU.mult, ALU.add).then_inc(evacuated, 1)

                @block.tensor
                def _(pe):
                    pe.wait_ge(scaled, TT)
                    for k in range(KT):
                        if k >= 4:
                            pe.wait_ge(evacuated, k - 3)
                        for i in range(TT):
                            mm = pe.transpose(PS[:, k % 4, i * P:(i + 1) * P],
                                              xn[:, i, :].rearrange("p (m k) -> p k m", k=KT)[:, k, :], ident[:])
                        mm.then_inc(turned, 1)

    def plain_norm(gain, result):
        with ExitStack() as scope:
            fg = sb(scope, "final_gain", [P, D])
            yo = sb(scope, "result", [P, TT, D])
            fin, squared, meaned, rooted, done, outs = (sem("f_gain"), sem("f_squared"), sem("f_meaned"), sem("f_rooted"),
                                                        sem("f_done"), sem("f_out"))
            with nc.Block() as block:
                @block.sync
                def _(sp):
                    sp.dma_start(fg[:], gain.partition_broadcast(P)).then_inc(fin, 16)
                    if result is not None:
                        for i in range(TT):
                            sp.wait_ge(done, i + 1)
                            sp.dma_start(result[0, i * P:(i + 1) * P, :], X[:, i, :]).then_inc(outs, 16)
                        sp.wait_ge(outs, 16 * TT)

                @block.scalar
                def _(act):
                    for i in range(TT):
                        act.activation(yo[:, i, :], X[:, i, :], ACT.Square, accum_out=stat[:, i:i + 1]).then_inc(squared, 1)
                    act.wait_ge(meaned, 1)
                    act.activation(stat[:, 4:6], stat[:, 2:4], ACT.Sqrt).then_inc(rooted, 1)

                @block.vector
                def _(dve):
                    step = stepper(dve, dve_step)
                    dve.wait_ge(squared, TT)
                    dve.tensor_scalar(stat[:, 2:4], stat[:, 0:2], 1.0 / D, EPS, ALU.mult, ALU.add).then_inc(meaned, 1)
                    dve.wait_ge(rooted, 1)
                    step(dve.reciprocal(stat[:, 6:8], stat[:, 4:6]))
                    dve.wait_ge(fin, 16)
                    for i in range(TT):
                        dve.scalar_tensor_tensor(out=X[:, i, :], in0=X[:, i, :], scalar=stat[:, 6 + i:7 + i], in1=fg[:],
                                                 op0=ALU.mult, op1=ALU.mult).then_inc(done, 1)

    def rows_chunk(pe, n, bank, src=None, ring=ring):
        src = HT if src is None else src
        w = w_slot(n, ring=ring)
        for m in range(2):
            for k in range(KT):
                mm = pe.matmul(PS[:, bank, m * S:(m + 1) * S], w[:, k, m * P:(m + 1) * P], src[:, k, :],
                               start=(k == 0), stop=(k == KT - 1))
        return mm

    def tokens_chunk(pe, n, bank, src=None, k0=0):
        src = HT if src is None else src
        w = w_slot(n)
        for i in range(TT):
            for k in range(KT):
                mm = pe.matmul(PS[:, bank, i * CW:(i + 1) * CW], src[:, k0 + k, i * P:(i + 1) * P], w[:, k, :],
                               start=(k == 0), stop=(k == KT - 1))
        return mm

    def project(parts, ada=None, stage=None):
        moved = sem("p_moved")
        todo = [(segs[s].base + c0 + j, kind, ev, j) for s, c0, n, kind, ev in parts for j in range(n)]
        with nc.Block() as block:
            @block.sync
            def _(sp):
                send_until(sp, todo[-1][0] + 1)

            @block.tensor
            def _(pe):
                for q, (n, kind, _, _) in enumerate(todo):
                    arrive(pe, n)
                    if q >= 4:
                        pe.wait_ge(moved, q - 3)
                    mm = (rows_chunk if kind == "rows" else tokens_chunk)(pe, n, q % 4)
                    mm.then_inc(used, 1)

            @block.scalar
            def _(act):
                for q, (n, kind, ev, j) in enumerate(todo):
                    act.wait_ge(used, n + 1)
                    ev(act, PS[:, q % 4, :].rearrange("p (a b) -> p a b", a=2), j).then_inc(moved, 1)

            if ada is not None:
                @block.gpsimd
                def _(pool):
                    ada.fetch_all(pool, stage)

                @block.vector
                def _(dve):
                    ada.add_all(dve, stage)

    def swiglu(name, source, count, gate, ada=None):
        base = segs[name].base
        hid_ready, silu_ready = sem("e_hid"), sem("e_silu")
        pairs_n = (count - 2) // 2
        order = expert_order(count)
        B0 = base + 5
        with ExitStack() as scope:
            silu = sb(scope, "silu", [P, 2, 2, S])
            hid = sb(scope, "hid", [P, 2, 2, S])
            if ada is not None:
                stage = sb(scope, "ada_stage", [P, ada.per_step, 2 * D])
                assert ada.steps == pairs_n
            with nc.Block() as block:
                def bank(kind, par):
                    return 2 * par + (kind == "u")

                @block.sync
                def _(sp):
                    assert sent[0] == base + RING
                    with sp.Fori(0, pairs_n - 1) as i:
                        for j in range(6):
                            idx = RING + j
                            kind, e = order[idx]
                            sp.wait_ge(used, base + idx - RING + 1 + i * 6)
                            src = source(kind, e + i * 2)
                            n = base + idx
                            dst = ring[:, n % RING, :].rearrange("p (a b) -> p a b", b=src.shape[2])
                            sp.dma_start(dst, src).then_inc(landed[n % RING], 16)
                    sent[0] += 6 * (pairs_n - 1)
                    send_until(sp, base + len(order))

                @block.tensor
                def _(pe):
                    def up_gate(kind, n, par):
                        rows_chunk(pe, n, bank(kind, par)).then_inc(used, 1)

                    def down(n, par, first, last):
                        w = w_slot(n, D)
                        for f in range(2):
                            for i in range(TT):
                                for h in range(2):
                                    mm = pe.matmul(PS[:, 4 + 2 * i + h, :], hid[:, par, f, i * P:(i + 1) * P],
                                                   w[:, f, h * 512:(h + 1) * 512], start=first and f == 0,
                                                   stop=last and f == 1)
                        mm.then_inc(used, 1)

                    for idx in range(5):
                        kind, e = order[idx]
                        arrive(pe, base + idx)
                        if kind == "d":
                            pe.wait_ge(hid_ready, e + 1)
                            down(base + idx, e % 2, True, False)
                        else:
                            up_gate(kind, base + idx, e % 2)
                    with pe.Fori(0, pairs_n) as i:
                        for j in range(6):
                            kind, e = order[5 + j]
                            n = B0 + j
                            pe.wait_ge(landed[n % RING], i * 16 + 16 * (n // RING + 1))
                            if kind == "d":
                                pe.wait_ge(hid_ready, i * 2 + e + 1)
                                down(n, e % 2, False, False)
                            else:
                                up_gate(kind, n, e % 2)
                    for idx in range(5 + 6 * pairs_n, len(order)):
                        kind, e = order[idx]
                        arrive(pe, base + idx)
                        if kind == "d":
                            pe.wait_ge(hid_ready, e + 1)
                            down(base + idx, e % 2, False, e == count - 1)
                        else:
                            up_gate(kind, base + idx, e % 2)

                def up_done(e):
                    return base + (2 if e == 0 else 3 * e + 1)

                @block.scalar
                def _(act):
                    def one(par, gate_done):
                        act.wait_ge(used, gate_done)
                        act.activation(silu[:, par], PS[:, 2 * par, :].rearrange("p (a b) -> p a b", a=2),
                                       ACT.Silu).then_inc(silu_ready, 1)
                    one(0, up_done(0) - 1)
                    one(1, up_done(1) - 1)
                    with act.Fori(0, pairs_n) as i:
                        one(0, i * 6 + up_done(2) - 1)
                        one(1, i * 6 + up_done(3) - 1)
                    for e in range(2 + 2 * pairs_n, count):
                        one(e % 2, up_done(e) - 1)

                if ada is not None:
                    @block.gpsimd
                    def _(pool):
                        ada.fetch_all(pool, stage)

                @block.vector
                def _(dve):
                    def one(par, up, nth):
                        dve.wait_ge(used, up)
                        u = PS[:, 2 * par + 1, :].rearrange("p (a b) -> p a b", a=2)
                        dve.wait_ge(silu_ready, nth)
                        dve.tensor_tensor(hid[:, par], u, silu[:, par], ALU.mult).then_inc(hid_ready, 1)

                    def pair(i, first=False):
                        for par in range(2):
                            one(par, i * 6 + up_done(2 + par), i * 2 + 3 + par)
                            if ada is not None:
                                half = ada.per_step // 2
                                ada.add(dve, stage, i, par * half, (par + 1) * half, first)

                    one(0, up_done(0), 1)
                    one(1, up_done(1), 2)
                    pair(0, True)
                    with dve.Fori(1, pairs_n) as i:
                        pair(i)
                    for e in range(2 + 2 * pairs_n, count):
                        one(e % 2, up_done(e), e + 1)
                    dve.wait_ge(used, base + len(order))
                    step = stepper(dve, dve_step)
                    add_gated(dve, step, PS[:, 4:8, :].rearrange("p (i h) n -> p i (h n)", i=TT), gate, scope)

    def routed_experts(pick, put, xn, sums):
        base = segs["moe"].base
        assert base + QC * QUADS == segs["hy_x"].base and QC % RING == 0
        scale, shift = mod[:, 3, :], mod[:, 2, :]
        with ExitStack() as scope:
            hs = sb(scope, "slot_rows", [P, KT, QUAD * SLOTS])
            silu = sb(scope, "silu", [P, CW])
            hid = sb(scope, "hid", [P, CW])
            hidT = sb(scope, "hid_T", [P, 2, P])
            ys = sb(scope, "slot_out", [P, D])
            put_now = sb(scope, "put_now", [P, S])
            gathered, hs_ready, silu_ready, hid_ready, turned, hidT_ready = (
                sem("m_gathered"), sem("m_hs"), sem("m_silu"), sem("m_hid"), sem("m_turned"), sem("m_hidT"))
            scattered, added, y_moved, staged = sem("m_scattered"), sem("m_added"), sem("m_y"), sem("m_staged")
            done_after = {item: pos + 1 for pos, item in enumerate(QUAD_ORDER)}

            def over_quads(eng, body):
                body(0, True, False)
                with eng.Fori(1, QUADS - 1) as q:
                    body(q, False, False)
                body(QUADS - 1, False, True)

            with nc.Block() as block:
                @block.sync
                def _(sp):
                    def quad(q, pos0, pos1):
                        for pos in range(pos0, pos1):
                            kind, e = QUAD_ORDER[pos]
                            n = base + pos
                            sp.wait_ge(used, q * QC + n - RING + 1)
                            src = moe_source(kind, q * QUAD + e)
                            dst = ring[:, n % RING, :].rearrange("p (a b) -> p a b", b=src.shape[2])
                            sp.dma_start(dst, src).then_inc(landed[n % RING], 16)
                    quad(0, RING, QC)
                    with sp.Fori(1, QUADS) as q:
                        quad(q, 0, QC)
                    sent[0] = base + QC * QUADS
                    send_until(sp, sent[0])

                @block.tensor
                def _(pe):
                    def gather(q, half):
                        for k in range(4):
                            for i in range(TT):
                                v = xn[:, i, :].rearrange("p (m k) -> p k m", k=KT)[:, 4 * half + k, :]
                                mm = pe.matmul(PS[:, half, k * P:(k + 1) * P], v,
                                               pick[:, i, ds(q * QUAD, QUAD), :].rearrange("p e s -> p (e s)"),
                                               start=(i == 0), stop=(i == TT - 1))
                        mm.then_inc(gathered, 1)

                    def up_gate(e, q):
                        for j, kind in enumerate("gu"):
                            n = base + done_after[(kind, e)] - 1
                            pe.wait_ge(landed[n % RING], q * (16 * QC // RING) + 16 * (n // RING + 1))
                            w = w_slot(n)
                            for k in range(KT):
                                mm = pe.matmul(PS[e * SLOTS:(e + 1) * SLOTS, 2, j * CW:(j + 1) * CW],
                                               hs[:, k, e * SLOTS:(e + 1) * SLOTS], w[:, k, :],
                                               start=(k == 0), stop=(k == KT - 1))
                            mm.then_inc(used, 1)

                    def turn(q):
                        pe.wait_ge(hid_ready, q + 1)
                        for f in range(2):
                            mm = pe.transpose(PS[:, 3, f * P:(f + 1) * P], hid[:, f * P:(f + 1) * P], ident[:])
                        mm.then_inc(turned, 1)

                    def down(e, q, first):
                        n = base + done_after[("d", e)] - 1
                        pe.wait_ge(landed[n % RING], q * (16 * QC // RING) + 16 * (n // RING + 1))
                        pe.wait_ge(hidT_ready, q + 1)
                        if e == 0 and not first:
                            pe.wait_ge(y_moved, q)
                        w = w_slot(n, D)
                        for h in range(2):
                            for f in range(2):
                                mm = pe.matmul(PS[e * SLOTS:(e + 1) * SLOTS, 4 + h, :],
                                               hidT[:, f, e * SLOTS:(e + 1) * SLOTS],
                                               w[:, f, h * 512:(h + 1) * 512], start=(f == 0), stop=(f == 1))
                        mm.then_inc(used, 1)

                    def scatter(h, q, first):
                        pe.wait_ge(y_moved, q + 1)
                        pe.wait_ge(staged, q + 1)
                        if not (first and h == 0):
                            pe.wait_ge(added, q * 2 + h)
                        for i in range(TT):
                            mm = pe.matmul(PS[:, 6 + i, :], put_now[:, i * P:(i + 1) * P], ys[:, h * 512:(h + 1) * 512],
                                           start=True, stop=True)
                        mm.then_inc(scattered, 1)

                    def quad(q, first, last, second=False):
                        pe.wait_ge(hs_ready, q * 2 + 2)
                        up_gate(0, q)
                        if not first:
                            scatter(0, q - 1, second)
                        up_gate(1, q)
                        if not first:
                            scatter(1, q - 1, second)
                        up_gate(2, q)
                        up_gate(3, q)
                        if not last:
                            gather(q + 1, 0)
                        turn(q)
                        if not last:
                            gather(q + 1, 1)
                        for e in range(QUAD):
                            down(e, q, first)

                    gather(0, 0)
                    gather(0, 1)
                    quad(0, True, False)
                    quad(1, False, False, True)
                    with pe.Fori(2, QUADS - 1) as q:
                        quad(q, False, False)
                    quad(QUADS - 1, False, True)
                    scatter(0, QUADS - 1, False)
                    scatter(1, QUADS - 1, False)

                @block.scalar
                def _(act):
                    def quad(q, first, last):
                        act.wait_ge(used, q * QC + base + done_after[("u", QUAD - 1)])
                        act.activation(silu[:], PS[:, 2, 0:CW], ACT.Silu).then_inc(silu_ready, 1)
                        act.wait_ge(turned, q + 1)
                        act.activation(hidT[:], PS[:, 3, 0:CW].rearrange("p (f s) -> p f s", f=2),
                                       ACT.Copy).then_inc(hidT_ready, 1)
                        act.wait_ge(used, q * QC + base + QC)
                        act.activation(ys[:], PS[:, 4:6, :].rearrange("p b n -> p (b n)"), ACT.Copy).then_inc(y_moved, 1)
                    over_quads(act, quad)

                @block.gpsimd
                def _(pool):
                    def quad(q, first, last):
                        if not first:
                            pool.wait_ge(scattered, q * 2)
                        pool.tensor_copy(put_now[:], put[:, ds(q, 1), :].rearrange("p q n -> p (q n)")).then_inc(staged, 1)
                    over_quads(pool, quad)

                @block.vector
                def _(dve):
                    def make_rows(q):
                        for half in range(2):
                            dve.wait_ge(gathered, q * 2 + half + 1)
                            for k in range(4):
                                c = 4 * half + k
                                last = dve.tensor_scalar(hs[:, c, :], PS[:, half, k * P:(k + 1) * P], scale[:, c:c + 1],
                                                         shift[:, c:c + 1], ALU.mult, ALU.add)
                            last.then_inc(hs_ready, 1)

                    def activate(q):
                        dve.wait_ge(silu_ready, q + 1)
                        dve.tensor_tensor(hid[:], PS[:, 2, CW:2 * CW], silu[:], ALU.mult).then_inc(hid_ready, 1)

                    def add(h, q):
                        dve.wait_ge(scattered, q * 2 + h + 1)
                        part = sums[:, :, h * 512:(h + 1) * 512]
                        dve.tensor_tensor(part, part, PS[:, 6:8, :], ALU.add).then_inc(added, 1)

                    def quad(q, first, last):
                        if not first:
                            add(0, q - 1)
                            add(1, q - 1)
                        activate(q)
                        if not last:
                            make_rows(q + 1)

                    step = stepper(dve, dve_step)
                    step(dve.memset(sums[:], 0.0))
                    make_rows(0)
                    over_quads(dve, quad)
                    add(0, QUADS - 1)
                    add(1, QUADS - 1)

    def overflow_experts(rest, rows_dram, some_left, sums):
        with ExitStack() as scope:
            CB = sb(scope, "rest_rows", [P, EXPERTS, S])
            wb = sb(scope, "rest_w", [P, 3, 8 * CW])
            silu = sb(scope, "rest_silu", [P, 2, S])
            up = sb(scope, "rest_up", [P, 2, S])
            hid = sb(scope, "rest_hid", [P, 2, S])
            stored, spread = pool_dma_sem("o_stored"), pool_dma_sem("o_spread")
            arrived = [sem(f"o_arrived{j}") for j in range(3)]
            products, silu_ready, weighted, hid_ready, downs, added = (
                sem("o_products"), sem("o_silu"), sem("o_weighted"), sem("o_hid"), sem("o_downs"), sem("o_added"))

            def if_some(eng):
                return eng.If(eng.value_load(some_left[0:1, 0:1], min_val=0, max_val=1) > 0)

            with nc.Block() as block:
                @block.gpsimd
                def _(pool):
                    with if_some(pool):
                        pool.dma_start(rows_dram, rest[:]).then_inc(stored, 16)
                        pool.wait_ge(stored, 16)
                        pool.dma_start(CB[:], rows_dram.partition_broadcast(P)).then_inc(spread, 16)
                        pool.wait_ge(spread, 16)

                @block.sync
                def _(sp):
                    with if_some(sp):
                        with sp.Fori(0, EXPERTS) as e:
                            sp.wait_ge(downs, e + 1)
                            for j, kind in enumerate("gud"):
                                src = moe_source(kind, e)
                                sp.dma_start(wb[:, j, :].rearrange("p (a b) -> p a b", b=src.shape[2]), src)\
                                    .then_inc(arrived[j], 16)

                @block.tensor
                def _(pe):
                    with if_some(pe):
                        pe.sem_inc(downs, 1)
                        with pe.Fori(0, EXPERTS) as e:
                            for j in range(2):
                                pe.wait_ge(arrived[j], e * 16 + 16)
                                w = wb[:, j, :].rearrange("p (a b) -> p a b", b=CW)
                                for m in range(2):
                                    for k in range(KT):
                                        mm = pe.matmul(PS[:, j, m * S:(m + 1) * S], w[:, k, m * P:(m + 1) * P],
                                                       HT[:, k, :], start=(k == 0), stop=(k == KT - 1))
                            mm.then_inc(products, 1)
                            pe.wait_ge(arrived[2], e * 16 + 16)
                            pe.wait_ge(hid_ready, e + 1)
                            w = wb[:, 2, :].rearrange("p (a b) -> p a b", b=D)
                            for i in range(TT):
                                for h in range(2):
                                    for f in range(2):
                                        mm = pe.matmul(PS[:, 4 + 2 * i + h, :], hid[:, f, i * P:(i + 1) * P],
                                                       w[:, f, h * 512:(h + 1) * 512], start=(f == 0), stop=(f == 1))
                            mm.then_inc(downs, 1)
                            pe.wait_ge(added, e + 1)

                @block.scalar
                def _(act):
                    with if_some(act):
                        with act.Fori(0, EXPERTS) as e:
                            act.wait_ge(products, e + 1)
                            act.activation(silu[:], PS[:, 0, :].rearrange("p (m n) -> p m n", m=2), ACT.Silu)\
                                .then_inc(silu_ready, 1)

                @block.vector
                def _(dve):
                    with if_some(dve):
                        dve.wait_ge(spread, 16)
                        with dve.Fori(0, EXPERTS) as e:
                            dve.wait_ge(products, e + 1)
                            dve.tensor_tensor(up[:], PS[:, 1, :].rearrange("p (m n) -> p m n", m=2),
                                              CB[:, ds(e, 1), :].broadcast_to([P, 2, S]), ALU.mult).then_inc(weighted, 1)
                            dve.wait_ge(weighted, e + 1)
                            dve.wait_ge(silu_ready, e + 1)
                            dve.tensor_tensor(hid[:], up[:], silu[:], ALU.mult).then_inc(hid_ready, 1)
                            dve.wait_ge(downs, e + 2)
                            dve.tensor_tensor(sums[:], sums[:], PS[:, 4:8, :].rearrange("p (i h) n -> p i (h n)", i=TT),
                                              ALU.add).then_inc(added, 1)

    def add_gated(dve, step, psum, gate, scope):
        tmp = sb(scope, "gated", [P, TT, D])
        step(dve.tensor_tensor(tmp[:], psum, bc(gate[:], 1, TT), ALU.mult))
        step(dve.tensor_tensor(X[:], X[:], tmp[:], ALU.add))

    def output_projection(seg, src, groups, gate, bias=None, ada=None):
        base = segs[seg].base
        with ExitStack() as scope:
            tmp = sb(scope, "op_tmp", [P, 2, TT, CW])
            if ada is not None:
                stage = sb(scope, "ada_stage", [P, ada.per_step, 2 * D])
            moved = sem("o_moved")
            with nc.Block() as block:
                @block.sync
                def _(sp):
                    send_until(sp, base + 4 * groups)

                @block.tensor
                def _(pe):
                    for c in range(4):
                        for i in range(TT):
                            if i == 0:
                                for g in range(groups):
                                    arrive(pe, base + c * groups + g)
                            if bias is not None:
                                pe.matmul(PS[:, c, i * CW:(i + 1) * CW], ones[0:1, :], bias[0:1, c * CW:(c + 1) * CW],
                                          start=True, stop=False)
                            for g in range(groups):
                                w = w_slot(base + c * groups + g)
                                for k in range(KT):
                                    mm = pe.matmul(PS[:, c, i * CW:(i + 1) * CW],
                                                   src[:, g * KT + k, i * P:(i + 1) * P], w[:, k, :],
                                                   start=(bias is None and g == 0 and k == 0),
                                                   stop=(g == groups - 1 and k == KT - 1))
                                if i == TT - 1:
                                    mm.then_inc(used, 1)

                if ada is not None:
                    @block.gpsimd
                    def _(pool):
                        ada.fetch_all(pool, stage)

                @block.vector
                def _(dve):
                    step = stepper(dve, dve_step)
                    if ada is not None:
                        ada.add_all(dve, stage)
                    for c in range(4):
                        dve.wait_ge(used, base + (c + 1) * groups)
                        step(dve.tensor_tensor(tmp[:, c % 2], PS[:, c, :].rearrange("p (i n) -> p i n", i=TT),
                                               bc(gate[:, c * CW:(c + 1) * CW], 1, TT), ALU.mult))
                        xc = X[:, :, c * CW:(c + 1) * CW]
                        step(dve.tensor_tensor(xc, xc, tmp[:, c % 2], ALU.add))

    def turn_features(src, dst, groups, gain):
        turned, moved = sem("t_turned"), sem("t_moved")
        n = groups * KT
        with nc.Block() as block:
            @block.tensor
            def _(pe):
                for k in range(n):
                    if k >= 4:
                        pe.wait_ge(moved, k - 3)
                    for i in range(TT):
                        v = src[:, i, (k // KT) * D:(k // KT + 1) * D].rearrange("p (m k) -> p k m", k=KT)
                        mm = pe.transpose(PS[:, k % 4, i * P:(i + 1) * P], v[:, k % KT, :], ident[:])
                    mm.then_inc(turned, 1)

            @block.vector
            def _(dve):
                for k in range(n):
                    dve.wait_ge(turned, k + 1)
                    if gain is None:
                        dve.tensor_copy(dst[:, k, :], PS[:, k % 4, 0:S]).then_inc(moved, 1)
                    else:
                        dve.tensor_scalar(dst[:, k, :], PS[:, k % 4, 0:S], gain[:, k:k + 1], None,
                                          ALU.mult).then_inc(moved, 1)

    ada_2 = t["c_2"], t["ada_w"][0], t["ada_b"][0], t["norm_mix_g"][0], t["norm_ffn_g"][0]
    ada_1 = t["c"], t["w_ada"][0], t["b_ada"][0], t["norm_mix"][0], t["norm_ffn"][0]
    with ExitStack() as scope:
        ada = Ada(scope, *ada_1, groups=(0,), per_step=4)
        stage = sb(scope, "ada_stage", [P, 4, 2 * D])
        with nc.Block() as block:
            @block.gpsimd
            def _(pool):
                ada.fetch_all(pool, stage)

            @block.vector
            def _(dve):
                ada.add_all(dve, stage)

            @block.sync
            def _(sp):
                sp.wait_ge(ada.summed, 4)
                send_until(sp, 0)
        ada.finish()
    norm_block(mod[:, 1, :], mod[:, 0, :])

    with ExitStack() as scope:
        merged = sb(scope, "merged", [P, TT, D])
        mix_gain = sb(scope, "mix_gain", [P, KT])
        inner = ExitStack()
        RT = sb(inner, "ret_tok", [P, TT, 4 * RET_W])
        HG = sb(inner, "hgrn_tok", [P, TT, 2 * HGRN_W])
        GG = sb(inner, "gla_tok", [P, TT, 2 * GLA_W])
        HF = sb(inner, "hgrn_rows", [P, 6, S])
        GF = sb(inner, "gla_rows", [P, 2, S])
        gaT = sb(inner, "gla_rank", [RANK, S])
        decay = sb(inner, "ret_decay", [P, RET_H, 384])
        level_mask = sb(inner, "level_mask", [P, LEVELS, P])
        freq = sb(inner, "freq", [P, 32])
        pos = sb(inner, "pos", [P, TT], I32)
        posf = sb(inner, "posf", [P, TT])
        wga = sb(inner, "wga", [P, KT, RANK])
        wa2 = sb(inner, "wa2", [RANK, P])
        gba = sb(inner, "gba", [P, 1])
        lb = sb(inner, "lb", [P, 8, 3])
        small = pool_dma_sem("mix_small")

        def mover(dst, width):
            def ev(act, bank, j):
                return act.activation(dst[:, :, j * CW:(j + 1) * CW] if width == "tokens" else
                                      dst[:, 2 * j:2 * j + 2, :], bank, ACT.Copy)
            return ev

        with nc.allow_non_contiguous_dma(reason="a few small vectors"):
            with nc.Block() as block:
                @block.gpsimd
                def _(pool):
                    loads = [
                        (decay[:], t["const_decay"]), (level_mask[:], t["const_levels"]),
                        (freq[:], t["const_freq"]),
                        (pos[:], t["positions"][0].rearrange("(i p) -> p i", p=P)),
                        (wga[:], wi[:, 15 * CW:].rearrange("(p k) n -> p k n", k=KT)),
                        (wa2[:], t["gla_wa2"][0]), (gba[:], t["gla_ba"][0].rearrange("(p a) -> p a", a=1)),
                        (lb[:, 0, :], t["hgrn_lb_logits"][0].rearrange("(m p) -> p m", p=P)),
                        (mix_gain[0:48, :], t["ret_norm"][0].rearrange("(p k) -> p k", k=KT)),
                        (mix_gain[48:96, :], t["hgrn_norm"][0].rearrange("(p k) -> p k", k=KT)),
                        (mix_gain[96:128, :], t["gla_norm"][0].rearrange("(p k) -> p k", k=KT)),
                    ]
                    for dst, src in loads:
                        pool.dma_start(dst, src).then_inc(small, 16)
                    pool.wait_ge(small, 16 * len(loads))

        with ExitStack() as beside:
            ada = Ada(beside, *ada_1, groups=(1, 2), per_step=4)
            stage = sb(beside, "ada_stage", [P, 4, 2 * D])
            project([("w_in", 0, 6, "tokens", mover(RT, "tokens")), ("w_in", 6, 3, "rows", mover(HF, "rows")),
                     ("w_in", 9, 3, "tokens", mover(HG, "tokens")), ("w_in", 12, 1, "rows", mover(GF, "rows")),
                     ("w_in", 13, 2, "tokens", mover(GG, "tokens"))], ada, stage)
            ada.finish()

        qd = sb(inner, "gated_q", [P, 4, S])
        kd = sb(inner, "gated_k", [P, 4, S])
        ad = sb(inner, "gated_a", [P, 4, S])
        g_low, g_gate, g_sig, g_e = sem("g_low"), sem("g_gate"), sem("g_sig"), sem("g_e")
        lb_e, ang, trig, lowc = sem("lb_e"), sem("ang"), sem("trig"), sem("lowc")
        y_ready, ln_ready, e_ready = sem("y_ready"), sem("ln_ready"), sem("e_ready")
        narrow = ExitStack()
        w1 = sb(narrow, "gla_w", [P, 3, S])
        rot = sb(narrow, "rot", [P, 2, TT, 2 * RET_W])
        angle = sb(narrow, "angle", [P, 6, TT, 32])
        MAGIC = 12582912.0
        with nc.Block() as block:
            @block.tensor
            def _(pe):
                for k in range(KT):
                    mm = pe.matmul(PS[0:RANK, 0, 0:S], wga[:, k, :], HT[:, k, :], start=(k == 0), stop=(k == KT - 1))
                mm.then_inc(g_low, 1)
                pe.wait_ge(lowc, 1)
                pe.matmul(PS[:, 1, 0:S], wa2[:], gaT[:], start=True, stop=True).then_inc(g_gate, 1)

            @block.scalar
            def _(act):
                act.wait_ge(g_low, 1)
                act.activation(gaT[:], PS[0:RANK, 0, 0:S], ACT.Copy).then_inc(lowc, 1)
                act.activation(kd[:, 0:3, :], HF[:, 3:6, :], ACT.Sigmoid, scale=-1.0)
                act.activation(ad[:, 0:3, :], HF[:, 3:6, :], ACT.Sigmoid).then_inc(g_sig, 1)
                act.activation(qd[:, 0:3, :], HF[:, 0:3, :], ACT.Silu).then_inc(g_sig, 1)
                act.activation(RT[:, :, 3 * RET_W:], RT[:, :, 3 * RET_W:], ACT.Silu)
                act.activation(HG[:, :, HGRN_W:], HG[:, :, HGRN_W:], ACT.Silu)
                act.activation(GG[:, :, GLA_W:], GG[:, :, GLA_W:], ACT.Silu)
                act.wait_ge(lb_e, 1)
                act.activation(lb[:, 2, :], lb[:, 1, :], ACT.Exp).then_inc(lb_e, 1)
                act.wait_ge(y_ready, 1)
                act.activation(w1[:, 1, :], w1[:, 1, :], ACT.Exp).then_inc(e_ready, 1)
                act.wait_ge(e_ready, 1)
                act.activation(w1[:, 2, :], w1[:, 1, :], ACT.Ln, bias=1.0).then_inc(ln_ready, 1)
                act.wait_ge(y_ready, 2)
                act.activation(ad[:, 3, :], w1[:, 0, :], ACT.Exp, scale=1.0 / TAU)
                act.wait_ge(ang, 1)
                act.activation(angle[:, 4:6], angle[:, 2:4], ACT.Sin).then_inc(trig, 1)

            @block.vector
            def _(dve):
                step = stepper(dve, dve_step)
                dve.wait_ge(g_gate, 1)
                step(dve.tensor_scalar(w1[:, 0, :], PS[:, 1, 0:S], gba[:, 0:1], None, ALU.add))
                step(dve.tensor_scalar(w1[:, 2, :], w1[:, 0, :], -1.0, None, ALU.mult))
                dve.tensor_tensor(w1[:, 1, :], w1[:, 0, :], w1[:, 2, :], ALU.min).then_inc(y_ready, 1)
                dve.tensor_tensor(lb[:, 1, :], lb[:, 0, :], lb[:, 0, :], ALU.subtract).then_inc(lb_e, 1)
                dve.wait_ge(lb_e, 2)
                step(dve.reciprocal(lb[:, 3, :], lb[:, 2, :]))
                step(dve.tensor_tensor(lb[:, 4, :], lb[:, 2, :], lb[:, 3, :], ALU.mult))
                step(dve.tensor_tensor(lb[:, 5, :], lb[:, 4, :], lb[:, 4, :], ALU.subtract))
                step(dve.tensor_scalar(lb[:, 6, :], lb[:, 5, :], -1.0, 1.0, ALU.mult, ALU.add))
                step(dve.tensor_copy(posf[:], pos[:]))
                for i in range(TT):
                    step(dve.tensor_scalar(angle[:, 0, i, :], freq[:], posf[:, i:i + 1], None, ALU.mult))
                step(dve.tensor_scalar(angle[:, 1], angle[:, 0], 0.15915494309189535, MAGIC, ALU.mult, ALU.add))
                step(dve.tensor_scalar(angle[:, 1], angle[:, 1], -MAGIC, None, ALU.add))
                for piece in (6.28125, 1.93530321e-03, 6.283185307179586 - 6.28125 - 1.93530321e-03):
                    step(dve.scalar_tensor_tensor(out=angle[:, 0], in0=angle[:, 1], scalar=-piece, in1=angle[:, 0],
                                                  op0=ALU.mult, op1=ALU.add))
                step(dve.tensor_scalar(angle[:, 2], angle[:, 0], 3.1415925, -3.1415925, ALU.min, ALU.max))
                step(dve.tensor_scalar(angle[:, 4], angle[:, 2], -1.0, None, ALU.mult))
                step(dve.tensor_tensor(angle[:, 3], angle[:, 2], angle[:, 4], ALU.max))
                dve.tensor_scalar(angle[:, 3], angle[:, 3], -1.0, 1.5707963267948966, ALU.mult,
                                  ALU.add).then_inc(ang, 1)
                dve.wait_ge(g_sig, 2)
                for m in range(3):
                    dve.tensor_scalar(ad[:, m, :], ad[:, m, :], lb[:, 6, m:m + 1], lb[:, 5, m:m + 1], ALU.mult, ALU.add)
                    dve.tensor_scalar(kd[:, m, :], kd[:, m, :], lb[:, 6, m:m + 1], None, ALU.mult)
                step(dve.tensor_scalar(qd[:, 0:3, :], qd[:, 0:3, :], HD ** -0.5, None, ALU.mult))
                step(dve.tensor_scalar(ad[:, 0:3, :], ad[:, 0:3, :], F_MIN, None, ALU.max))
                dve.tensor_scalar(qd[:, 3, :], GF[:, 0, :], GLA_DK ** -0.5, None, ALU.mult)
                dve.tensor_copy(kd[:, 3, :], GF[:, 1, :])
                dve.wait_ge(ln_ready, 1)
                dve.scalar_tensor_tensor(out=w1[:, 0, :], in0=w1[:, 0, :], scalar=0.0, in1=w1[:, 2, :],
                                         op0=ALU.min, op1=ALU.subtract).then_inc(y_ready, 1)
                dve.wait_ge(trig, 1)
                for i in range(TT):
                    qk = RT[:, i, 0:2 * RET_W].rearrange("p (h a d) -> p h a d", a=2, d=32)
                    for j, tab in ((0, 5), (1, 4)):
                        for a in range(2):
                            last = dve.tensor_tensor(rot[:, j, i, :].rearrange("p (h a d) -> p h a d", a=2, d=32)[:, :, a, :],
                                              qk[:, :, a, :], bc(angle[:, tab, i, :], 1, 2 * RET_H), ALU.mult)
                    c4 = rot[:, 0, i, :].rearrange("p (h a d) -> p h a d", a=2, d=32)
                    s4 = rot[:, 1, i, :].rearrange("p (h a d) -> p h a d", a=2, d=32)
                    step(last)
                    dve.tensor_tensor(qk[:, :, 0, :], c4[:, :, 0, :], s4[:, :, 1, :], ALU.subtract)
                    dve.tensor_tensor(qk[:, :, 1, :], c4[:, :, 1, :], s4[:, :, 0, :], ALU.add)

        narrow.close()

        QT = sb(inner, "ret_T", [P, 6, S])
        SW = sb(inner, "ret_scores", [P, 2, 384])
        QL = sb(inner, "level_q", [P, LEVELS, 2, S])
        KL = sb(inner, "level_k", [P, LEVELS, 2, S])
        prefix = sb(inner, "prefix", [P, 2, S])
        suffix = sb(inner, "suffix", [P, 2, S])

        def o_cols(head, i):
            c = head * HD
            return PS[:, 4 + 2 * i + c // 512, c % 512:c % 512 + HD]

        def level_factors(eng, marks, m0, tile):
            step = stepper(eng, marks)
            q, k, pre, suf = qd[:, m0 + tile, :], kd[:, m0 + tile, :], prefix[:, tile, :], suffix[:, tile, :]
            eng.tensor_copy(pre, ad[:, m0 + tile, :])
            step(eng.memset(suf, 1.0))
            for l in range(1, LEVELS + 1):
                b = 1 << (l - 1)
                eng.tensor_tensor(QL[:, l % LEVELS, tile, :], q, pre, ALU.mult)
                step(eng.tensor_tensor(KL[:, l % LEVELS, tile, :], k, suf, ALU.mult))
                if l < LEVELS:
                    n = S // (2 * b)
                    pv = pre.rearrange("p (n h b) -> p n h b", h=2, b=b)
                    sv = suf.rearrange("p (n h b) -> p n h b", h=2, b=b)
                    step(eng.tensor_tensor(sv[:, :, 0, :], sv[:, :, 0, :],
                                           pv[:, :, 1, b - 1:b].broadcast_to([P, n, b]), ALU.mult))
                    step(eng.tensor_tensor(pv[:, :, 1, :], pv[:, :, 1, :],
                                           pv[:, :, 0, b - 1:b].broadcast_to([P, n, b]), ALU.mult))

        turned, tmoved, r_sc, r_w = sem("r_turned"), sem("r_tmoved"), sem("r_scores"), sem("r_weights")
        with nc.Block() as block:
            @block.gpsimd
            def _(pool):
                level_factors(pool, pool_step, 0, 0)

            @block.tensor
            def _(pe):
                for j in range(6):
                    if j >= 4:
                        pe.wait_ge(tmoved, j - 3)
                    for i in range(TT):
                        mm = pe.transpose(PS[:, j % 4, i * P:(i + 1) * P], RT[:, i, j * P:(j + 1) * P], ident[:])
                    mm.then_inc(turned, 1)
                pe.wait_ge(tmoved, 6)

                def values(h):
                    pe.wait_ge(r_w, h + 1)
                    w = SW[:, h % 2, :]
                    v = RT[:, :, 2 * RET_W + h * HD:2 * RET_W + (h + 1) * HD]
                    pe.matmul(o_cols(h, 0), w[:, 0:P], v[:, 0, :], start=True, stop=True)
                    pe.matmul(o_cols(h, 1), w[:, P:2 * P], v[:, 0, :], start=True, stop=False)
                    pe.matmul(o_cols(h, 1), w[:, 2 * P:3 * P], v[:, 1, :], start=False, stop=True)

                for h in range(RET_H):
                    r0, m = HD * (h % 2), h // 2
                    q, k = QT[r0:r0 + HD, m, :], QT[r0:r0 + HD, 3 + m, :]
                    pe.matmul(PS[:, h % 4, 0:S], k[:, 0:P], q, start=True, stop=True)
                    pe.matmul(PS[:, h % 4, S:384], k[:, P:S], q[:, P:S], start=True, stop=True).then_inc(r_sc, 1)
                    if h:
                        values(h - 1)
                values(RET_H - 1)

            @block.vector
            def _(dve):
                for j in range(6):
                    dve.wait_ge(turned, j + 1)
                    dve.tensor_copy(QT[:, j, :], PS[:, j % 4, 0:S]).then_inc(tmoved, 1)
                for h in range(RET_H):
                    dve.wait_ge(r_sc, h + 1)
                    dve.scalar_tensor_tensor(out=SW[:, h % 2, :], in0=PS[:, h % 4, 0:384], scalar=HD ** -0.5,
                                             in1=decay[:, h, :], op0=ALU.mult, op1=ALU.mult).then_inc(r_w, 1)
                level_factors(dve, dve_step, 0, 1)

        GWT = sb(inner, "gated_scores", [P, LEVELS, P])
        GS = sb(inner, "gated_sums", [P, 3, P])
        CR = sb(inner, "cross", [P, 6, P])

        def cross_place(gated, c):
            r0 = gated[c][1]
            k = sum(g[1] == r0 for g in gated[:c])
            return PS[:, r0 // 32, k * P:(k + 1) * P]

        def gated_heads(gated, m0):
            g_sc, g_w, g_cr, g_crw = sem("g_scores"), sem("g_weights"), sem("g_cross"), sem("g_crossw")
            g_masked = sem("g_masked")
            units = [(g, i) for g in gated for i in range(TT)]
            n = len(gated)
            with nc.Block() as block:
                @block.tensor
                def _(pe):
                    for c, (m, r0, dk, _, _, _) in enumerate(gated):
                        mm = pe.matmul(cross_place(gated, c), KL[r0:r0 + dk, 0, m - m0, 0:P],
                                       QL[r0:r0 + dk, 0, m - m0, P:S], start=True, stop=True)
                    mm.then_inc(g_cr, 1)
                    pe.wait_ge(g_crw, 1)

                    def scores(u):
                        (m, r0, dk, _, _, _), i = units[u]
                        for l in range(LEVELS):
                            q = (qd[r0:r0 + dk, m] if l == 0 else QL[r0:r0 + dk, l, m - m0])[:, i * P:(i + 1) * P]
                            k = (kd[r0:r0 + dk, m] if l == 0 else KL[r0:r0 + dk, l, m - m0])[:, i * P:(i + 1) * P]
                            mm = pe.matmul(PS[:, 2 * (u % 2) + l // 4, (l % 4) * P:(l % 4 + 1) * P], k, q,
                                           start=True, stop=True)
                        mm.then_inc(g_sc, 1)

                    def values(u):
                        (_, _, _, src, v0, head), i = units[u]
                        pe.wait_ge(g_w, u + 1)
                        pe.matmul(o_cols(head, i), GS[:, u % 3, :], src[:, i, v0:v0 + HD], start=True, stop=(i == 0))
                        if i:
                            pe.matmul(o_cols(head, i), CR[:, u // 2, :], src[:, 0, v0:v0 + HD], start=False, stop=True)

                    for u in range(2 * n):
                        if u >= 2:
                            pe.wait_ge(g_masked, u - 1)
                        scores(u)
                        if u >= 2:
                            values(u - 2)
                    values(2 * n - 2)
                    values(2 * n - 1)

                @block.vector
                def _(dve):
                    dve.wait_ge(g_cr, 1)
                    for c in range(n):
                        last = dve.tensor_copy(CR[:, c, :], cross_place(gated, c))
                    last.then_inc(g_crw, 1)
                    for u in range(2 * n):
                        dve.wait_ge(g_sc, u + 1)
                        b = 2 * (u % 2)
                        if u:
                            dve.wait_ge(g_w, u)
                        dve.tensor_tensor(GWT[:], PS[:, b:b + 2, :].rearrange("p a (l n) -> p (a l) n", n=P),
                                          level_mask[:], ALU.mult).then_inc(g_masked, 1)
                        dve.wait_ge(g_masked, u + 1)
                        dve.tensor_reduce(GS[:, u % 3, :], GWT[:].rearrange("p l n -> p n l"), AX.X,
                                          ALU.add).then_inc(g_w, 1)

        gated = [(h // 2, HD * (h % 2), HD, HG, h * HD, RET_H + h) for h in range(HGRN_H)]
        gated += [(3, GLA_DK * h, GLA_DK, GG, h * HD, RET_H + HGRN_H + h) for h in range(GLA_H)]
        gated_heads(gated[:4], 0)
        with nc.Block() as block:
            @block.gpsimd
            def _(pool):
                level_factors(pool, pool_step, 2, 0)

            @block.vector
            def _(dve):
                level_factors(dve, dve_step, 2, 1)
        gated_heads(gated[4:], 2)

        hs = sb(inner, "head_sums", [P, 4, TT * HEADS])
        squared, meaned, rooted = sem("h_squared"), sem("h_meaned"), sem("h_rooted")
        O = PS[:, 4:8, :].rearrange("p (i b) n -> p i (b n)", i=TT)
        with nc.Block() as block:
            @block.scalar
            def _(act):
                act.activation(merged[:], O, ACT.Square).then_inc(squared, 1)
                act.wait_ge(meaned, 1)
                act.activation(hs[:, 2, :], hs[:, 1, :], ACT.Sqrt).then_inc(rooted, 1)

            @block.vector
            def _(dve):
                step = stepper(dve, dve_step)
                dve.wait_ge(squared, 1)
                step(dve.tensor_reduce(hs[:, 0, :], merged[:].rearrange("p i (h d) -> p (i h) d", d=HD), AX.X, ALU.add))
                dve.tensor_scalar(hs[:, 1, :], hs[:, 0, :], 1.0 / HD, EPS, ALU.mult, ALU.add).then_inc(meaned, 1)
                dve.wait_ge(rooted, 1)
                step(dve.reciprocal(hs[:, 3, :], hs[:, 2, :]))
                step(dve.tensor_tensor(merged[:].rearrange("p i (h d) -> p (i h) d", d=HD),
                                       PS[:, 4:8, :].rearrange("p b (h d) -> p (b h) d", d=HD),
                                       bc(hs[:, 3, :], 2, HD), ALU.mult))
                for c0, g in ((0, RT[:, :, 3 * RET_W:]), (RET_W, HG[:, :, HGRN_W:]),
                              (RET_W + HGRN_W, GG[:, :, GLA_W:])):
                    part = merged[:, :, c0:c0 + g.shape[2]]
                    dve.tensor_tensor(part, part, g, ALU.mult)
        inner.close()
        MT = sb(scope, "merged_T", [P, KT, S])
        turn_features(merged, MT, 1, mix_gain)
        with ExitStack() as beside:
            ada = Ada(beside, *ada_2, groups=(0,), per_step=4)
            output_projection("w_out", MT, 1, gate_a, ada=ada)
            ada.finish(mod_next)

    clear_phase_sems()

    with ExitStack() as scope:
        xn = sb(scope, "normed", [P, TT, D])
        pick = sb(scope, "pick", [P, TT, EXPERTS, SLOTS])
        put = sb(scope, "put", [P, QUADS, S])
        rest = sb(scope, "rest_T", [EXPERTS, S])
        some_left = sb(scope, "some_left", [P, 1], I32)
        norm_block(mod[:, 3, :], mod[:, 2, :], xn)
        route = ExitStack()
        NR = GROUPS + EXPERTS
        wr = sb(route, "w_router", [P, KT, NR])
        br = sb(route, "b_router", [P, NR])
        lg = sb(route, "logits", [P, TT, NR])
        order4 = sb(route, "order4", [P, 16])
        g4 = sb(route, "group_scratch", [P, 4, TT, GROUPS])
        e8 = sb(route, "expert_scratch", [P, 8, TT, PER_GROUP])
        s1 = sb(route, "scalars", [P, 16, TT])
        em = sb(route, "by_group", [P, TT, EXPERTS])
        slots = sb(route, "slot_numbers", [P, SLOTS])
        member = sb(route, "member", [P, TT, EXPERTS])
        place = sb(route, "place", [P, TT, EXPERTS])
        keep = sb(route, "past_slots", [P, TT, EXPERTS])
        heavy = sb(route, "weighted_pick", [P, TT, EXPERTS, SLOTS])
        most = sb(route, "most", [P, 2])
        ranked, rank_ready, heavied, turned, moved, restd = (sem("r_ranked"), sem("r_rank"), sem("r_heavy"),
                                                             sem("r_turned"), sem("r_moved"), sem("r_rest"))
        small, lgm, xin, xout = pool_dma_sem("r_small"), sem("r_logits"), sem("r_expin"), sem("r_expout")
        rows_dram = nc.dram_tensor("combine_rows", (EXPERTS, S), F32, kind="Internal").ap()
        with nc.Block() as block:
            @block.gpsimd
            def _(pool):
                with nc.allow_non_contiguous_dma(reason="small router weights"):
                    pool.dma_start(wr[:, :, 0:GROUPS],
                                   t["router_group_w"][0].rearrange("(p k) n -> p k n", k=KT)).then_inc(small, 16)
                    pool.dma_start(wr[:, :, GROUPS:],
                                   t["router_expert_w"][0].rearrange("(p k) n -> p k n", k=KT)).then_inc(small, 16)
                pool.dma_start(br[:, 0:GROUPS], t["router_group_b"][0].partition_broadcast(P)).then_inc(small, 16)
                pool.dma_start(br[:, GROUPS:], t["router_expert_b"][0].partition_broadcast(P)).then_inc(small, 16)
                pool.dma_start(order4[:], t["const_order"]).then_inc(small, 16)
                pool.dma_start(slots[:], t["const_slots"]).then_inc(small, 16)

            @block.tensor
            def _(pe):
                pe.wait_ge(small, 96)
                for i in range(TT):
                    for k in range(KT):
                        mm = pe.matmul(PS[:, i, 0:NR], HT[:, k, i * P:(i + 1) * P], wr[:, k, :],
                                       start=(k == 0), stop=(k == KT - 1))
                mm.then_inc(lgm, 1)
                pe.wait_ge(ranked, 1)
                pe.matmul(PS[:, 2, 0:EXPERTS], pairs[:, 0:P], member[:, 0, :], start=True, stop=True)
                pe.matmul(PS[:, 2, EXPERTS:2 * EXPERTS], ones[:], member[:, 0, :], start=True, stop=False)
                pe.matmul(PS[:, 2, EXPERTS:2 * EXPERTS], pairs[:, 0:P], member[:, 1, :], start=False, stop=True)
                pe.matmul(PS[:, 3, 0:EXPERTS], ones[:], member[:, 0, :], start=True, stop=False)
                pe.matmul(PS[:, 3, 0:EXPERTS], ones[:], member[:, 1, :], start=False, stop=True).then_inc(rank_ready, 1)
                pe.wait_ge(restd, 1)
                for i in range(TT):
                    mm = pe.transpose(PS[0:EXPERTS, 0, i * P:(i + 1) * P], keep[:, i, :], ident[:])
                mm.then_inc(lgm, 1)
                pe.wait_ge(heavied, TT)
                for q in range(QUADS):
                    if q >= 4:
                        pe.wait_ge(moved, q - 3)
                    for i in range(TT):
                        mm = pe.transpose(PS[:, 4 + q % 4, i * P:(i + 1) * P],
                                          heavy[:, i, q * QUAD:(q + 1) * QUAD, :].rearrange("p e s -> p (e s)"), ident[:])
                    mm.then_inc(turned, 1)

            @block.scalar
            def _(act):
                act.wait_ge(xin, 1)
                act.activation(g4[:, 0], g4[:, 0], ACT.Exp).then_inc(xout, 1)
                act.wait_ge(xin, 2)
                act.activation(s1[:, 6, :], s1[:, 6, :], ACT.Exp).then_inc(xout, 1)
                for q in range(QUADS):
                    act.wait_ge(turned, q + 1)
                    act.activation(put[:, q, :], PS[:, 4 + q % 4, 0:S], ACT.Copy).then_inc(moved, 1)

            @block.vector
            def _(dve):
                step = stepper(dve, dve_step)
                dve.wait_ge(lgm, 1)
                step(dve.tensor_tensor(lg[:], PS[:, 0:2, 0:NR], bc(br[:], 1, TT), ALU.add))
                gl = lg[:, :, 0:GROUPS]
                step(dve.tensor_reduce(s1[:, 0, :], gl, AX.X, ALU.max))
                dve.tensor_tensor(g4[:, 0], gl, bc(s1[:, 0, :], 2, GROUPS), ALU.subtract).then_inc(xin, 1)

                def first_of_equals(x, top, n, tmp, best, onehot):
                    step(dve.tensor_tensor(tmp, x, bc(top, 2, n), ALU.is_equal))
                    step(dve.tensor_tensor(tmp, tmp, bc(order4[:, 0:n], 1, TT), ALU.mult))
                    step(dve.tensor_reduce(best, tmp, AX.X, ALU.max))
                    step(dve.tensor_tensor(onehot, tmp, bc(best, 2, n), ALU.is_equal))

                first_of_equals(gl, s1[:, 0, :], GROUPS, g4[:, 1], s1[:, 1, :], g4[:, 2])
                dve.wait_ge(xout, 1)
                step(dve.tensor_reduce(s1[:, 2, :], g4[:, 0], AX.X, ALU.add))
                step(dve.reciprocal(s1[:, 3, :], s1[:, 2, :]))
                for i in range(TT):
                    last = dve.tensor_tensor(em[:, i, :].rearrange("p (g e) -> p g e", g=GROUPS),
                                             lg[:, i, GROUPS:].rearrange("p (g e) -> p g e", g=GROUPS),
                                             bc(g4[:, 2, i, :], 2, PER_GROUP), ALU.mult)
                step(last)
                for i in range(TT):
                    last = dve.tensor_reduce(e8[:, 0, i, :], em[:, i, :].rearrange("p (g e) -> p e g", g=GROUPS),
                                             AX.X, ALU.add)
                step(last)
                step(dve.tensor_reduce(s1[:, 4, :], e8[:, 0], AX.X, ALU.max))
                first_of_equals(e8[:, 0], s1[:, 4, :], PER_GROUP, e8[:, 1], s1[:, 1, :], e8[:, 2])
                step(dve.scalar_tensor_tensor(out=e8[:, 3], in0=e8[:, 2], scalar=NEG, in1=e8[:, 0],
                                              op0=ALU.mult, op1=ALU.add))
                step(dve.tensor_reduce(s1[:, 5, :], e8[:, 3], AX.X, ALU.max))
                dve.tensor_tensor(s1[:, 6, :], s1[:, 5, :], s1[:, 4, :], ALU.subtract).then_inc(xin, 1)
                first_of_equals(e8[:, 3], s1[:, 5, :], PER_GROUP, e8[:, 1], s1[:, 1, :], e8[:, 4])
                dve.wait_ge(xout, 2)
                step(dve.tensor_scalar(s1[:, 7, :], s1[:, 6, :], 1.0, None, ALU.add))
                step(dve.reciprocal(s1[:, 8, :], s1[:, 7, :]))
                step(dve.tensor_tensor(s1[:, 9, :], s1[:, 8, :], s1[:, 3, :], ALU.mult))
                step(dve.tensor_tensor(s1[:, 10, :], s1[:, 9, :], s1[:, 6, :], ALU.mult))
                dve.tensor_tensor(e8[:, 5], e8[:, 2], bc(s1[:, 9, :], 2, PER_GROUP), ALU.mult)
                step(dve.tensor_tensor(e8[:, 6], e8[:, 4], bc(s1[:, 10, :], 2, PER_GROUP), ALU.mult))
                step(dve.tensor_tensor(e8[:, 7], e8[:, 5], e8[:, 6], ALU.add))
                for i in range(TT):
                    last = dve.tensor_tensor(em[:, i, :].rearrange("p (g e) -> p g e", g=GROUPS),
                                             bc(g4[:, 2, i, :], 2, PER_GROUP), bc(e8[:, 7, i, :], 1, GROUPS), ALU.mult)
                step(last)
                step(dve.tensor_tensor(e8[:, 5], e8[:, 2], e8[:, 4], ALU.add))
                for i in range(TT):
                    last = dve.tensor_tensor(member[:, i, :].rearrange("p (g e) -> p g e", g=GROUPS),
                                             bc(g4[:, 2, i, :], 2, PER_GROUP), bc(e8[:, 5, i, :], 1, GROUPS), ALU.mult)
                last.then_inc(ranked, 1)
                dve.wait_ge(rank_ready, 1)
                step(dve.tensor_tensor(place[:], PS[:, 2, 0:2 * EXPERTS].rearrange("p (i e) -> p i e", i=TT), member[:],
                                       ALU.mult))
                step(dve.tensor_scalar(place[:], place[:], -1.0, None, ALU.add))
                step(dve.tensor_scalar(keep[:], place[:], float(SLOTS), None, ALU.is_ge))
                dve.tensor_tensor(keep[:], keep[:], em[:], ALU.mult).then_inc(restd, 1)
                step(dve.tensor_reduce(most[:, 0:1], PS[:, 3, 0:EXPERTS], AX.X, ALU.max))
                step(dve.tensor_scalar(most[:, 1:2], most[:, 0:1], float(SLOTS), None, ALU.is_gt))
                dve.tensor_copy(some_left[:], most[:, 1:2])
                for i in range(TT):
                    step(dve.tensor_tensor(pick[:, i], bc(place[:, i, :], 2, SLOTS), bc(slots[:], 1, EXPERTS),
                                           ALU.is_equal))
                    dve.tensor_tensor(heavy[:, i], pick[:, i], bc(em[:, i, :], 2, SLOTS), ALU.mult).then_inc(heavied, 1)
                dve.wait_ge(lgm, 2)
                dve.tensor_copy(rest[:], PS[0:EXPERTS, 0, 0:S])
        route.close()
        sums = sb(scope, "expert_sums", [P, TT, D])
        routed_experts(pick, put, xn, sums)
        overflow_experts(rest, rows_dram, some_left, sums)
        with nc.Block() as block:
            @block.vector
            def _(dve):
                step = stepper(dve, dve_step)
                step(dve.tensor_tensor(sums[:], sums[:], bc(gate_b[:], 1, TT), ALU.mult))
                dve.tensor_tensor(X[:], X[:], sums[:], ALU.add)

    plain_norm(t["norm_final"], None)

    clear_phase_sems()

    norm_block(mod_next[:, 1, :], mod_next[:, 0, :])

    with ExitStack() as scope:
        att = sb(scope, "att", [P, TT, KV_H * HD])
        y = sb(scope, "y", [P, TT, SSM_IN])
        ssm_gain = sb(scope, "ssm_gain", [P, 2 * KT])
        wide = ExitStack()
        ZV = sb(wide, "z_v", [P, TT, SSM_IN + KV_H * HD])
        XB = sb(wide, "xbc", [P, XT, S + CONV - 1])
        dt = sb(wide, "dt", [P, TT, SSM_H])
        convT = sb(wide, "conv_T", [P, (CONV + 1) * XT])
        rowc = sb(wide, "row_consts", [P, 3, SSM_H])

        inner = ExitStack()
        QT = sb(inner, "att_q", [P, ATT_G * KT, S])
        KTT = sb(inner, "att_k", [P, KT, S])
        wdt = sb(inner, "w_dt", [P, KT, SSM_H])
        rawc = sb(inner, "conv_raw", [P, P])
        table = sb(inner, "rel_table", [BUCKETS, ATT_G * KV_H])
        onehot = sb(inner, "bucket_onehot", [BUCKETS, 384])
        gsel = sb(inner, "group_select", [ATT_G, ATT_G * KV_H])
        gmask = sb(inner, "group_mask", [ATT_G, 384])
        flip = sb(inner, "flip", [P, P])
        bias_rows = sb(inner, "bias_rows", [ATT_G * KV_H, 384])
        bias_dram = nc.dram_tensor("bias_rows_dram", (ATT_G * KV_H, 384), F32, kind="Internal").ap()
        small, made, moved1, stored = pool_dma_sem("a_small"), sem("a_made"), sem("a_moved"), pool_dma_sem("a_stored")
        with nc.Block() as block:
            @block.gpsimd
            def _(pool):
                with nc.allow_non_contiguous_dma(reason="small vectors"):
                    loads = [
                        (wdt[:], hi[:, HY_DT:HY_DT + SSM_H].rearrange("(p k) n -> p k n", k=KT)),
                        (rawc[0:CONV * XT, :], t["hy_conv_w"][0].rearrange("j (m p) -> (j m) p", p=P)),
                        (rawc[CONV * XT:(CONV + 1) * XT, :], t["hy_conv_b"][0].rearrange("(m p) -> m p", p=P)),
                        (table[:], t["rel_table"]), (onehot[:], t["const_onehot"]), (gsel[:], t["const_gsel"]),
                        (gmask[:], t["const_gmask"]), (flip[:], t["const_flip"]),
                        (rowc[:, 0, :], t["hy_dt_bias"][0].partition_broadcast(P)),
                        (rowc[:, 1, :], t["hy_a_log"][0].partition_broadcast(P)),
                        (rowc[:, 2, :], t["hy_d_skip"][0].partition_broadcast(P)),
                        (ssm_gain[:, 0:KT], t["hy_ssm_norm_g"][0][0:D].rearrange("(p k) -> p k", k=KT)),
                        (ssm_gain[:, KT:], t["hy_ssm_norm_g"][0][D:].rearrange("(p k) -> p k", k=KT)),
                    ]
                    for dst, src in loads:
                        pool.dma_start(dst, src).then_inc(small, 16)
                pool.wait_ge(moved1, 1)
                pool.dma_start(bias_dram, bias_rows[:]).then_inc(stored, 16)
                pool.wait_ge(stored, 16)

            @block.tensor
            def _(pe):
                pe.wait_ge(small, 16 * 13)
                n = (CONV + 1) * XT
                pe.matmul(PS[0:ATT_G * KV_H, 1, 0:384], table[:], onehot[:], start=True, stop=False)
                pe.matmul(PS[0:ATT_G * KV_H, 1, 0:384], gsel[:], gmask[:], start=False, stop=True)
                pe.transpose(PS[:, 0, 0:n], rawc[0:n, :], ident[0:n, 0:n]).then_inc(made, 1)
                for i in range(TT):
                    for k in range(KT):
                        mm = pe.matmul(PS[:, 2, i * SSM_H:(i + 1) * SSM_H], HT[:, k, i * P:(i + 1) * P], wdt[:, k, :],
                                       start=(k == 0), stop=(k == KT - 1))
                mm.then_inc(made, 1)

            @block.vector
            def _(dve):
                dve.memset(XB[:, :, 0:CONV - 1], 0.0)
                dve.wait_ge(made, 1)
                dve.tensor_copy(bias_rows[:], PS[0:ATT_G * KV_H, 1, 0:384]).then_inc(moved1, 1)
                dve.tensor_copy(convT[:], PS[:, 0, 0:(CONV + 1) * XT])
                dve.wait_ge(made, 2)
                dve.tensor_tensor(dt[:], PS[:, 2, 0:TT * SSM_H].rearrange("p (i h) -> p i h", i=TT),
                                  bc(rowc[:, 0, :], 1, TT), ALU.add)

        def move_x(act, bank, j):
            return act.activation(XB[:, 2 * j:2 * j + 2, CONV - 1:], bank, ACT.Copy)

        def move_rows(dst):
            return lambda act, bank, j: act.activation(dst[:, 2 * j:2 * j + 2, :], bank, ACT.Copy)

        def move_q(act, bank, j):
            return act.activation(QT[:, 2 * j:2 * j + 2, :].rearrange("p a (i n) -> p (a i) n", n=P),
                                  bank.rearrange("p a (i n) -> p (a i) n", n=P)[:, :, ::-1], ACT.Copy)

        def move_tokens(dst, c0, func=ACT.Copy):
            return lambda act, bank, j: act.activation(dst[:, :, c0 + j * CW:c0 + (j + 1) * CW], bank, func)

        with ExitStack() as beside:
            ada = Ada(beside, *ada_2, groups=(1,), per_step=1)
            stage = sb(beside, "ada_stage", [P, 1, 2 * D])
            project([("hy_x", 0, 12, "rows", move_x), ("hy_q", 0, 12, "rows", move_q),
                     ("hy_k", 0, 4, "rows", move_rows(KTT)), ("hy_z", 0, 8, "tokens", move_tokens(ZV, 0, ACT.Silu)),
                     ("hy_v", 0, 4, "tokens", move_tokens(ZV, SSM_IN))], ada, stage)
            ada.finish()

        BT = sb(inner, "bias_tiles", [P, 2, ATT_G, S])
        SC = sb(inner, "att_scores", [P, 3, ATT_G, S])
        PT = sb(inner, "att_probs_T", [P, 2, S])
        nmax = sb(inner, "neg_max", [P, 4])
        zsum = sb(inner, "prob_sums", [P, 4])
        zinv = sb(inner, "prob_inv", [P, 4])
        FL = sb(inner, "flip_scaled", [P, 2, P])
        flipped = sem("a_flipped")
        bias_in = [pool_dma_sem("bias_in0"), pool_dma_sem("bias_in1")]
        scored, biased, maxed, exped, summed, copied, valued, normed = (
            sem("a_scored"), sem("a_biased"), sem("a_maxed"), sem("a_exped"), sem("a_summed"), sem("a_copied"),
            sem("a_valued"), sem("a_normed"))
        U = KV_H * TT
        with nc.Block() as block:
            @block.gpsimd
            def _(pool):
                for h in range(KV_H):
                    if h >= 2:
                        pool.wait_ge(biased, 2 * (h - 1))
                    pool.dma_start(BT[:, h % 2], bass.AP(tensor=bias_dram.tensor, offset=h * 384,
                                                         ap=[[1, P], [KV_H * 384, ATT_G], [1, S]]))\
                        .then_inc(bias_in[h % 2], 16)

            @block.tensor
            def _(pe):
                def score(u):
                    h, i = u // TT, u % TT
                    r0, n = HD * (h % 2), (i + 1) * P
                    for g in range(ATT_G):
                        b = 2 * (u % 2) + g // 2
                        mm = pe.matmul(PS[:, b, (g % 2) * S:(g % 2) * S + n],
                                       QT[r0:r0 + HD, g * KT + h // 2, i * P:(i + 1) * P],
                                       KTT[r0:r0 + HD, h // 2, 0:n], start=True, stop=True)
                    mm.then_inc(scored, 1)

                def add_groups(u):
                    i = u % TT
                    pe.wait_ge(flipped, u + 1)
                    for st in range(i + 1):
                        for g in range(ATT_G):
                            mm = pe.matmul(PS[:, 4 + u % 2, st * P:(st + 1) * P], SC[:, u % 3, g, st * P:(st + 1) * P],
                                           FL[:, u % 2, :], start=(g == 0), stop=(g == ATT_G - 1))
                    mm.then_inc(summed, 1)

                def value(u):
                    h, i = u // TT, u % TT
                    pe.wait_ge(copied, u + 1)
                    if u >= 2:
                        pe.wait_ge(normed, u - 1)
                    for st in range(i + 1):
                        mm = pe.matmul(PS[:, 6 + u % 2, 0:HD], PT[:, u % 2, st * P:(st + 1) * P],
                                       ZV[:, st, SSM_IN + h * HD:SSM_IN + (h + 1) * HD], start=(st == 0), stop=(st == i))
                    mm.then_inc(valued, 1)

                for u in range(U + 3):
                    if u < U:
                        if u >= 2:
                            pe.wait_ge(biased, u - 1)
                        score(u)
                    if 2 <= u < U + 2:
                        add_groups(u - 2)
                    if u >= 3:
                        value(u - 3)

            @block.vector
            def _(dve):
                step = stepper(dve, dve_step)
                for u in range(U + 4):
                    if u < U:
                        h, i = u // TT, u % TT
                        n = (i + 1) * P
                        dve.wait_ge(bias_in[h % 2], 16 * (h // 2 + 1))
                        dve.wait_ge(scored, u + 1)
                        if u >= 3:
                            dve.wait_ge(summed, u - 2)
                        ps = PS[:, 2 * (u % 2):2 * (u % 2) + 2, :].rearrange("p a (g s) -> p (a g) s", s=S)
                        dve.scalar_tensor_tensor(out=SC[:, u % 3, :, 0:n], in0=ps[:, 0:ATT_G, 0:n], scalar=HD ** -0.5,
                                                 in1=BT[:, h % 2, :, S - n:], op0=ALU.mult, op1=ALU.add)\
                            .then_inc(biased, 1)
                        dve.wait_ge(biased, u + 1)
                        dve.tensor_reduce(nmax[:, u % 4:u % 4 + 1], SC[:, u % 3, :, 0:n], AX.XY, ALU.max, negate=True)\
                            .then_inc(maxed, 1)
                    if 1 <= u <= U:
                        v = u - 1
                        if u == U:
                            dve.wait_ge(summed, v - 1)
                        dve.wait_ge(exped, v + 1)
                        step(dve.reciprocal(zinv[:, v % 4:v % 4 + 1], zsum[:, v % 4:v % 4 + 1]))
                        dve.tensor_scalar(FL[:, v % 2, :], flip[:], zinv[:, v % 4:v % 4 + 1], None,
                                          ALU.mult).then_inc(flipped, 1)
                    if u >= 4:
                        v = u - 4
                        h, i = v // TT, v % TT
                        dve.wait_ge(valued, v + 1)
                        dve.tensor_copy(att[:, i, h * HD:(h + 1) * HD], PS[:, 6 + v % 2, 0:HD]).then_inc(normed, 1)

            @block.scalar
            def _(act):
                for u in range(U + 2):
                    if u < U:
                        n = (u % TT + 1) * P
                        act.wait_ge(maxed, u + 1)
                        act.activation(SC[:, u % 3, :, 0:n], SC[:, u % 3, :, 0:n], ACT.Exp,
                                       bias=nmax[:, u % 4:u % 4 + 1], accum_out=zsum[:, u % 4:u % 4 + 1])\
                            .then_inc(exped, 1)
                    if u >= 2:
                        v = u - 2
                        n = (v % TT + 1) * P
                        act.wait_ge(summed, v + 1)
                        act.activation(PT[:, v % 2, 0:n], PS[:, 4 + v % 2, 0:n], ACT.Copy).then_inc(copied, 1)
        inner.close()

        inner = ExitStack()
        xs = sb(inner, "xs", [P, TT, SSM_IN])
        acc = sb(inner, "conv_acc", [P, 4, S])
        la = sb(inner, "dt_a", [P, TT, SSM_H])
        sp8 = sb(inner, "softplus", [P, 8, TT * SSM_H])
        conv, conved, xturned, xmoved = sem("s_conv"), sem("s_conved"), sem("s_turned"), sem("s_moved")
        e_in, e_out, scan_ps = sem("s_ein"), sem("s_eout"), sem("s_scan")
        with nc.Block() as block:
            @block.vector
            def _(dve):
                step = stepper(dve, dve_step)
                dtf = dt[:].rearrange("p i h -> p (i h)")
                step(dve.tensor_scalar(sp8[:, 0, :], dtf, -1.0, None, ALU.mult))
                dve.tensor_tensor(sp8[:, 1, :], sp8[:, 0, :], dtf, ALU.min).then_inc(e_in, 1)
                dve.wait_ge(e_out, 1)
                step(dve.tensor_scalar(sp8[:, 2, :], sp8[:, 1, :], 2.0, None, ALU.add))
                step(dve.reciprocal(sp8[:, 3, :], sp8[:, 2, :]))
                step(dve.tensor_tensor(sp8[:, 4, :], sp8[:, 1, :], sp8[:, 3, :], ALU.mult))
                step(dve.tensor_tensor(sp8[:, 5, :], sp8[:, 4, :], sp8[:, 4, :], ALU.mult))
                step(dve.tensor_scalar(sp8[:, 6, :], sp8[:, 5, :], 1.0 / 17, None, ALU.mult))
                for k in range(7, 0, -1):
                    step(dve.scalar_tensor_tensor(out=sp8[:, 6, :], in0=sp8[:, 6, :], scalar=1.0 / (2 * k + 1),
                                                  in1=sp8[:, 5, :], op0=ALU.add, op1=ALU.mult))
                step(dve.scalar_tensor_tensor(out=sp8[:, 6, :], in0=sp8[:, 6, :], scalar=1.0, in1=sp8[:, 4, :],
                                              op0=ALU.add, op1=ALU.mult))
                step(dve.tensor_scalar(sp8[:, 7, :], dtf, 0.0, None, ALU.max))
                step(dve.scalar_tensor_tensor(out=dtf, in0=sp8[:, 6, :], scalar=2.0, in1=sp8[:, 7, :],
                                              op0=ALU.mult, op1=ALU.add))
                dve.wait_ge(e_out, 2)
                step(dve.scalar_tensor_tensor(out=la[:], in0=dt[:], scalar=-1.0, in1=bc(rowc[:, 1, :], 1, TT),
                                              op0=ALU.mult, op1=ALU.mult))
                for m in range(XT):
                    a = acc[:, m % 4, :]
                    if m >= 4:
                        dve.wait_ge(conved, m - 3)
                    for j in range(CONV):
                        w = convT[:, j * XT + m:j * XT + m + 1]
                        if j == 0:
                            ins = dve.tensor_scalar(a, XB[:, m, 0:S], w, convT[:, CONV * XT + m:CONV * XT + m + 1],
                                                    ALU.mult, ALU.add)
                        else:
                            ins = dve.scalar_tensor_tensor(out=a, in0=XB[:, m, j:j + S], scalar=w, in1=a,
                                                           op0=ALU.mult, op1=ALU.add)
                        if j < CONV - 1:
                            step(ins)
                        else:
                            ins.then_inc(conv, 1)

            @block.scalar
            def _(act):
                act.wait_ge(e_in, 1)
                act.activation(sp8[:, 1, :], sp8[:, 1, :], ACT.Exp).then_inc(e_out, 1)
                act.activation(rowc[:, 1, :], rowc[:, 1, :], ACT.Exp).then_inc(e_out, 1)
                for m in range(XT):
                    act.wait_ge(conv, m + 1)
                    act.activation(XB[:, m, CONV - 1:], acc[:, m % 4, :], ACT.Silu).then_inc(conved, 1)
                    if m >= 1 and m - 1 < SSM_IN // P:
                        n = m - 1
                        act.wait_ge(xturned, n + 1)
                        act.activation(xs[:, :, n * P:(n + 1) * P],
                                       PS[:, n % 4, 0:S].rearrange("p (i n) -> p i n", i=TT), ACT.Copy)\
                            .then_inc(xmoved, 1)

            @block.tensor
            def _(pe):
                for m in range(SSM_IN // P):
                    pe.wait_ge(conved, m + 1)
                    if m >= 4:
                        pe.wait_ge(xmoved, m - 3)
                    for i in range(TT):
                        mm = pe.transpose(PS[:, m % 4, i * P:(i + 1) * P],
                                          XB[:, m, CONV - 1 + i * P:CONV - 1 + (i + 1) * P], ident[:])
                    mm.then_inc(xturned, 1)

        xdt = sb(inner, "xdt", [P, TT, SSM_IN])
        cbm = sb(inner, "cb_masked", [P, SSM_G, 384])
        cums = sb(inner, "cums", [P, TT, SSM_H])
        dd = sb(inner, "decays", [P, 3, 384])
        W = sb(inner, "ssm_weights", [P, 3, 384])
        cb_ps, cb_mv, cum_ps, bcast, diffed, exped, weighted, vdone, xready, ymoved, yinit = (
            sem("s_cb"), sem("s_cbm"), sem("s_cum"), sem("s_bcast"), sem("s_diff"), sem("s_exp"), sem("s_weight"),
            sem("s_value"), sem("s_xready"), sem("s_ymoved"), sem("s_yinit"))
        GH = SSM_H // SSM_G

        def move_y(dve, g):
            dve.wait_ge(vdone, (g + 1) * GH)
            dve.wait_ge(yinit, TT)
            c = slice(g * GH * HD, (g + 1) * GH * HD)
            b = 4 + 2 * (g % 2)
            dve.tensor_tensor(y[:, :, c], y[:, :, c], PS[:, b:b + 2, :], ALU.add).then_inc(ymoved, 1)

        with nc.Block() as block:
            @block.tensor
            def _(pe):
                pe.matmul(PS[:, 2, 0:SSM_H], pairs[:, 0:P], la[:, 0, :], start=True, stop=True)
                pe.matmul(PS[:, 2, SSM_H:2 * SSM_H], ones[:], la[:, 0, :], start=True, stop=False)
                pe.matmul(PS[:, 2, SSM_H:2 * SSM_H], pairs[:, 0:P], la[:, 1, :], start=False, stop=True)\
                    .then_inc(cum_ps, 1)
                for g in range(SSM_G):
                    B = XB[:, SSM_IN // P + g, CONV - 1:]
                    C = XB[:, SSM_IN // P + SSM_G + g, CONV - 1:]
                    if g >= 2:
                        pe.wait_ge(cb_mv, g - 1)
                    pe.matmul(PS[:, g % 2, 0:S], B[:, 0:P], C, start=True, stop=True)
                    pe.matmul(PS[:, g % 2, S:384], B[:, P:S], C[:, P:S], start=True, stop=True).then_inc(cb_ps, 1)
                pe.wait_ge(cb_mv, SSM_G)
                pe.wait_ge(xready, 1)

                def spread(h):
                    if h >= 4:
                        pe.wait_ge(diffed, h - 3)
                    pe.matmul(PS[:, h % 4, 0:S], la[:, 0, h:h + 1].broadcast_to([P, P]), pairs[:, 0:S],
                              start=True, stop=False)
                    pe.matmul(PS[:, h % 4, P:S], la[:, 1, h:h + 1].broadcast_to([P, P]), pairs[:, 0:P],
                              start=False, stop=True).then_inc(bcast, 1)

                def values(h):
                    g = h // GH
                    if g >= 2 and h % GH == 0:
                        pe.wait_ge(ymoved, g - 1)
                    pe.wait_ge(weighted, h + 1)
                    w = W[:, h % 3, :]
                    c = (h % GH) * HD
                    x = xdt[:, :, h * HD:(h + 1) * HD]
                    o = [PS[:, 4 + 2 * (g % 2) + i, c:c + HD] for i in range(TT)]
                    pe.matmul(o[0], w[:, 0:P], x[:, 0, :], start=True, stop=True)
                    pe.matmul(o[1], w[:, P:2 * P], x[:, 0, :], start=True, stop=False)
                    pe.matmul(o[1], w[:, 2 * P:3 * P], x[:, 1, :], start=False, stop=True).then_inc(vdone, 1)

                for h in range(SSM_H + 2):
                    if h < SSM_H:
                        spread(h)
                    if h >= 2:
                        values(h - 2)

            @block.vector
            def _(dve):
                dve.wait_ge(cum_ps, 1)
                dve.tensor_copy(cums[:], PS[:, 2, 0:2 * SSM_H].rearrange("p (i h) -> p i h", i=TT))
                for g in range(SSM_G):
                    dve.wait_ge(cb_ps, g + 1)
                    dve.tensor_tensor(cbm[:, g, :], PS[:, g % 2, 0:384], pairs[:], ALU.mult).then_inc(cb_mv, 1)
                dve.wait_ge(cb_mv, SSM_G)
                v4 = lambda ap: ap.rearrange("p i (h d) -> p (i h) d", d=HD)
                dve.tensor_tensor(v4(xdt[:]), v4(xs[:]), bc(dt[:].rearrange("p i h -> p (i h)"), 2, HD),
                                  ALU.mult).then_inc(xready, 1)
                for h in range(SSM_H):
                    dve.wait_ge(bcast, h + 1)
                    if h >= 3:
                        dve.wait_ge(weighted, h - 2)
                    dve.tensor_scalar(dd[:, h % 3, 0:S], PS[:, h % 4, 0:S], cums[:, 0, h:h + 1], 0.0,
                                      ALU.subtract, ALU.min)
                    dve.tensor_scalar(dd[:, h % 3, S:384], PS[:, h % 4, P:S], cums[:, 1, h:h + 1], 0.0,
                                      ALU.subtract, ALU.min).then_inc(diffed, 1)
                    if h % GH == 2 and h > GH:
                        move_y(dve, h // GH - 1)
                move_y(dve, SSM_G - 1)

            @block.scalar
            def _(act):
                for h in range(SSM_H):
                    act.wait_ge(diffed, h + 1)
                    act.activation(dd[:, h % 3, :], dd[:, h % 3, :], ACT.Exp).then_inc(exped, 1)

            @block.gpsimd
            def _(pool):
                for i in range(TT):
                    pool.tensor_tensor(y[:, i, :].rearrange("p (h d) -> p h d", d=HD),
                                       xs[:, i, :].rearrange("p (h d) -> p h d", d=HD),
                                       bc(rowc[:, 2, :], 2, HD), ALU.mult).then_inc(yinit, 1)
                for h in range(SSM_H):
                    pool.wait_ge(exped, h + 1)
                    if h >= 3:
                        pool.wait_ge(vdone, h - 2)
                    pool.tensor_tensor(W[:, h % 3, :], dd[:, h % 3, :], cbm[:, h // GH, :], ALU.mult)\
                        .then_inc(weighted, 1)

        squared, meaned, rooted = sem("y_squared"), sem("y_meaned"), sem("y_rooted")
        gated_y = sem("y_gated")
        with nc.Block() as block:
            @block.vector
            def _(dve):
                step = stepper(dve, dve_step)
                for i in range(TT):
                    dve.tensor_tensor(y[:, i, :], y[:, i, :], ZV[:, i, 0:SSM_IN], ALU.mult).then_inc(gated_y, 1)
                dve.wait_ge(squared, TT)
                dve.tensor_scalar(stat[:, 2:4], stat[:, 0:2], 1.0 / SSM_IN, EPS, ALU.mult, ALU.add).then_inc(meaned, 1)
                dve.wait_ge(rooted, 1)
                step(dve.reciprocal(stat[:, 6:8], stat[:, 4:6]))
                for i in range(TT):
                    dve.tensor_scalar(y[:, i, :], y[:, i, :], stat[:, 6 + i:7 + i], None, ALU.mult)

            @block.scalar
            def _(act):
                for i in range(TT):
                    act.wait_ge(gated_y, i + 1)
                    act.activation(xs[:, i, :], y[:, i, :], ACT.Square, accum_out=stat[:, i:i + 1]).then_inc(squared, 1)
                act.wait_ge(meaned, 1)
                act.activation(stat[:, 4:6], stat[:, 2:4], ACT.Sqrt).then_inc(rooted, 1)
        inner.close()
        wide.close()
        YT = sb(scope, "y_T", [P, 3 * KT, S])
        turn_features(y, YT[:, 0:2 * KT, :], 2, ssm_gain)
        turn_features(att, YT[:, 2 * KT:, :], 1, None)
        ada = Ada(scope, *ada_2, groups=(2,), per_step=4)
        output_projection("hy_out", YT, 3, gate_a, ada=ada)
        ada.finish()

    norm_block(mod[:, 3, :], mod[:, 2, :])
    between = ExitStack()
    ada_3 = Ada(between, t["c_2"], t["ada_w"][1], t["ada_b"][1], t["norm_mix_g"][1], t["norm_ffn_g"][1],
                groups=(0, 1, 2), per_step=6)
    swiglu("ffn0", ffn_source(0), FFN_CHUNKS, gate_b, ada_3)

    clear_phase_sems()

    ada_3.finish()
    between.close()
    norm_block(mod[:, 1, :], mod[:, 0, :])

    with ExitStack() as scope:
        U0 = TAPS - 1
        UP = sb(scope, "conv_in", [P, KT, S + U0])
        CA = sb(scope, "conv_out", [P, KT, S])
        SG = sb(scope, "conv_gate", [P, KT, S])
        SQ = sb(scope, "conv_sq", [P, KT, S])
        raw = sb(scope, "vec_raw", [P, 3, P])
        vec = sb(scope, "vec_T", [P, 3, P])
        b2 = sb(scope, "pw2_bias", [1, D])
        rstd = sb(scope, "ln_rstd", [P, 3, S])
        meanw = sb(scope, "mean_weights", [P, P])
        small, made = pool_dma_sem("c_small"), sem("c_made")
        HALF = TAPS * KT // 2
        with nc.Block() as block:
            @block.gpsimd
            def _(pool):
                taps = t["cv_w_dw"][0].rearrange("j (m p) -> (j m) p", p=P)
                loads = [(raw[0:HALF, 0, :], taps[0:HALF, :]), (raw[0:HALF, 1, :], taps[HALF:, :]),
                         (raw[0:16, 2, :], t["cv_b_pw1"][0].rearrange("(m p) -> m p", p=P)),
                         (raw[16:24, 2, :], t["cv_b_dw"][0].rearrange("(m p) -> m p", p=P)),
                         (raw[24:32, 2, :], t["cv_ln_g"][0].rearrange("(m p) -> m p", p=P)),
                         (raw[32:40, 2, :], t["cv_ln_b"][0].rearrange("(m p) -> m p", p=P)),
                         (b2[:], t["cv_b_pw2"][0].rearrange("(a n) -> a n", a=1))]
                for dst, src in loads:
                    pool.dma_start(dst, src).then_inc(small, 16)
                pool.wait_ge(small, 16 * len(loads))

            @block.tensor
            def _(pe):
                pe.wait_ge(small, 16 * 7)
                for j, n in enumerate((HALF, HALF, 40)):
                    mm = pe.transpose(PS[:, j, 0:n], raw[0:n, j, :], ident[0:n, 0:n])
                mm.then_inc(made, 1)

            @block.vector
            def _(dve):
                dve.memset(UP[:, :, 0:U0], 0.0)
                dve.memset(meanw[:], 1.0 / D)
                dve.wait_ge(made, 1)
                for j, n in enumerate((HALF, HALF, 40)):
                    dve.tensor_copy(vec[:, j, 0:n], PS[:, j, 0:n])

        vb = vec[:, 2, :]
        base = segs["pw1"].base
        moved, glu = sem("g_moved"), sem("g_glu")
        with nc.Block() as block:
            @block.sync
            def _(sp):
                send_until(sp, base + 8)

            @block.tensor
            def _(pe):
                for q in range(8):
                    arrive(pe, base + q)
                    if q >= 4:
                        pe.wait_ge(moved, 2 * (q - 3))
                    rows_chunk(pe, base + q, q % 4).then_inc(used, 1)

            @block.scalar
            def _(act):
                for q in range(8):
                    act.wait_ge(used, base + q + 1)
                    c, half = q // 2, q % 2
                    for m in range(2):
                        f = 2 * c + m
                        bank = PS[:, q % 4, m * S:(m + 1) * S]
                        if half:
                            act.activation(SG[:, f, :], bank, ACT.Sigmoid, bias=vb[:, 8 + f:9 + f]).then_inc(moved, 1)
                        else:
                            act.activation(CA[:, f, :], bank, ACT.Identity, bias=vb[:, f:f + 1]).then_inc(moved, 1)

            @block.vector
            def _(dve):
                for c in range(4):
                    dve.wait_ge(moved, 4 * (c + 1))
                    f = slice(2 * c, 2 * c + 2)
                    dve.tensor_tensor(UP[:, f, U0:], CA[:, f, :], SG[:, f, :], ALU.mult)

        tap, means, centred, sqd, vars_, rooted, rs = (sem("d_tap"), sem("d_mean"), sem("d_centred"), sem("d_sq"),
                                                       sem("d_var"), sem("d_rooted"), sem("d_rs"))
        var_ready, diag_ready, diag_used, pe_tiles = (
            sem("d_vready"), [sem("d_diag_even"), sem("d_diag_odd")], sem("d_diag_used"), sem("d_tiles"))
        ON_DVE = 4
        DIAGS = 8
        diag = sb(scope, "tap_diag", [P, DIAGS, P])
        pe_work = [(m, j) for m in range(ON_DVE, KT) for j in range(TAPS)]

        def tap_weight(m, j):
            c = j * KT + m
            return vec[:, c // HALF, c % HALF:c % HALF + 1]

        with nc.Block() as block:
            @block.vector
            def _(dve):
                step = stepper(dve, dve_step)
                for j in range(TAPS):
                    for m in range(ON_DVE):
                        w = tap_weight(m, j)
                        if j == 0:
                            ins = dve.tensor_scalar(CA[:, m, :], UP[:, m, 0:S], w, vb[:, 16 + m:17 + m], ALU.mult, ALU.add)
                        else:
                            dve.wait_ge(tap, (j - 1) * ON_DVE + m + 1)
                            ins = dve.scalar_tensor_tensor(out=CA[:, m, :], in0=UP[:, m, j:j + S], scalar=w,
                                                           in1=CA[:, m, :], op0=ALU.mult, op1=ALU.add)
                        ins.then_inc(tap, 1)
                dve.wait_ge(means, 1)
                dve.tensor_tensor(CA[:], CA[:], bc(PS[:, 0, 0:S], 1, KT), ALU.subtract).then_inc(centred, 1)
                dve.wait_ge(vars_, 1)
                dve.tensor_scalar(rstd[:, 0, :], PS[:, 1, 0:S], EPS, None, ALU.add).then_inc(var_ready, 1)
                dve.wait_ge(rooted, 1)
                step(dve.reciprocal(rstd[:, 2, :], rstd[:, 1, :]))
                dve.tensor_tensor(CA[:], CA[:], bc(rstd[:, 2, :], 1, KT), ALU.mult).then_inc(rs, 1)

            @block.tensor
            def _(pe):
                for n, (m, j) in enumerate(pe_work):
                    pe.wait_ge(diag_ready[n % 2], n // 2 + 1)
                    pe.matmul(PS[:, 2 + m - ON_DVE, 0:S], diag[:, n % DIAGS, :], UP[:, m, j:j + S],
                              start=(j == 0), stop=(j == TAPS - 1)).then_inc(diag_used, 1)
                pe.wait_ge(pe_tiles, KT - ON_DVE)
                pe.wait_ge(tap, TAPS * ON_DVE)
                for m in range(KT):
                    mm = pe.matmul(PS[:, 0, 0:S], meanw[:], CA[:, m, :], start=(m == 0), stop=(m == KT - 1))
                mm.then_inc(means, 1)
                pe.wait_ge(sqd, 1)
                for m in range(KT):
                    mm = pe.matmul(PS[:, 1, 0:S], meanw[:], SQ[:, m, :], start=(m == 0), stop=(m == KT - 1))
                mm.then_inc(vars_, 1)

            @block.gpsimd
            def _(pool):
                for n in range(0, len(pe_work), 2):
                    if n >= DIAGS:
                        pool.wait_ge(diag_used, n - DIAGS + 1)
                    pool.tensor_scalar(diag[:, n % DIAGS, :], ident[:], tap_weight(*pe_work[n]), None,
                                       ALU.mult).then_inc(diag_ready[0], 1)

            @block.scalar
            def _(act):
                for n in range(1, len(pe_work), 2):
                    if n >= DIAGS:
                        act.wait_ge(diag_used, n - DIAGS + 1)
                    act.activation(diag[:, n % DIAGS, :], ident[:], ACT.Copy,
                                   scale=tap_weight(*pe_work[n])).then_inc(diag_ready[1], 1)
                for m in range(ON_DVE, KT):
                    act.wait_ge(diag_used, (m - ON_DVE + 1) * TAPS)
                    act.activation(CA[:, m, :], PS[:, 2 + m - ON_DVE, 0:S], ACT.Identity,
                                   bias=vb[:, 16 + m:17 + m]).then_inc(pe_tiles, 1)
                act.wait_ge(centred, 1)
                act.activation(SQ[:], CA[:], ACT.Square).then_inc(sqd, 1)
                act.wait_ge(var_ready, 1)
                act.activation(rstd[:, 1, :], rstd[:, 0, :], ACT.Sqrt).then_inc(rooted, 1)
                act.wait_ge(rs, 1)
                for m in range(KT):
                    act.activation(SQ[:, m, :], CA[:, m, :], ACT.Silu, scale=vb[:, 24 + m:25 + m],
                                   bias=vb[:, 32 + m:33 + m])
        output_projection("pw2", SQ, 1, gate_a, bias=b2)

    norm_block(mod[:, 3, :], mod[:, 2, :])
    swiglu("ffn1", ffn_source(1), FFN_CHUNKS, gate_b)

    plain_norm(t["final_norm_g"], out)


def _constants(np):
    p = np.arange(P)
    tri = (p[:, None] <= p[None, :]).astype(np.float32)
    pairs = np.concatenate([tri, np.ones((P, P), np.float32), tri], axis=1)
    levels = np.zeros((P, LEVELS, P), np.float32)
    levels[:, 0, :] = np.eye(P)
    for l in range(1, LEVELS):
        b = 1 << (l - 1)
        block, half = p // (2 * b), (p // b) % 2
        levels[:, l, :] = ((block[:, None] == block[None, :]) & (half[:, None] == 0) & (half[None, :] == 1))
    log_gamma = np.log1p(-np.exp2(-5.0 - np.arange(RET_H)))
    rel = np.concatenate([np.arange(S)[None, :] - p[:, None], p[None, :] - p[:, None]], axis=1)
    decay = np.where(rel[:, None, :] >= 0, np.exp(log_gamma[None, :, None] * np.maximum(rel, 0)[:, None, :]), 0.0)
    freq = np.float32(10000.0) ** (-np.arange(0, HD, 2, dtype=np.float32) / np.float32(HD))
    dist = 255 - np.arange(384)
    exact = BUCKETS // 2
    n = np.maximum(dist, 1).astype(np.float64)
    large = np.minimum((exact + np.log(n / exact) / np.log(2048 / exact) * (BUCKETS - exact)).astype(np.int64), BUCKETS - 1)
    bucket = np.where(dist < exact, np.maximum(dist, 0), large)
    onehot = (np.arange(BUCKETS)[:, None] == bucket[None, :]).astype(np.float32)
    gmask = np.stack([np.where((dist >= 0) & (dist % dil == 0) & (dist <= w), 0.0, NEG)
                      for w, dil in ((128, 1), (512, 4), (2048, 16))])
    gsel = np.repeat(np.eye(ATT_G), KV_H, axis=1)
    order = np.tile(16.0 - np.arange(16), (P, 1))
    out = {"ident": np.eye(P), "pairs": pairs, "levels": levels, "decay": decay, "freq": np.tile(freq, (P, 1)),
           "onehot": onehot, "gmask": gmask, "gsel": gsel, "order": order, "flip": np.eye(P)[::-1],
           "slots": np.tile(np.arange(SLOTS), (P, 1))}
    return {f"const_{k}": np.ascontiguousarray(v, dtype=np.float32) for k, v in out.items()}


_FIRST = ["x", "c", "positions", "w_ada", "b_ada", "norm_mix", "norm_ffn", "w_in", "ret_norm", "hgrn_norm",
          "hgrn_lb_logits", "gla_wa2", "gla_ba", "gla_norm", "w_out", "router_group_w", "router_group_b",
          "router_expert_w", "router_expert_b", "expert_w_gate", "expert_w_up", "expert_w_down",
          "norm_final"]
_SECOND = ["c_2", "ada_w_2", "ada_b_2", "norm_mix_g_2", "norm_ffn_g_2", "hy_w_in_2", "hy_conv_w_2", "hy_conv_b_2",
           "hy_dt_bias_2", "hy_a_log_2", "hy_d_skip_2", "hy_ssm_norm_g_2", "hy_w_out_2", "rel_table_2", "cv_w_pw1_2",
           "cv_b_pw1_2", "cv_w_dw_2", "cv_b_dw_2", "cv_ln_g_2", "cv_ln_b_2", "cv_w_pw2_2", "cv_b_pw2_2",
           "ffn_w_gate_2", "ffn_w_up_2", "ffn_w_down_2", "final_norm_g_2"]


def kernel(**inputs):
    import numpy as np
    import concourse.bacc as bacc
    from concourse.bass_utils import run_bass_kernel_spmd

    nc = bacc.Bacc("TRN2", target_bir_lowering=False, num_devices=1)
    arrays, t = {}, {}
    sources = {n: inputs[n] for n in _FIRST + _SECOND}
    sources.update(_constants(np))
    for name, value in sources.items():
        a = np.ascontiguousarray(value)
        arrays[f"in_{name}"] = a
        ap = nc.dram_tensor(f"in_{name}", a.shape, mybir.dt.from_np(a.dtype), kind="ExternalInput").ap()
        t[name if name == "c_2" or not name.endswith("_2") else name[:-2]] = ap
    out = nc.dram_tensor("out", (1, S, D), F32, kind="ExternalOutput").ap()
    build(nc, t, out)
    r = run_bass_kernel_spmd(nc, [arrays], core_ids=[0])
    return r.results[0]["out"]
```
